# Optimizing a Trainium2 kernel written in Bass

```python
import math
import jax
import jax.numpy as jnp
from jax import lax
import numpy as np
import jax, jax.numpy as jnp

D_MODEL = 2048
BATCH = 1
SEQ = 512
DEPTH = 1

CTX_LEN = 256
GRID_W = 64
N_DIR = 2
D_MIX = D_MODEL
SSD_WIDTH = D_MIX // 2
GDN_WIDTH = D_MIX - SSD_WIDTH
SSD_HEAD_DIM = 64
SSD_HEADS = SSD_WIDTH // SSD_HEAD_DIM
SSD_GROUPS = 2
SSD_HEADS_PER_GROUP = SSD_HEADS // SSD_GROUPS
SSD_STATE = 128
SSD_CONV_DIM = SSD_WIDTH + 2 * SSD_GROUPS * SSD_STATE
GDN_HEAD_DIM = 128
GDN_HEADS = GDN_WIDTH // GDN_HEAD_DIM
GDN_CONV_DIM = 3 * GDN_WIDTH
CONV_K = 5
CHUNK = 128
EPS = 1e-6

OFF_XBC = D_MIX
OFF_DT = OFF_XBC + SSD_CONV_DIM
OFF_QKV = OFF_DT + N_DIR * SSD_HEADS
OFF_BETA = OFF_QKV + GDN_CONV_DIM
OFF_ALPHA = OFF_BETA + N_DIR * GDN_HEADS
IN_DIM = OFF_ALPHA + N_DIR * GDN_HEADS


def rms_norm(x, w):
    xf = x.astype(jnp.float32)
    y = xf * lax.rsqrt(jnp.mean(xf * xf, axis=-1, keepdims=True) + EPS)
    return (y * w.astype(jnp.float32)).astype(x.dtype)

def l2_norm(t):
    return t * lax.rsqrt(jnp.sum(t * t, axis=-1, keepdims=True) + EPS)

def _flip(t):
    return t[:, ::-1]

def _same(t):
    return t

def centred_dwconv(x, w):
    pad = CONV_K // 2
    L = x.shape[1]
    xp = jnp.pad(x, ((0, 0), (pad, pad), (0, 0)))
    out = xp[:, 0:L] * w[0]
    for k in range(1, CONV_K):
        out = out + xp[:, k:k + L] * w[k]
    return out

def conv_latent(x, w):
    bsz, L, ch = x.shape
    rows = L // GRID_W
    y = centred_dwconv(x.reshape(bsz * rows, GRID_W, ch), w)
    return y.reshape(bsz, L, ch)

def _chunks(t):
    return t.reshape(t.shape[0], t.shape[1] // CHUNK, CHUNK, *t.shape[2:])

def ssd_scan(xs, dt, a_neg, bm, cm, h0):
    loga = _chunks(dt * a_neg)
    xdt = _chunks(xs * dt[..., None])
    bmc, cmc = _chunks(bm), _chunks(cm)
    acum = jnp.cumsum(loga, axis=2)
    causal = jnp.tril(jnp.ones((CHUNK, CHUNK), bool))
    a_t = jnp.moveaxis(acum, 2, -1)
    seg = a_t[..., :, None] - a_t[..., None, :]
    lmat = jnp.exp(jnp.where(causal, seg, -jnp.inf))
    cb = jnp.einsum('bcqgn,bcsgn->bcgqs', cmc, bmc)
    y_diag = jnp.einsum('bcgrqs,bcsgrp->bcqgrp', cb[:, :, :, None] * lmat, xdt)
    decay_end = jnp.exp(acum[:, :, -1:] - acum)
    states = jnp.einsum('bcsgn,bcsgrp->bcgrpn', bmc, xdt * decay_end[..., None])
    chunk_decay = jnp.exp(acum[:, :, -1])

    def step(h, inp):
        st, dec = inp
        return h * dec[..., None, None] + st, h

    h_last, h_prev = lax.scan(step, h0, (jnp.moveaxis(states, 1, 0), jnp.moveaxis(chunk_decay, 1, 0)))
    h_prev = jnp.moveaxis(h_prev, 0, 1)
    y_off = jnp.einsum('bcqgn,bcgrpn->bcqgrp', cmc, h_prev) * jnp.exp(acum)[..., None]
    return (y_diag + y_off).reshape(xs.shape), h_last

def gdn_scan(q, k, v, g, beta, s0):
    bsz, L, H, V = v.shape

    def heads_first(t):
        return jnp.moveaxis(_chunks(t), 3, 1)

    q, k, v, g, beta = (heads_first(t) for t in (q, k, v, g, beta))
    gcum = jnp.cumsum(g, axis=-1)
    incl = jnp.tril(jnp.ones((CHUNK, CHUNK), bool))
    strict = jnp.tril(jnp.ones((CHUNK, CHUNK), bool), -1)
    decay = jnp.exp(jnp.where(incl, gcum[..., :, None] - gcum[..., None, :], -jnp.inf))
    k_beta = k * beta[..., None]
    a_strict = jnp.where(strict, jnp.einsum('bhcik,bhcjk->bhcij', k_beta, k) * decay, 0.0)
    rhs = jnp.concatenate([v * beta[..., None], k_beta * jnp.exp(gcum)[..., None]], axis=-1)
    sol = lax.linalg.triangular_solve(a_strict, rhs, left_side=True, lower=True, unit_diagonal=True)
    u, w = sol[..., :V], sol[..., V:]
    attn = jnp.einsum('bhcik,bhcjk->bhcij', q, k) * decay
    q_dec = q * jnp.exp(gcum)[..., None]
    k_end = k * jnp.exp(gcum[..., -1:] - gcum)[..., None]
    chunk_decay = jnp.exp(gcum[..., -1])

    def step(S, inp):
        qd, ke, ui, wi, ai, dec = inp
        v_new = ui - jnp.einsum('bhqk,bhkv->bhqv', wi, S)
        o = jnp.einsum('bhqk,bhkv->bhqv', qd, S) + jnp.einsum('bhqs,bhsv->bhqv', ai, v_new)
        S = S * dec[..., None, None] + jnp.einsum('bhsk,bhsv->bhkv', ke, v_new)
        return S, o

    xs = tuple(jnp.moveaxis(t, 2, 0) for t in (q_dec, k_end, u, w, attn, chunk_decay))
    s_last, o = lax.scan(step, s0, xs)
    o = jnp.moveaxis(jnp.moveaxis(o, 0, 2), 1, 3).reshape(bsz, L, H, V)
    return o, s_last

def ssd_mixer(xbc_c, dt_c, xbc_l, dt_l, a_log, dt_bias, d_skip):
    G, R, P, N = SSD_GROUPS, SSD_HEADS_PER_GROUP, SSD_HEAD_DIM, SSD_STATE
    a_neg = -jnp.exp(a_log.astype(jnp.float32)).reshape(N_DIR, G, R)
    bias = dt_bias.astype(jnp.float32).reshape(N_DIR, G, R)

    def unpack(xbc, dt_raw):
        bsz, L = xbc.shape[:2]
        xbc = xbc.astype(jnp.float32)
        xs = xbc[..., :SSD_WIDTH].reshape(bsz, L, G, R, P)
        bm = xbc[..., SSD_WIDTH:SSD_WIDTH + G * N].reshape(bsz, L, G, N)
        cm = xbc[..., SSD_WIDTH + G * N:].reshape(bsz, L, G, N)
        dt = jax.nn.softplus(dt_raw.astype(jnp.float32).reshape(bsz, L, N_DIR, G, R) + bias)
        return xs, bm, cm, dt

    xc, bc, cc, dtc = unpack(xbc_c, dt_c)
    xl, bl, cl, dtl = unpack(xbc_l, dt_l)
    dsk = d_skip.astype(jnp.float32).reshape(G, R)[..., None]
    y_c, y_l = xc * dsk, xl * dsk
    h0 = jnp.zeros((xc.shape[0], G, R, P, N), jnp.float32)
    for d in range(N_DIR):
        f = _flip if d else _same
        yc_d, h_ctx = ssd_scan(f(xc), f(dtc[:, :, d]), a_neg[d], f(bc), f(cc), h0)
        yl_d, _ = ssd_scan(f(xl), f(dtl[:, :, d]), a_neg[d], f(bl), f(cl), h_ctx)
        y_c = y_c + f(yc_d)
        y_l = y_l + f(yl_d)
    return y_c.reshape(*xc.shape[:2], SSD_WIDTH), y_l.reshape(*xl.shape[:2], SSD_WIDTH)

def gdn_mixer(qkv_c, b_c, a_c, qkv_l, b_l, a_l, a_log, dt_bias):
    H, K = GDN_HEADS, GDN_HEAD_DIM
    rate = jnp.exp(a_log.astype(jnp.float32))
    bias = dt_bias.astype(jnp.float32)

    def unpack(qkv, b_raw, a_raw):
        bsz, L = qkv.shape[:2]
        qkv = qkv.astype(jnp.float32).reshape(bsz, L, 3, H, K)
        q = l2_norm(qkv[:, :, 0]) * (K ** -0.5)
        k = l2_norm(qkv[:, :, 1])
        v = qkv[:, :, 2]
        beta = jax.nn.sigmoid(b_raw.astype(jnp.float32).reshape(bsz, L, N_DIR, H))
        g = -rate * jax.nn.softplus(a_raw.astype(jnp.float32).reshape(bsz, L, N_DIR, H) + bias)
        return q, k, v, beta, g

    qc, kc, vc, bec, gc = unpack(qkv_c, b_c, a_c)
    ql, kl, vl, bel, gl = unpack(qkv_l, b_l, a_l)
    s0 = jnp.zeros((qc.shape[0], H, K, K), jnp.float32)
    o_c = jnp.zeros_like(vc)
    o_l = jnp.zeros_like(vl)
    for d in range(N_DIR):
        f = _flip if d else _same
        oc_d, s_ctx = gdn_scan(f(qc), f(kc), f(vc), f(gc[:, :, d]), f(bec[:, :, d]), s0)
        ol_d, _ = gdn_scan(f(ql), f(kl), f(vl), f(gl[:, :, d]), f(bel[:, :, d]), s_ctx)
        o_c = o_c + f(oc_d)
        o_l = o_l + f(ol_d)
    return o_c, o_l

def ssd_out_norm(y, z, w):
    bsz, L = y.shape[:2]
    yg = (y * jax.nn.silu(z.astype(jnp.float32))).reshape(bsz, L, SSD_GROUPS, SSD_WIDTH // SSD_GROUPS)
    yg = yg * lax.rsqrt(jnp.mean(yg * yg, axis=-1, keepdims=True) + EPS)
    return yg.reshape(bsz, L, SSD_WIDTH) * w.astype(jnp.float32)

def gdn_out_norm(o, z, w):
    bsz, L = o.shape[:2]
    o = o * lax.rsqrt(jnp.mean(o * o, axis=-1, keepdims=True) + EPS) * w.astype(jnp.float32)
    return o.reshape(bsz, L, GDN_WIDTH) * jax.nn.silu(z.astype(jnp.float32))

def _split_proj(p):
    return (p[..., :OFF_XBC], p[..., OFF_XBC:OFF_DT], p[..., OFF_DT:OFF_QKV],
            p[..., OFF_QKV:OFF_BETA], p[..., OFF_BETA:OFF_ALPHA], p[..., OFF_ALPHA:IN_DIM])

def hybrid_layer(h_lat, h_ctx, mod_lat, mod_ctx, pre_w, post_w, w_in, conv_ssd_w, conv_ssd_b,
                 conv_gdn_w, ssd_a_log, ssd_dt_bias, ssd_d, ssd_norm_w, gdn_a_log, gdn_dt_bias,
                 gdn_norm_w, w_out, update_ctx):
    shift_l, scale_l, gate_l = jnp.split(mod_lat, 3, axis=-1)
    shift_c, scale_c, gate_c = jnp.split(mod_ctx, 3, axis=-1)
    u_l = rms_norm(h_lat, pre_w) * (1 + scale_l[:, None]) + shift_l[:, None]
    u_c = rms_norm(h_ctx, pre_w) * (1 + scale_c) + shift_c
    z_l, xbc_l, dt_l, qkv_l, b_l, a_l = _split_proj(u_l @ w_in)
    z_c, xbc_c, dt_c, qkv_c, b_c, a_c = _split_proj(u_c @ w_in)
    xbc_l = jax.nn.silu(conv_latent(xbc_l, conv_ssd_w) + conv_ssd_b)
    xbc_c = jax.nn.silu(centred_dwconv(xbc_c, conv_ssd_w) + conv_ssd_b)
    qkv_l = jax.nn.silu(conv_latent(qkv_l, conv_gdn_w))
    qkv_c = jax.nn.silu(centred_dwconv(qkv_c, conv_gdn_w))
    ssd_c, ssd_l = ssd_mixer(xbc_c, dt_c, xbc_l, dt_l, ssd_a_log, ssd_dt_bias, ssd_d)
    gdn_c, gdn_l = gdn_mixer(qkv_c, b_c, a_c, qkv_l, b_l, a_l, gdn_a_log, gdn_dt_bias)

    def merge(ssd_y, gdn_o, z, dtype):
        y = jnp.concatenate([ssd_out_norm(ssd_y, z[..., :SSD_WIDTH], ssd_norm_w),
                             gdn_out_norm(gdn_o, z[..., SSD_WIDTH:], gdn_norm_w)], axis=-1)
        return rms_norm(y.astype(dtype) @ w_out, post_w)

    h_lat = h_lat + gate_l[:, None] * merge(ssd_l, gdn_l, z_l, h_lat.dtype)
    if update_ctx:
        h_ctx = h_ctx + gate_c * merge(ssd_c, gdn_c, z_c, h_ctx.dtype)
    return h_lat, h_ctx

def _dt_bias_init(key, shape):
    dt = jnp.exp(jax.random.uniform(key, shape, jnp.float32, math.log(1e-3), math.log(1e-1)))
    return dt + jnp.log(-jnp.expm1(-dt))

def first_inputs(seed: int = 0) -> dict:
    key = jax.random.key(seed)
    ks = jax.random.split(key, 20)
    f32 = jnp.float32

    def nrm(k, shape, s):
        return jax.random.normal(k, shape, f32) * s

    return {
        'x': nrm(ks[0], (BATCH, SEQ, D_MODEL), 1.0),
        'c': nrm(ks[1], (BATCH, D_MODEL), 1.0),
        'ctx': nrm(ks[2], (BATCH, CTX_LEN, D_MODEL), 1.0),
        'c_ctx': nrm(ks[3], (D_MODEL,), 1.0),
        'w_ada': nrm(ks[4], (DEPTH, D_MODEL, 3 * D_MODEL), 0.5 * D_MODEL ** -0.5),
        'b_ada': nrm(ks[5], (DEPTH, 3 * D_MODEL), 0.01),
        'pre_norm_w': 1.0 + nrm(ks[6], (DEPTH, D_MODEL), 0.05),
        'post_norm_w': 1.0 + nrm(ks[7], (DEPTH, D_MODEL), 0.05),
        'w_in': nrm(ks[8], (DEPTH, D_MODEL, IN_DIM), D_MODEL ** -0.5),
        'conv_ssd_w': nrm(ks[9], (DEPTH, CONV_K, SSD_CONV_DIM), CONV_K ** -0.5),
        'conv_ssd_b': nrm(ks[10], (DEPTH, SSD_CONV_DIM), 0.02),
        'conv_gdn_w': nrm(ks[11], (DEPTH, CONV_K, GDN_CONV_DIM), CONV_K ** -0.5),
        'ssd_a_log': jnp.log(jax.random.uniform(ks[12], (DEPTH, N_DIR, SSD_HEADS), f32, 1.0, 16.0)),
        'ssd_dt_bias': _dt_bias_init(ks[13], (DEPTH, N_DIR, SSD_HEADS)),
        'ssd_d': 1.0 + nrm(ks[14], (DEPTH, SSD_HEADS), 0.1),
        'ssd_norm_w': 1.0 + nrm(ks[15], (DEPTH, SSD_WIDTH), 0.05),
        'gdn_a_log': jnp.log(jax.random.uniform(ks[16], (DEPTH, N_DIR, GDN_HEADS), f32, 1.0, 16.0)),
        'gdn_dt_bias': _dt_bias_init(ks[17], (DEPTH, N_DIR, GDN_HEADS)),
        'gdn_norm_w': 1.0 + nrm(ks[18], (DEPTH, GDN_HEAD_DIM), 0.05),
        'w_out': nrm(ks[19], (DEPTH, D_MIX, D_MODEL), D_MIX ** -0.5),
    }

def first_block(x, c, ctx, c_ctx, w_ada, b_ada, pre_norm_w, post_norm_w, w_in, conv_ssd_w, conv_ssd_b,
              conv_gdn_w, ssd_a_log, ssd_dt_bias, ssd_d, ssd_norm_w, gdn_a_log, gdn_dt_bias,
              gdn_norm_w, w_out):
    h_lat, h_ctx = x, ctx
    c_act = jax.nn.silu(c)
    cc_act = jax.nn.silu(c_ctx)
    for l in range(DEPTH):
        mod_lat = c_act @ w_ada[l] + b_ada[l]
        mod_ctx = cc_act @ w_ada[l] + b_ada[l]
        h_lat, h_ctx = hybrid_layer(
            h_lat, h_ctx, mod_lat, mod_ctx, pre_norm_w[l], post_norm_w[l], w_in[l],
            conv_ssd_w[l], conv_ssd_b[l], conv_gdn_w[l], ssd_a_log[l], ssd_dt_bias[l], ssd_d[l],
            ssd_norm_w[l], gdn_a_log[l], gdn_dt_bias[l], gdn_norm_w[l], w_out[l],
            update_ctx=(l < DEPTH - 1))
    return h_lat


DEPTH_2 = 2

N_MEM = 256
W_MEM = D_MODEL // 4
W_CONV = (D_MODEL - W_MEM) // 2
W_DIFF = D_MODEL - W_MEM - W_CONV
W_MIX = W_CONV + W_DIFF + W_MEM
CONV_GROUP_DIM = 128
CONV_GROUPS = W_CONV // CONV_GROUP_DIM
CONV_WIDTH = 3
DIFF_V_DIM = 128
DIFF_HALF_DIM = 64
DIFF_HEADS = W_DIFF // DIFF_V_DIM
MEM_HEAD_DIM = 128
MEM_HEADS = W_MEM // MEM_HEAD_DIM
Q_BLOCK = 128
SPLIT_SIZES = (W_CONV, W_CONV, W_CONV, W_CONV,
               W_DIFF, W_DIFF, W_DIFF, W_DIFF,
               W_MEM, W_MEM)
IN_COLS = sum(SPLIT_SIZES)


def rmsnorm(x, g):
    xf = x.astype(jnp.float32)
    y = xf * lax.rsqrt(jnp.mean(xf * xf, axis=-1, keepdims=True) + EPS)
    return (y * g.astype(jnp.float32)).astype(x.dtype)

def alibi_slopes(n_heads):
    return jnp.asarray(np.array([2.0 ** (-8.0 * (h + 1) / n_heads) for h in range(n_heads)], dtype=np.float32))

def short_gated_conv(a_x, a_b, a_c, w, b):
    u = a_c * a_x
    up = jnp.pad(u, ((0, 0), (1, 1), (0, 0)))
    z = up[:, :-2] * w[0] + up[:, 1:-1] * w[1] + up[:, 2:] * w[2] + b
    return a_b * z

def diff_attention(q, k, v, lam, slopes):
    b, s = q.shape[0], q.shape[1]
    nb = s // Q_BLOCK
    scale = DIFF_HALF_DIM ** -0.5
    kt = k.transpose(0, 2, 3, 1, 4)
    vt = v.transpose(0, 2, 1, 3)
    qb = q.reshape(b, nb, Q_BLOCK, DIFF_HEADS, 2, DIFF_HALF_DIM).transpose(1, 0, 3, 4, 2, 5)
    key_pos = jnp.arange(s, dtype=jnp.float32)

    def block(args):
        qi, i = args
        qpos = (i * Q_BLOCK + jnp.arange(Q_BLOCK)).astype(jnp.float32)
        bias = -slopes[:, None, None] * jnp.abs(qpos[:, None] - key_pos[None, :])
        sc = jnp.einsum('bhcqd,bhckd->bhcqk', qi, kt).astype(jnp.float32) * scale + bias[None, :, None]
        p = jax.nn.softmax(sc, axis=-1).astype(vt.dtype)
        o = jnp.einsum('bhcqk,bhkd->bhcqd', p, vt)
        return o[:, :, 0] - lam.astype(o.dtype) * o[:, :, 1]

    out = lax.map(block, (qb, jnp.arange(nb)))
    return out.transpose(1, 0, 3, 2, 4).reshape(b, s, DIFF_HEADS, DIFF_V_DIM)

def memory_attention(q, mk, mv):
    sc = jnp.einsum('bshd,bmhd->bhsm', q, mk).astype(jnp.float32) * (MEM_HEAD_DIM ** -0.5)
    p = jax.nn.softmax(sc, axis=-1).astype(mv.dtype)
    return jnp.einsum('bhsm,bmhd->bshd', p, mv)

def second_inputs(seed: int = 0) -> dict:
    key = jax.random.key(seed)
    ks = jax.random.split(key, 18)
    nrm = jax.random.normal
    f32 = jnp.float32
    gain = lambda k, shape: 1.0 + 0.02 * nrm(k, shape, f32)
    return {
        "x": nrm(ks[0], (BATCH, SEQ, D_MODEL), f32),
        "mem": nrm(ks[1], (BATCH, N_MEM, D_MODEL), f32),
        "norm_g": gain(ks[2], (DEPTH_2, D_MODEL)),
        "w_in": nrm(ks[3], (DEPTH_2, D_MODEL, IN_COLS), f32) * D_MODEL ** -0.5,
        "conv_w": nrm(ks[4], (DEPTH_2, CONV_WIDTH, W_CONV), f32) * CONV_WIDTH ** -0.5,
        "conv_b": 0.02 * nrm(ks[5], (DEPTH_2, W_CONV), f32),
        "diff_q_norm_g": gain(ks[6], (DEPTH_2, DIFF_HALF_DIM)),
        "diff_k_norm_g": gain(ks[7], (DEPTH_2, DIFF_HALF_DIM)),
        "lambda_q1": 0.1 * nrm(ks[8], (DEPTH_2, DIFF_HALF_DIM), f32),
        "lambda_k1": 0.1 * nrm(ks[9], (DEPTH_2, DIFF_HALF_DIM), f32),
        "lambda_q2": 0.1 * nrm(ks[10], (DEPTH_2, DIFF_HALF_DIM), f32),
        "lambda_k2": 0.1 * nrm(ks[11], (DEPTH_2, DIFF_HALF_DIM), f32),
        "diff_head_norm_g": gain(ks[12], (DEPTH_2, DIFF_V_DIM)),
        "mem_norm_g": gain(ks[13], (DEPTH_2, D_MODEL)),
        "w_mem_kv": nrm(ks[14], (DEPTH_2, D_MODEL, 2 * W_MEM), f32) * D_MODEL ** -0.5,
        "mem_q_norm_g": gain(ks[15], (DEPTH_2, MEM_HEAD_DIM)),
        "mem_k_norm_g": gain(ks[16], (DEPTH_2, MEM_HEAD_DIM)),
        "w_out": nrm(ks[17], (DEPTH_2, W_MIX, D_MODEL), f32) * W_MIX ** -0.5,
    }

def second_block(x, mem, norm_g, w_in, conv_w, conv_b, diff_q_norm_g, diff_k_norm_g,
              lambda_q1, lambda_k1, lambda_q2, lambda_k2, diff_head_norm_g,
              mem_norm_g, w_mem_kv, mem_q_norm_g, mem_k_norm_g, w_out):
    b, s = x.shape[0], x.shape[1]
    slopes = alibi_slopes(DIFF_HEADS)
    offsets = list(np.cumsum(SPLIT_SIZES)[:-1])
    for l in range(DEPTH_2):
        h = rmsnorm(x, norm_g[l])
        proj = h @ w_in[l]
        a_x, a_b, a_c, a_g, d_q, d_k, d_v, d_g, m_q, m_g = jnp.split(proj, offsets, axis=-1)

        y_a = short_gated_conv(a_x, a_b, a_c, conv_w[l], conv_b[l]) * jax.nn.silu(a_g)

        q = rmsnorm(d_q.reshape(b, s, DIFF_HEADS, 2, DIFF_HALF_DIM), diff_q_norm_g[l])
        k = rmsnorm(d_k.reshape(b, s, DIFF_HEADS, 2, DIFF_HALF_DIM), diff_k_norm_g[l])
        v = d_v.reshape(b, s, DIFF_HEADS, DIFF_V_DIM)
        lam_init = 0.8 - 0.6 * float(np.exp(-0.3 * l))
        lam = (jnp.exp(jnp.sum(lambda_q1[l].astype(jnp.float32) * lambda_k1[l].astype(jnp.float32)))
               - jnp.exp(jnp.sum(lambda_q2[l].astype(jnp.float32) * lambda_k2[l].astype(jnp.float32)))
               + lam_init)
        o_d = diff_attention(q, k, v, lam, slopes)
        o_d = rmsnorm(o_d, diff_head_norm_g[l]) * (1.0 - lam_init)
        y_d = o_d.reshape(b, s, W_DIFF) * jax.nn.silu(d_g)

        mn = rmsnorm(mem, mem_norm_g[l])
        mkv = mn @ w_mem_kv[l]
        mk = rmsnorm(mkv[..., :W_MEM].reshape(b, N_MEM, MEM_HEADS, MEM_HEAD_DIM), mem_k_norm_g[l])
        mv = mkv[..., W_MEM:].reshape(b, N_MEM, MEM_HEADS, MEM_HEAD_DIM)
        mq = rmsnorm(m_q.reshape(b, s, MEM_HEADS, MEM_HEAD_DIM), mem_q_norm_g[l])
        y_m = memory_attention(mq, mk, mv).reshape(b, s, W_MEM) * jax.nn.silu(m_g)

        y = jnp.concatenate([y_a, y_d, y_m], axis=-1) @ w_out[l]
        x = x + y
    return x


def setup_inputs(seed=0):
    out = dict(first_inputs(seed))
    for name, value in second_inputs(seed + 1).items():
        if name != "x":
            out[name + "_2"] = value
    return out


def reference(
    x, c, ctx, c_ctx, w_ada, b_ada, pre_norm_w, post_norm_w, w_in, conv_ssd_w, conv_ssd_b,
    conv_gdn_w, ssd_a_log, ssd_dt_bias, ssd_d, ssd_norm_w, gdn_a_log, gdn_dt_bias, gdn_norm_w,
    w_out, mem_2, norm_g_2, w_in_2, conv_w_2, conv_b_2, diff_q_norm_g_2, diff_k_norm_g_2,
    lambda_q1_2, lambda_k1_2, lambda_q2_2, lambda_k2_2, diff_head_norm_g_2, mem_norm_g_2,
    w_mem_kv_2, mem_q_norm_g_2, mem_k_norm_g_2, w_out_2,
):
    x = first_block(
        x, c, ctx, c_ctx, w_ada, b_ada, pre_norm_w, post_norm_w, w_in, conv_ssd_w, conv_ssd_b,
        conv_gdn_w, ssd_a_log, ssd_dt_bias, ssd_d, ssd_norm_w, gdn_a_log, gdn_dt_bias,
        gdn_norm_w, w_out,
    )
    return second_block(
        x, mem_2, norm_g_2, w_in_2, conv_w_2, conv_b_2, diff_q_norm_g_2, diff_k_norm_g_2,
        lambda_q1_2, lambda_k1_2, lambda_q2_2, lambda_k2_2, diff_head_norm_g_2, mem_norm_g_2,
        w_mem_kv_2, mem_q_norm_g_2, mem_k_norm_g_2, w_out_2,
    )


_drawn_inputs = setup_inputs


def setup_inputs(seed=0):
    import zlib

    import numpy as np

    out = dict(_drawn_inputs(seed))
    spreads = {}
    factors = {'c_ctx': 3.634,
     'b_ada': 3.205,
     'conv_ssd_b': 5.177,
     'ssd_d': 3.224,
     'ssd_norm_w': 2.763,
     'gdn_norm_w': 4.775,
     'conv_b_2': 6.095,
     'diff_q_norm_g_2': 7.679,
     'diff_k_norm_g_2': 8.0,
     'lambda_k2_2': 5.373,
     'diff_head_norm_g_2': 7.5,
     'mem_norm_g_2': 8.0,
     'mem_q_norm_g_2': 8.0,
     'mem_k_norm_g_2': 8.0}
    for name, (base, spread) in spreads.items():
        noise = np.random.default_rng([zlib.crc32(name.encode()), seed]).standard_normal(out[name].shape)
        drawn = base * np.exp(spread * noise) if base else spread * noise
        out[name] = jnp.asarray(drawn.astype(out[name].dtype))
    for name, factor in factors.items():
        out[name] = (out[name] * factor).astype(out[name].dtype)
    return out
```

```python
import numpy as np
import concourse.bass as bass
from concourse import mybir
from contextlib import ExitStack

F32 = mybir.dt.float32
F32R = mybir.dt.float32r
BF16 = mybir.dt.bfloat16
ACT = mybir.ActivationFunctionType
ALU = mybir.AluOpType
AX = mybir.AxisListType

P = 128
D = 2048
KT = D // P
LAT, CTX = 512, 256
TOK = LAT + CTX
EPS = 1e-6
GRID = 64
TAPS = 5
SSD_W, SSD_H, SSD_P, SSD_N, SSD_G = 1024, 16, 64, 128, 2
GDN_W, GDN_H = 1024, 8
XBC = SSD_W + 2 * SSD_G * SSD_N
OFF_XBC = D
OFF_DT = OFF_XBC + XBC
OFF_QKV = OFF_DT + 2 * SSD_H
OFF_BETA = OFF_QKV + 3 * GDN_W
NSMALL = 2 * SSD_H + 4 * GDN_H
LCH, CCH = LAT // P, CTX // P
NCH = LCH + CCH
SCAN = ([LCH + c for c in range(CCH)] + list(range(LCH)),
        [LCH + c for c in range(CCH)][::-1] + list(range(LCH))[::-1])
BETA0, ALPHA0 = 2 * SSD_H, 2 * SSD_H + 2 * GDN_H

LAYERS = 2
W_CONV, W_DIFF, W_MEM = 768, 768, 512
IN2 = 4 * W_CONV + 4 * W_DIFF + 2 * W_MEM
MEMTOK = 256
DH, MH = W_DIFF // P, W_MEM // P
DIFF_HALF = 64
ABIAS = LAT + LAT - P
NEG = -1e30

C_ID, C_ONES, C_HALF, C_CUM, C_NEG, C_STRICT, C_LEVEL = 0, 128, 256, 384, 640, 896, 1152
NLEVEL = 7
C_END = C_LEVEL + 2 * NLEVEL * P


def constants():
    i = np.arange(P)[:, None]
    j = np.arange(P)[None, :]
    c = np.zeros((P, C_END), np.float32)
    c[:, C_ID:C_ID + P] = i == j
    c[:, C_ONES:C_ONES + P] = 1.0
    c[:, C_HALF:C_HALF + P] = (i // 64) == (j // 64)
    c[:, C_CUM:C_CUM + P] = i <= j
    c[:, C_CUM + P:C_CUM + 2 * P] = i >= j
    c[:, C_NEG:C_NEG + P] = np.where(i <= j, 0.0, NEG)
    c[:, C_NEG + P:C_NEG + 2 * P] = np.where(i >= j, 0.0, NEG)
    c[:, C_STRICT:C_STRICT + P] = i < j
    c[:, C_STRICT + P:C_STRICT + 2 * P] = i > j
    for d in range(2):
        for v in range(NLEVEL):
            s = 1 << v
            a, b = (i, j) if d == 0 else (j, i)
            pair = (a // (2 * s) == b // (2 * s)) & ((a // s) % 2 == 1) & ((b // s) % 2 == 0)
            at = C_LEVEL + (d * NLEVEL + v) * P
            c[:, at:at + P] = pair | (i == j)
    m = np.arange(ABIAS)[None, :] - (LAT - P)
    dist = np.abs(m - i).astype(np.float32)
    slopes = np.array([2.0 ** (-8.0 * (h + 1) / DH) for h in range(DH)], np.float32)
    bias = (-slopes[None, :, None] * dist[:, None, :]).astype(np.float32)
    return c, np.ascontiguousarray(bias.reshape(P, DH * ABIAS))


ROWS = [
    [("mod", 96), ("pre_norm_w", 16), ("post_norm_w", 16)],
    [("norm_g_2", 32), ("mem_norm_g_2", 32), ("conv_ssd_w", 60), ("gdn_norm_w", 1), ("diff_head_norm_g_2", 2)],
    [("conv_gdn_w", 120), ("ssd_norm_w", 8)],
    [("conv_ssd_b", 12), ("conv_w_2", 36), ("conv_b_2", 12), ("diff_q_norm_g_2", 2),
     ("diff_k_norm_g_2", 2), ("mem_q_norm_g_2", 2), ("mem_k_norm_g_2", 2)],
]
COL = {}
for _t, _rows in enumerate(ROWS):
    _at = 0
    for _name, _n in _rows:
        COL[_name] = _t * P + _at
        _at += _n
NCOL = 4 * P


class Phase:

    def __init__(self, nc, name):
        self.nc, self.name, self.ctx, self.sems = nc, name, ExitStack(), []

    def __enter__(self):
        self.ctx.__enter__()
        return self

    def __exit__(self, *a):
        if self.sems:
            self.nc.clear_and_free_semaphores(self.sems)
            self.nc.all_engine_barrier()
        return self.ctx.__exit__(*a)

    def sb(self, name, shape, dt=F32):
        return self.ctx.enter_context(self.nc.sbuf_tensor(f"{self.name}_{name}", shape, dt))

    def pb(self, name, n=512):
        return self.ctx.enter_context(self.nc.psum_tensor(f"{self.name}_{name}", [P, n], F32))

    def sem(self, name):
        self.sems.append(self.nc.alloc_semaphore(f"{self.name}_{name}"))
        return self.sems[-1]


def bc(ap, n, at):
    v = ap.unsqueeze(at)
    shape = list(v.shape)
    shape[at] = n
    return v.to_broadcast(shape)


def modulate(nc, dr):
    with Phase(nc, "ada") as ph:
        NB = 3 * D // 512
        ident = ph.sb("ident", [P, P])
        crow = ph.sb("crow", [2 * KT, P])
        cact = ph.sb("cact", [2 * KT, P])
        ccol = ph.sb("ccol", [P, KT, 2])
        w = ph.sb("w", [P, 2, KT, 512])
        bias = ph.sb("bias", [2, 3 * D])
        rows = ph.sb("rows", [2, 3 * D])
        pst = ph.pb("pst")
        acc = [ph.pb(f"acc{j}") for j in range(2)]
        c_loaded, bias_loaded, w_loaded = ph.sem("c_loaded"), ph.sem("bias_loaded"), [ph.sem(f"w_loaded{j}") for j in range(2)]
        act_done, turned, col_done = ph.sem("act_done"), ph.sem("turned"), ph.sem("col_done")
        block_done, bank_free, stored = ph.sem("block_done"), ph.sem("bank_free"), ph.sem("stored")
        w_v = dr.w_ada.rearrange("a (k p) n -> p (a k) n", p=P)

        with nc.Block() as block:
            @block.sync
            def _(sp):
                sp.dma_start(ident[:], dr.consts[:, C_ID:C_ID + P]).then_inc(c_loaded, 16)
                sp.dma_start(crow[0:KT, :], dr.c.rearrange("a (k p) -> (a k) p", p=P)).then_inc(c_loaded, 16)
                sp.dma_start(crow[KT:2 * KT, :], dr.c_ctx.rearrange("(k p) -> k p", p=P)).then_inc(c_loaded, 16)
                sp.dma_start(bias[:], dr.b_ada[0, :].partition_broadcast(2)).then_inc(bias_loaded, 16)
                with sp.Fori(0, NB // 2) as i:
                    for j in range(2):
                        sp.wait_ge(bank_free, i * 2 + j + 1)
                        sp.dma_start(w[:, j, :, :], w_v[:, :, bass.ds(i * 1024 + j * 512, 512)])\
                            .then_inc(w_loaded[j], 16)
                sp.wait_ge(bank_free, NB + 2)
                sp.dma_start(dr.mod, rows[:]).then_inc(stored, 16)
                sp.wait_ge(stored, 16)

            @block.scalar
            def _(act):
                act.wait_ge(c_loaded, 48)
                act.activation(cact[:], crow[:], ACT.Silu).then_inc(act_done, 1)

            @block.tensor
            def _(pe):
                pe.wait_ge(act_done, 1)
                pe.transpose(pst[:, 0:2 * KT], cact[:], ident[0:2 * KT, 0:2 * KT]).then_inc(turned, 1)
                pe.wait_ge(col_done, 1)
                with pe.Fori(0, NB // 2) as i:
                    for j in range(2):
                        pe.wait_ge(w_loaded[j], i * 16 + 16)
                        pe.wait_ge(bank_free, i * 2 + j + 1)
                        for k in range(KT):
                            mm = pe.matmul(acc[j][0:2, :], ccol[:, k, :], w[:, j, k, :],
                                           start=(k == 0), stop=(k == KT - 1))
                        mm.then_inc(block_done, 1)

            @block.vector
            def _(dve):
                dve.sem_inc(bank_free, 2)
                dve.wait_ge(turned, 1)
                dve.tensor_copy(ccol[:].rearrange("p k v -> p v k"),
                                pst[:, 0:2 * KT].rearrange("p (v k) -> p v k", v=2)).then_inc(col_done, 1)
                dve.wait_ge(bias_loaded, 16)
                with dve.Fori(0, NB // 2) as i:
                    for j in range(2):
                        dve.wait_ge(block_done, i * 2 + j + 1)
                        at = bass.ds(i * 1024 + j * 512, 512)
                        dve.tensor_tensor(rows[:, at], acc[j][0:2, :], bias[:, at], ALU.add).then_inc(bank_free, 1)


def columns(nc, dr, cols, ident):
    with Phase(nc, "col") as ph:
        rowt = ph.sb("rowt", [P, len(ROWS), P])
        xin = ph.sb("xin", [P, 2, D])
        xout = ph.sb("xout", [P, 2, KT, P])
        pst = [ph.pb(f"pst{j}") for j in range(4)]
        rows_loaded, turned, taken = ph.sem("rows_loaded"), ph.sem("turned"), ph.sem("taken")
        x_loaded = [ph.sem(f"x_loaded{j}") for j in range(2)]
        x_turned, x_stored = ph.sem("x_turned"), [ph.sem(f"x_stored{j}") for j in range(2)]
        NR = len(ROWS)
        height = [sum(n for _, n in rows) for rows in ROWS]
        tiles = [("x", dr.x, t, dr.xT, t) for t in range(LCH)] + [("c", dr.ctx, t, dr.xT, LCH + t) for t in range(CCH)] \
            + [("m", dr.mem, t, dr.memT, t) for t in range(MEMTOK // P)]
        NTL = len(tiles)
        views = {
            "mod": dr.mod.rearrange("v (k p) -> (v k) p", p=P),
            "gdn_norm_w": dr.gdn_norm_w, "diff_head_norm_g_2": dr.diff_head_norm_g_2,
            "mem_q_norm_g_2": dr.mem_q_norm_g_2, "mem_k_norm_g_2": dr.mem_k_norm_g_2,
            "conv_ssd_w": dr.conv_ssd_w.rearrange("a t (k p) -> (a t k) p", p=P),
            "conv_gdn_w": dr.conv_gdn_w.rearrange("a t (k p) -> (a t k) p", p=P),
            "conv_w_2": dr.conv_w_2.rearrange("a t (k p) -> (a t k) p", p=P),
        }
        for n, v in (("pre_norm_w", dr.pre_norm_w), ("post_norm_w", dr.post_norm_w), ("norm_g_2", dr.norm_g_2),
                     ("mem_norm_g_2", dr.mem_norm_g_2), ("ssd_norm_w", dr.ssd_norm_w),
                     ("conv_ssd_b", dr.conv_ssd_b), ("conv_b_2", dr.conv_b_2)):
            views[n] = v.rearrange("a (k p) -> (a k) p", p=P)
        ndma = sum(len(r) for r in ROWS) + 2 + 1

        with nc.Block() as block:
            @block.sync
            def _(sp):
                sp.dma_start(ident[:], dr.consts[:, C_ID:C_ID + P]).then_inc(rows_loaded, 16)
                for t, rows in enumerate(ROWS):
                    at = 0
                    for name, n in rows:
                        if name in ("diff_q_norm_g_2", "diff_k_norm_g_2"):
                            src = dr.diff_q_norm_g_2 if name == "diff_q_norm_g_2" else dr.diff_k_norm_g_2
                            for half in range(2):
                                sp.dma_start(rowt[at:at + n, t, half * 64:half * 64 + 64], src).then_inc(rows_loaded, 16)
                        else:
                            sp.dma_start(rowt[at:at + n, t, :], views[name]).then_inc(rows_loaded, 16)
                        at += n
                for n, (_, src, t, _, _) in enumerate(tiles):
                    if n >= 2:
                        sp.wait_ge(x_turned, (n - 1) * 4)
                    sp.dma_start(xin[:, n % 2, :], src[0, t * P:(t + 1) * P, :]).then_inc(x_loaded[n % 2], 16)

            @block.tensor
            def _(pe):
                pe.wait_ge(rows_loaded, 16 * ndma)
                for t in range(NR):
                    pe.transpose(pst[0][:, t * P:t * P + height[t]], rowt[0:height[t], t, :],
                                 ident[0:height[t], 0:height[t]]).then_inc(turned, 1)
                for n in range(NTL):
                    pe.wait_ge(x_loaded[n % 2], 16 * (n // 2 + 1))
                    for g in range(4):
                        if n or g:
                            pe.wait_ge(taken, 1 + max(0, 4 * n + g - 3))
                        for k in range(4):
                            mm = pe.transpose(pst[(4 * n + g + 1) % 4][:, k * P:(k + 1) * P],
                                              xin[:, n % 2, (4 * g + k) * P:(4 * g + k + 1) * P], ident[:])
                        mm.then_inc(x_turned, 1)

            @block.vector
            def _(dve):
                dve.wait_ge(turned, NR)
                dve.memset(cols[:], 0.0)
                dve.drain()
                for t in range(NR):
                    op = dve.tensor_copy(cols[:, t * P:t * P + height[t]], pst[0][:, t * P:t * P + height[t]])
                op.then_inc(taken, 1)
                for n in range(NTL):
                    if n >= 2:
                        dve.wait_ge(x_stored[n % 2], 16 * (n // 2))
                    for g in range(4):
                        dve.wait_ge(x_turned, 4 * n + g + 1)
                        dve.tensor_copy(xout[:, n % 2, 4 * g:4 * g + 4, :],
                                        pst[(4 * n + g + 1) % 4][:].rearrange("p (k t) -> p k t", k=4)).then_inc(taken, 1)

            @block.scalar
            def _(act):
                for n, (_, _, _, dst, t) in enumerate(tiles):
                    act.wait_ge(taken, 1 + 4 * (n + 1))
                    act.dma_start(dst.rearrange("(k p) t -> p k t", p=P)[:, :, t * P:(t + 1) * P],
                                  xout[:, n % 2, :, :]).then_inc(x_stored[n % 2], 16)
                for j in range(2):
                    act.wait_ge(x_stored[j], 16 * NTL // 2)


class Stream:

    UK = KT // 2

    def __init__(self, ph, sets=2, ctx=True):
        self.stage = ph.sb("stage", [P, 2, self.UK, 256])
        self.whi = ph.sb("whi", [P, 2, self.UK, 256], F32R)
        self.wlo = ph.sb("wlo", [P, 2, self.UK, 256], F32R)
        self.w_loaded = [ph.sem(f"w_loaded{j}") for j in range(2)]
        self.hi_ready, self.lo_ready = ph.sem("hi_ready"), ph.sem("lo_ready")
        self.unit_done, self.bank_free = ph.sem("unit_done"), ph.sem("bank_free")
        self.lat = [[ph.pb(f"lat{s}{m}") for m in range(2)] for s in range(2)]
        self.ctx = [ph.pb(f"ctx{s}") for s in range(2)] if ctx else None

    def load(self, sp, b, pieces, first=False):
        for j in range(2):
            if not first:
                sp.wait_ge(self.lo_ready, b * 2 + j - 1)
            for at, src in pieces:
                n = src.shape[2]
                sp.dma_start(self.stage[:, j, :, at:at + n], src[:, j * self.UK:(j + 1) * self.UK, :])\
                    .then_inc(self.w_loaded[j], 16)

    def split_hi(self, act, b, loaded, n=256, first=False):
        for j in range(2):
            act.wait_ge(self.w_loaded[j], loaded)
            if not first:
                act.wait_ge(self.unit_done, b * 2 + j - 1)
            act.activation(self.whi[:, j, :, 0:n], self.stage[:, j, :, 0:n], ACT.Copy).then_inc(self.hi_ready, 1)

    def split_lo(self, dve, b, n=256):
        for j in range(2):
            dve.wait_ge(self.hi_ready, b * 2 + j + 1)
            dve.tensor_tensor(self.wlo[:, j, :, 0:n], self.stage[:, j, :, 0:n],
                              self.whi[:, j, :, 0:n].bitcast(F32), ALU.subtract).then_inc(self.lo_ready, 1)

    def products(self, pe, b, s, u_hi, u_lo, tiles=2, lat=True, ctx=True):
        pe.wait_ge(self.bank_free, b + 1)
        for j in range(2):
            pe.wait_ge(self.lo_ready, b * 2 + j + 1)
            for k in range(self.UK):
                kt = j * self.UK + k
                for m in range(tiles):
                    for wt, ut, p in ((self.whi, u_hi, 0), (self.whi, u_lo, 1), (self.wlo, u_hi, 2)):
                        w = wt[:, j, k, m * P:(m + 1) * P]
                        head, last = kt == 0 and p == 0, kt == KT - 1 and p == 2
                        if lat:
                            mm = pe.matmul(self.lat[s][m][:], w, ut[:, kt, 0:LAT], start=head, stop=last)
                        if ctx:
                            mm = pe.matmul(self.ctx[s][:, m * CTX:(m + 1) * CTX], w, ut[:, kt, LAT if lat else 0:][:, 0:CTX],
                                           start=head and m == 0, stop=last, skip_group_check=True)
            mm.then_inc(self.unit_done, 1)




def norm_split(nc, dr, name, src, T, u_hi, u_lo, cols, segs, modulated=False):
    with Phase(nc, name) as ph:
        x = ph.sb("x", [P, KT, T])
        sq = ph.sb("sq", [P, 2, T])
        ones = ph.sb("ones", [P, P])
        rs = ph.sb("rs", [P, T])
        sc = ph.sb("sc", [P, len(segs), KT])
        banks = [(0, LAT if T > LAT else T)] + ([(LAT, CTX)] if T > LAT else [])
        pss = [ph.pb(f"pss{i}") for i in range(len(banks))]
        c_loaded, x_loaded = ph.sem("c_loaded"), [ph.sem(f"x_loaded{g}") for g in range(4)]
        sq_ready, sq_used, var_ready, root_ready = ph.sem("sq_ready"), ph.sem("sq_used"), ph.sem("var_ready"), ph.sem("root_ready")
        scaled, moved, hi_ready, scale_ready = ph.sem("scaled"), ph.sem("moved"), ph.sem("hi_ready"), ph.sem("scale_ready")
        x_v = src.rearrange("(k p) t -> p k t", p=P)

        with nc.Block() as block:
            @block.sync
            def _(sp):
                sp.dma_start(ones[:], dr.consts[:, C_ONES:C_ONES + P]).then_inc(c_loaded, 16)
                for g in range(4):
                    sp.dma_start(x[:, 4 * g:4 * g + 4, :], x_v[:, 4 * g:4 * g + 4, 0:T]).then_inc(x_loaded[g], 16)

            @block.scalar
            def _(act):
                for k in range(KT):
                    if k % 4 == 0:
                        act.wait_ge(x_loaded[k // 4], 16)
                    if k >= 2:
                        act.wait_ge(sq_used, k - 1)
                    act.activation(sq[:, k % 2, :], x[:, k, :], ACT.Square).then_inc(sq_ready, 1)
                act.wait_ge(var_ready, 1)
                act.activation(rs[:], rs[:], ACT.Sqrt).then_inc(root_ready, 1)
                act.wait_ge(scale_ready, 1)
                for k in range(KT):
                    act.wait_ge(scaled, k + 1)
                    for n, (t0, nt, _, shift) in enumerate(segs):
                        if shift is None:
                            op = act.activation(x[:, k, t0:t0 + nt], x[:, k, t0:t0 + nt], ACT.Copy, scale=sc[:, n, k:k + 1])
                        else:
                            op = act.activation(x[:, k, t0:t0 + nt], x[:, k, t0:t0 + nt], ACT.Identity,
                                                bias=shift[:, k:k + 1], scale=sc[:, n, k:k + 1])
                    op.then_inc(moved, 1)
                    act.wait_ge(moved, k + 1)
                    act.activation(u_hi[:, k, :], x[:, k, :], ACT.Copy).then_inc(hi_ready, 1)

            @block.tensor
            def _(pe):
                pe.wait_ge(c_loaded, 16)
                for k in range(KT):
                    pe.wait_ge(sq_ready, k + 1)
                    for i, (t0, nt) in enumerate(banks):
                        mm = pe.matmul(pss[i][:, 0:nt], ones[:], sq[:, k % 2, t0:t0 + nt], start=(k == 0), stop=(k == KT - 1))
                    mm.then_inc(sq_used, 1)

            @block.vector
            def _(dve):
                for n, (_, _, scale, _) in enumerate(segs):
                    if modulated:
                        dve.scalar_tensor_tensor(out=sc[:, n, :], in0=scale, scalar=1.0,
                                                 in1=cols[:, COL["pre_norm_w"]:COL["pre_norm_w"] + KT],
                                                 op0=ALU.add, op1=ALU.mult)
                    else:
                        dve.tensor_copy(sc[:, n, :], scale)
                dve.drain().then_inc(scale_ready, 1)
                dve.wait_ge(sq_used, KT)
                for i, (t0, nt) in enumerate(banks):
                    dve.tensor_scalar(rs[:, t0:t0 + nt], pss[i][:, 0:nt], 1.0 / D, EPS, ALU.mult, ALU.add)
                dve.drain().then_inc(var_ready, 1)
                dve.wait_ge(root_ready, 1)
                dve.reciprocal(rs[:], rs[:])
                dve.drain()
                for k in range(KT):
                    dve.tensor_tensor(x[:, k, :], x[:, k, :], rs[:], ALU.mult).then_inc(scaled, 1)
                    if k >= 1:
                        dve.wait_ge(hi_ready, k)
                        dve.tensor_tensor(u_lo[:, k - 1, :], x[:, k - 1, :], u_hi[:, k - 1, :].bitcast(F32), ALU.subtract)
                dve.wait_ge(hi_ready, KT)
                dve.tensor_tensor(u_lo[:, KT - 1, :], x[:, KT - 1, :], u_hi[:, KT - 1, :].bitcast(F32), ALU.subtract)


def project(nc, dr, cols, u_hi, u_lo):
    w_v = dr.w_in.rearrange("a (k p) n -> p (a k) n", p=P)
    GT = 3 * GDN_W // P
    SEGS = [
        (XBC // 256, OFF_XBC, True, COL["conv_ssd_w"], XBC // P, COL["conv_ssd_b"], dr.xbcT),
        (GDN_W // 256, OFF_QKV, False, COL["conv_gdn_w"], GT, None, dr.qT),
        (2 * GDN_W // 256, OFF_QKV + GDN_W, True, COL["conv_gdn_w"] + GDN_W // P, GT, None, dr.kvT),
        (D // 256, 0, False, None, None, None, dr.zT),
    ]
    with Phase(nc, "proj") as ph:
        st = Stream(ph)
        obuf = ph.sb("obuf", [P, 2, TOK])
        zeroed, center, taps_done = ph.sem("zeroed"), ph.sem("center"), ph.sem("taps_done")
        out_ready, stored = [ph.sem(f"out_ready{m}") for m in range(2)], [ph.sem(f"stored{m}") for m in range(2)]
        BASE = [1]
        for seg in SEGS:
            BASE.append(BASE[-1] + seg[0])
        CONVS = [0, SEGS[0][0], SEGS[0][0] + SEGS[1][0], SEGS[0][0] + SEGS[1][0] + SEGS[2][0]]

        with nc.Block() as block:
            @block.sync
            def _(sp):
                sp.wait_ge(zeroed, 1)
                st.load(sp, 0, [(0, w_v[:, :, OFF_DT:OFF_DT + BETA0]), (BETA0, w_v[:, :, OFF_BETA:OFF_BETA + NSMALL - BETA0])], first=True)
                for n, (nb, c0, *_) in enumerate(SEGS):
                    with sp.Fori(0, nb) as i:
                        st.load(sp, i + BASE[n], [(0, w_v[:, :, bass.ds(i * 256 + c0, 256)])])

            @block.gpsimd
            def _(pool):
                pool.memset(st.stage[:, :, :, NSMALL:P], 0.0).then_inc(zeroed, 1)
                pool.wait_ge(out_ready[0], 1)
                pool.dma_start(dr.smallT, obuf[0:NSMALL, 0, :]).then_inc(stored[0], 16)
                for n, (nb, _, ctx, _, _, _, out) in enumerate(SEGS):
                    T = TOK if ctx else LAT
                    with pool.Fori(0, nb) as i:
                        for m in range(2):
                            pool.wait_ge(out_ready[m], i + (BASE[n] + 1 - m))
                            pool.dma_start(out[bass.ds(i * 256 + m * P, P), :], obuf[:, m, 0:T]).then_inc(stored[m], 16)
                for m in range(2):
                    pool.wait_ge(stored[m], 16 * (BASE[-1] - m))

            @block.tensor
            def _(pe):
                st.products(pe, 0, 0, u_hi, u_lo, tiles=1)
                for n, (nb, _, ctx, *_) in enumerate(SEGS):
                    with pe.Fori(0, nb // 2) as i:
                        for c in range(2):
                            st.products(pe, i * 2 + (BASE[n] + c), (BASE[n] + c) % 2, u_hi, u_lo, ctx=ctx)

            @block.scalar
            def _(act):
                def written_out(b):
                    for m in range(2):
                        act.wait_ge(stored[m], (b - m + 1) * 16)

                def epilogue(n, i, c):
                    nb, _, ctx, wcol, step, bcol, _ = SEGS[n]
                    b, s = i * 2 + (BASE[n] + c), (BASE[n] + c) % 2
                    act.wait_ge(st.unit_done, b * 2 + 2)
                    if wcol is None:
                        for m in range(2):
                            act.activation(obuf[:, m, 0:LAT], st.lat[s][m][:], ACT.Silu).then_inc(out_ready[m], 1)
                        written_out(b)
                        return
                    for m in range(2):
                        mid = cols[:, bass.ds(i * 4 + (wcol + 2 * step + 2 * c + m), 1)]
                        for src, at, nt in ([(st.lat[s][m][:], 0, LAT)] + ([(st.ctx[s][:, m * CTX:(m + 1) * CTX], LAT, CTX)] if ctx else [])):
                            if bcol is None:
                                op = act.activation(obuf[:, m, at:at + nt], src, ACT.Copy, scale=mid)
                            else:
                                op = act.activation(obuf[:, m, at:at + nt], src, ACT.Identity, scale=mid,
                                                    bias=cols[:, bass.ds(i * 4 + (bcol + 2 * c + m), 1)])
                        op.then_inc(center, 1)
                    T = TOK if ctx else LAT
                    for m in range(2):
                        act.wait_ge(taps_done, i * 4 + (2 * CONVS[n] + 2 * c + m + 1))
                        act.activation(obuf[:, m, 0:T], obuf[:, m, 0:T], ACT.Silu).then_inc(out_ready[m], 1)
                    written_out(b)

                act.wait_ge(zeroed, 1)
                st.split_hi(act, 0, 32, n=P, first=True)
                st.split_hi(act, 1, 48)
                act.wait_ge(st.unit_done, 2)
                act.activation(obuf[:, 0, 0:LAT], st.lat[0][0][:], ACT.Copy)
                act.activation(obuf[:, 0, LAT:TOK], st.ctx[0][:, 0:CTX], ACT.Copy)
                act.drain().then_inc(out_ready[0], 1)
                act.wait_ge(stored[0], 16)
                for n in range(len(SEGS)):
                    last = n == len(SEGS) - 1
                    with act.Fori(0, SEGS[n][0] // 2 - last) as i:
                        for c in range(2):
                            b = i * 2 + (BASE[n] + c + 1)
                            st.split_hi(act, b, (b + 2) * 16)
                            epilogue(n, i, c)
                    if last:
                        i = SEGS[n][0] // 2 - 1
                        b = i * 2 + BASE[n] + 1
                        st.split_hi(act, b, (b + 2) * 16)
                        epilogue(n, i, 0)
                        epilogue(n, i, 1)

            @block.vector
            def _(dve):
                def taps(n, i, c):
                    nb, _, ctx, wcol, step, bcol, _ = SEGS[n]
                    if wcol is None:
                        dve.wait_ge(out_ready[1], i * 2 + (BASE[n] + c))
                        dve.sem_inc(st.bank_free, 1)
                        return
                    s = (BASE[n] + c) % 2
                    dve.wait_ge(center, i * 4 + (2 * CONVS[n] + 2 * c + 2))
                    for m in range(2):
                        views = [(st.lat[s][m][:].rearrange("p (r w) -> p r w", w=GRID),
                                  obuf[:, m, 0:LAT].rearrange("p (r w) -> p r w", w=GRID), GRID)]
                        if ctx:
                            views.append((st.ctx[s][:, m * CTX:(m + 1) * CTX].unsqueeze(1), obuf[:, m, LAT:TOK].unsqueeze(1), CTX))
                        for tap in (0, 1, 3, 4):
                            off = tap - TAPS // 2
                            a, z = max(0, -off), max(0, off)
                            if tap:
                                dve.drain()
                            for x, o, w in views:
                                op = dve.scalar_tensor_tensor(
                                    out=o[:, :, a:w - z], in0=x[:, :, a + off:w - z + off],
                                    scalar=cols[:, bass.ds(i * 4 + (wcol + tap * step + 2 * c + m), 1)],
                                    in1=o[:, :, a:w - z], op0=ALU.mult, op1=ALU.add)
                        op.then_inc(taps_done, 1)
                    dve.drain().then_inc(st.bank_free, 1)

                dve.sem_inc(st.bank_free, 2)
                st.split_lo(dve, 0, n=P)
                st.split_lo(dve, 1)
                dve.wait_ge(out_ready[0], 1)
                dve.sem_inc(st.bank_free, 1)
                for n in range(len(SEGS)):
                    last = n == len(SEGS) - 1
                    with dve.Fori(0, SEGS[n][0] // 2 - last) as i:
                        for c in range(2):
                            st.split_lo(dve, i * 2 + (BASE[n] + c + 1))
                            taps(n, i, c)
                    if last:
                        i = SEGS[n][0] // 2 - 1
                        st.split_lo(dve, i * 2 + BASE[n] + 1)
                        taps(n, i, 0)
                        taps(n, i, 1)



Q_NA, Q_EA, Q_NEA, Q_ETOT, Q_DT, Q_DTEND, Q_BETA, Q_NBETA, Q_BEND = range(9)
NQ = 9


def decays(nc, dr, tq, ident):
    with Phase(nc, "dec") as ph:
        raw = ph.sb("raw", [NSMALL, TOK])
        bias = ph.sb("bias", [NSMALL, 2])
        xs, ab, ex = ph.sb("xs", [NSMALL, TOK]), ph.sb("ab", [NSMALL, TOK]), ph.sb("ex", [NSMALL, TOK])
        u, ln, sg = ph.sb("u", [NSMALL, TOK]), ph.sb("ln", [NSMALL, TOK]), ph.sb("sg", [NSMALL, TOK])
        lnu = ph.sb("lnu", [NSMALL, TOK])
        rate = ph.sb("rate", [NSMALL, 1])
        cum = ph.sb("cum", [P, 3, P])
        lg, a, tot = ph.sb("lg", [P, NCH, NSMALL]), ph.sb("a", [P, NCH, NSMALL]), ph.sb("tot", [P, NCH, NSMALL])
        arow = ph.sb("arow", [NSMALL, TOK])
        bank = [ph.pb(f"bank{i}") for i in range(8)]
        zeroed, c_loaded, raw_loaded = ph.sem("zeroed"), ph.sem("c_loaded"), ph.sem("raw_loaded")
        d_done, a_done, p_done, stored = ph.sem("d_done"), ph.sem("a_done"), ph.sem("p_done"), ph.sem("stored")
        W = NCH * NSMALL

        def flat(t):
            return t.rearrange("p c r -> p (c r)")

        with nc.Block() as block:
            @block.sync
            def _(sp):
                sp.dma_start(raw[:], dr.smallT).then_inc(raw_loaded, 16)
                sp.dma_start(cum[:, 0:2, :], dr.consts[:, C_CUM:C_CUM + 2 * P].rearrange("p (n q) -> p n q", n=2)).then_inc(c_loaded, 16)
                sp.dma_start(cum[:, 2, :], dr.consts[:, C_ONES:C_ONES + P]).then_inc(c_loaded, 16)
                sp.wait_ge(zeroed, 1)
                for n, (s, g) in enumerate(((dr.ssd_dt_bias, dr.gdn_dt_bias), (dr.ssd_a_log, dr.gdn_a_log))):
                    sp.dma_start(bias[0:BETA0, n:n + 1], s.rearrange("a d h -> (d h) a")).then_inc(c_loaded, 16)
                    sp.dma_start(bias[ALPHA0:NSMALL, n:n + 1], g.rearrange("a d h -> (d h) a")).then_inc(c_loaded, 16)
                sp.wait_ge(d_done, 6)
                sp.dma_start(dr.arow, arow[:]).then_inc(stored, 16)
                sp.wait_ge(stored, 16)

            @block.vector
            def _(dve):
                dve.memset(bias[:], 0.0).then_inc(zeroed, 1)
                dve.wait_ge(c_loaded, 96)
                dve.wait_ge(raw_loaded, 16)
                dve.tensor_scalar(xs[:], raw[:], bias[:, 0:1], None, ALU.add).then_inc(d_done, 1)
                dve.wait_ge(a_done, 2)
                dve.tensor_scalar(u[:], ab[:], 1.0, None, ALU.add)
                dve.tensor_scalar(ex[:], ex[:], 1.0, None, ALU.add)
                dve.drain().then_inc(d_done, 1)
                dve.reciprocal(sg[:], ex[:])
                dve.tensor_scalar(ln[:], u[:], -1.0, None, ALU.add)
                dve.drain()
                dve.tensor_tensor(ln[:], ab[:], ln[:], ALU.subtract)
                dve.reciprocal(ex[:], u[:])
                dve.drain()
                dve.tensor_tensor(ln[:], ln[:], ex[:], ALU.mult)
                dve.tensor_scalar(xs[:], xs[:], 0.0, None, ALU.max)
                dve.drain()
                dve.tensor_tensor(xs[:], xs[:], ln[:], ALU.add)
                dve.wait_ge(a_done, 3)
                dve.drain()
                dve.tensor_tensor(xs[:], xs[:], lnu[:], ALU.add)
                dve.tensor_scalar(rate[:], rate[:], -1.0, None, ALU.mult)
                dve.drain()
                dve.tensor_scalar(ab[:], xs[:], rate[:], None, ALU.mult)
                dve.drain().then_inc(d_done, 1)
                dve.wait_ge(p_done, 1)
                dve.tensor_copy(flat(lg[:]), bank[0][:, 0:W])
                dve.tensor_copy(flat(tq[:, Q_DT]), bank[1][:, 0:W])
                dve.tensor_copy(flat(tq[:, Q_BETA]), bank[2][:, 0:W])
                dve.drain().then_inc(d_done, 1)
                dve.wait_ge(p_done, 2)
                dve.tensor_copy(flat(a[:]), bank[3][:, 0:W])
                dve.tensor_copy(flat(tot[:]), bank[5][:, 0:W])
                dve.drain()
                back = bank[4][:, 0:W].rearrange("p (c r) -> p c r", c=NCH)
                for r0, n in ((SSD_H, SSD_H), (ALPHA0 + GDN_H, GDN_H)):
                    dve.tensor_copy(a[:, :, r0:r0 + n], back[:, :, r0:r0 + n])
                dve.drain()
                dve.tensor_scalar(flat(tq[:, Q_NA]), flat(a[:]), -1.0, None, ALU.mult)
                dve.tensor_tensor(flat(lg[:]), flat(tot[:]), flat(a[:]), ALU.subtract)
                dve.tensor_scalar(flat(tq[:, Q_NBETA]), flat(tq[:, Q_BETA]), -1.0, None, ALU.mult)
                dve.drain().then_inc(d_done, 1)
                dve.wait_ge(p_done, 3)
                for n in range(2):
                    w = LAT if n == 0 else CTX
                    dve.tensor_copy(arow[:, n * LAT:n * LAT + w], bank[6 + n][0:NSMALL, 0:w])
                dve.drain().then_inc(d_done, 1)
                dve.wait_ge(a_done, 4)
                dve.tensor_scalar(flat(tq[:, Q_NEA]), flat(tq[:, Q_EA]), -1.0, None, ALU.mult)
                dve.tensor_tensor(flat(tq[:, Q_DTEND]), flat(tq[:, Q_DT]), flat(lg[:]), ALU.mult)
                dve.memset(tq[:, Q_BEND], 0.0)
                dve.drain()
                dve.tensor_tensor(tq[:, Q_BEND, :, BETA0:ALPHA0], tq[:, Q_BETA, :, BETA0:ALPHA0],
                                  lg[:, :, ALPHA0:NSMALL], ALU.mult)
                dve.drain()

            @block.scalar
            def _(act):
                act.wait_ge(d_done, 1)
                act.activation(ab[:], xs[:], ACT.Abs)
                act.activation(rate[:], bias[:, 1:2], ACT.Exp)
                act.activation(ex[:], raw[:], ACT.Exp, scale=-1.0).then_inc(a_done, 1)
                act.drain()
                act.activation(ab[:], ab[:], ACT.Exp, scale=-1.0).then_inc(a_done, 1)
                act.wait_ge(d_done, 2)
                act.activation(lnu[:], u[:], ACT.Ln).then_inc(a_done, 1)
                act.wait_ge(d_done, 5)
                act.activation(flat(tq[:, Q_EA]), flat(a[:]), ACT.Exp)
                act.activation(flat(tq[:, Q_ETOT]), flat(tot[:]), ACT.Exp)
                act.activation(flat(lg[:]), flat(lg[:]), ACT.Exp)
                act.drain().then_inc(a_done, 1)

            @block.tensor
            def _(pe):
                pe.wait_ge(d_done, 3)
                for n, src in enumerate((ab, xs, sg)):
                    for c in range(NCH):
                        mm = pe.transpose(bank[n][:, c * NSMALL:(c + 1) * NSMALL], src[:, c * P:(c + 1) * P],
                                          ident[0:NSMALL, 0:NSMALL])
                mm.then_inc(p_done, 1)
                pe.wait_ge(d_done, 4)
                for n in range(3):
                    mm = pe.matmul(bank[3 + n][:, 0:W], cum[:, n, :], flat(lg[:]), start=True, stop=True)
                mm.then_inc(p_done, 1)
                pe.wait_ge(d_done, 5)
                for c in range(NCH):
                    mm = pe.transpose(bank[6 + c // LCH][0:NSMALL, (c % LCH) * P:(c % LCH + 1) * P], a[:, c, :], ident[:])
                mm.then_inc(p_done, 1)


def ssd(nc, dr, cols, tq, ident):
    XT, NT = SSD_W // P, XBC // P
    GW = SSD_W // SSD_G
    HG = SSD_H // SSD_G
    with Phase(nc, "ssd") as ph:
        xT = ph.sb("xT", [P, NT, TOK])
        x_tok, b_tok = ph.sb("x_tok", [P, NCH, SSD_W]), ph.sb("b_tok", [P, NCH, SSD_G * SSD_N])
        cb = ph.sb("cb", [P, SSD_G, LCH, P])
        h = ph.sb("h", [P, 2, SSD_G, GW])
        y = ph.sb("y", [P, LCH, SSD_W])
        dsk = ph.sb("dsk", [P, SSD_H])
        neg = ph.sb("neg", [P, 2, P])
        ones = ph.sb("ones", [P, P])
        E = ph.sb("E", [P, 2, 2, LCH, P])
        M = ph.sb("M", [P, 2, 2, LCH, P])
        tmp, xw = ph.sb("tmp", [P, 2, GW]), ph.sb("xw", [P, 2, GW])
        zT, sq = ph.sb("zT", [P, XT, LAT]), ph.sb("sq", [P, 2, LAT])
        rs = ph.sb("rs", [P, SSD_G, LAT])
        tb = [ph.pb(f"tb{i}") for i in range(4)]
        pb = [ph.pb(f"pb{i}") for i in range(4)]
        loaded, c_loaded, z_loaded = ph.sem("loaded"), ph.sem("c_loaded"), ph.sem("z_loaded")
        turned, taken_d, taken_a = ph.sem("turned"), ph.sem("taken_d"), ph.sem("taken_a")
        cb_done, cb_taken, y_init = ph.sem("cb_done"), ph.sem("cb_taken"), ph.sem("y_init")
        yoff_done, tmp_ready, y_added = ph.sem("yoff_done"), ph.sem("tmp_ready"), ph.sem("y_added")
        xw_ready, st_done, h_ready = ph.sem("xw_ready"), ph.sem("st_done"), ph.sem("h_ready")
        e_loaded, e_masked = [ph.sem(f"e_loaded{j}") for j in range(2)], ph.sem("e_masked")
        e_ready, m_ready, diag_done, y_ready = ph.sem("e_ready"), ph.sem("m_ready"), ph.sem("diag_done"), ph.sem("y_ready")
        out_turned, gated, squared, summed = ph.sem("out_turned"), ph.sem("gated"), ph.sem("squared"), ph.sem("summed")
        var_ready, root_ready, out_ready, stored = ph.sem("var_ready"), ph.sem("root_ready"), ph.sem("out_ready"), ph.sem("stored")

        steps = [(t, d, g) for t in range(NCH) for d in range(2) for g in range(SSD_G)]
        lat_steps = [s for s in steps if t_lat(s)]
        st_steps = [s for s in steps if s[0] < NCH - 1]
        groups = []
        for c in range(NCH):
            groups += [(c, 0, 4), (c, 4, 4), (c, XT, SSD_G)]

        def heads(ap, n=SSD_P):
            return bc(ap, n, 2)

        with nc.Block() as block:
            @block.sync
            def _(sp):
                sp.dma_start(xT[:], dr.xbcT.rearrange("(k p) t -> p k t", p=P)).then_inc(loaded, 16)
                sp.dma_start(neg[:], dr.consts[:, C_NEG:C_NEG + 2 * P].rearrange("p (d q) -> p d q", d=2)).then_inc(c_loaded, 16)
                sp.dma_start(ones[:], dr.consts[:, C_ONES:C_ONES + P]).then_inc(c_loaded, 16)
                sp.dma_start(dsk[:], dr.ssd_d[0, :].partition_broadcast(P)).then_inc(c_loaded, 16)
                sp.dma_start(zT[:], dr.zT.rearrange("(k p) t -> p k t", p=P)[:, 0:XT, :]).then_inc(z_loaded, 16)
                for g in range(SSD_G):
                    with sp.Fori(0, HG // 2) as i:
                        for j in range(2):
                            n = i * 2 + (g * HG + j)
                            sp.wait_ge(m_ready, n + 1)
                            for d in range(2):
                                sp.dma_start(E[:, j, d, :, :].rearrange("p c q -> p (c q)"),
                                             dr.arow[bass.ds(n + d * SSD_H, 1), 0:LAT].rearrange("a t -> (a t)").partition_broadcast(P))\
                                    .then_inc(e_loaded[j], 16)
                for k in range(XT):
                    sp.wait_ge(out_ready, k + 1)
                    sp.dma_start(dr.yT[k * P:(k + 1) * P, :], zT[:, k, :]).then_inc(stored, 16)
                sp.wait_ge(stored, 16 * XT)

            @block.gpsimd
            def _(pool):
                pool.wait_ge(c_loaded, 48)
                pool.wait_ge(taken_d, len(groups) // 2)
                pool.wait_ge(taken_a, len(groups) // 2)
                for c in range(LCH):
                    op = pool.tensor_tensor(y[:, c, :].rearrange("p (h e) -> p h e", e=SSD_P),
                                            x_tok[:, c, :].rearrange("p (h e) -> p h e", e=SSD_P), heads(dsk[:]), ALU.mult)
                ns = ny = 0
                for t, d, g in steps:
                    c = SCAN[d][t]
                    if t < NCH - 1:
                        if ns >= 2:
                            pool.wait_ge(st_done, ns - 1)
                        r0 = d * SSD_H + g * HG
                        pool.tensor_tensor(xw[:, ns % 2, :].rearrange("p (h e) -> p h e", e=SSD_P),
                                           x_tok[:, c, g * GW:(g + 1) * GW].rearrange("p (h e) -> p h e", e=SSD_P),
                                           heads(tq[:, Q_DTEND, c, r0:r0 + HG]), ALU.mult).then_inc(xw_ready, 1)
                        ns += 1
                    if c < LCH:
                        pool.wait_ge(tmp_ready, ny + 1)
                        pool.drain()
                        at = y[:, c, g * GW:(g + 1) * GW]
                        pool.tensor_tensor(at, at, tmp[:, ny % 2, :], ALU.add).then_inc(y_added, 1)
                        ny += 1
                for g in range(SSD_G):
                    with pool.Fori(0, HG // 2) as i:
                        for j in range(2):
                            n = i * 2 + (g * HG + j)
                            pool.wait_ge(e_loaded[j], i * 32 + (g * HG // 2 * 32 + 32))
                            for d in range(2):
                                op = pool.tensor_tensor(E[:, j, d], E[:, j, d], bc(neg[:, d, :], LCH, 1), ALU.add)
                            op.then_inc(e_masked, 1)

            def sum_squares(pe, k):
                pe.wait_ge(squared, k + 1)
                g, n = k // 4, k % 4
                pe.matmul(pb[g][:], ones[:], sq[:, k % 2, :], start=(n == 0), stop=(n == 3)).then_inc(summed, 1)

            @block.tensor
            def _(pe):
                pe.wait_ge(loaded, 16)
                for q, (c, k0, n) in enumerate(groups):
                    if q >= 4:
                        pe.wait_ge(taken_a if q % 2 else taken_d, (q - 4) // 2 + 1)
                    for k in range(n):
                        mm = pe.transpose(tb[q % 4][:, k * P:(k + 1) * P], xT[:, k0 + k, c * P:(c + 1) * P], ident[:])
                    mm.then_inc(turned, 1)
                for g in range(SSD_G):
                    for c in range(LCH):
                        mm = pe.matmul(pb[g][:, c * P:(c + 1) * P], xT[:, XT + g, c * P:(c + 1) * P],
                                       xT[:, XT + SSD_G + g, c * P:(c + 1) * P], start=True, stop=True)
                    mm.then_inc(cb_done, 1)
                pe.wait_ge(taken_d, len(groups) // 2)
                pe.wait_ge(taken_a, len(groups) // 2)
                ns = ny = 0
                for t, d, g in steps:
                    c = SCAN[d][t]
                    if c < LCH:
                        pe.wait_ge(h_ready, steps.index((t - 1, d, g)) + 1)
                        if ny >= 2:
                            pe.wait_ge(tmp_ready, ny - 1)
                        pe.matmul(tb[ny % 2][:], xT[:, XT + SSD_G + g, c * P:(c + 1) * P], h[:, d, g, :],
                                  start=True, stop=True).then_inc(yoff_done, 1)
                        ny += 1
                    if t < NCH - 1:
                        pe.wait_ge(xw_ready, ns + 1)
                        if ns >= 2:
                            pe.wait_ge(h_ready, ns - 1)
                        pe.matmul(tb[2 + ns % 2][:], b_tok[:, c, g * P:(g + 1) * P], xw[:, ns % 2, :],
                                  start=True, stop=True).then_inc(st_done, 1)
                        ns += 1
                pe.wait_ge(cb_taken, 2)
                for g in range(SSD_G):
                    with pe.Fori(0, HG // 2) as i:
                        for j in range(2):
                            n = i * 2 + (g * HG + j)
                            pe.wait_ge(m_ready, n + 3)
                            pe.wait_ge(y_ready, n + 1)
                            for c in range(LCH):
                                for d in range(2):
                                    mm = pe.matmul(pb[2 + j][:, c * SSD_P:(c + 1) * SSD_P], M[:, j, d, c, :],
                                                   x_tok[:, c, bass.ds(i * 2 * SSD_P + (g * HG + j) * SSD_P, SSD_P)],
                                                   start=(d == 0), stop=(d == 1))
                            mm.then_inc(diag_done, 1)
                pe.wait_ge(y_ready, SSD_H + 2)
                for k in range(XT):
                    if k >= 4:
                        pe.wait_ge(gated, k - 3)
                    for c in range(LCH):
                        mm = pe.transpose(tb[k % 4][:, c * P:(c + 1) * P], y[:, c, k * P:(k + 1) * P], ident[:])
                    mm.then_inc(out_turned, 1)
                    if k >= 1:
                        sum_squares(pe, k - 1)
                sum_squares(pe, XT - 1)

            @block.scalar
            def _(act):
                for q, (c, k0, n) in enumerate(groups):
                    if q % 2 == 0:
                        continue
                    act.wait_ge(turned, q + 1)
                    dst = x_tok[:, c, k0 * P:(k0 + n) * P] if k0 < XT else b_tok[:, c, :]
                    act.activation(dst, tb[q % 4][:, 0:n * P], ACT.Copy).then_inc(taken_a, 1)
                for g in range(SSD_G):
                    act.wait_ge(cb_done, g + 1)
                    act.activation(cb[:, g].rearrange("p c q -> p (c q)"), pb[g][:], ACT.Copy).then_inc(cb_taken, 1)
                for g in range(SSD_G):
                    with act.Fori(0, HG // 2) as i:
                        for j in range(2):
                            n = i * 2 + (g * HG + j)
                            act.wait_ge(e_masked, n + 1)
                            for d in range(2):
                                for c in range(LCH):
                                    op = act.activation(E[:, j, d, c, :], E[:, j, d, c, :], ACT.Exp,
                                                        bias=tq[:, Q_NA, c, bass.ds(n + d * SSD_H, 1)])
                            op.then_inc(e_ready, 1)
                act.wait_ge(gated, 1)
                for k in range(XT):
                    act.wait_ge(gated, k + 1)
                    if k >= 2:
                        act.wait_ge(summed, k - 1)
                    act.activation(sq[:, k % 2, :], zT[:, k, :], ACT.Square).then_inc(squared, 1)
                act.wait_ge(var_ready, 1)
                act.activation(rs[:], rs[:], ACT.Sqrt).then_inc(root_ready, 1)

            @block.vector
            def _(dve):
                for q, (c, k0, n) in enumerate(groups):
                    if q % 2 == 1:
                        continue
                    dve.wait_ge(turned, q + 1)
                    dst = x_tok[:, c, k0 * P:(k0 + n) * P] if k0 < XT else b_tok[:, c, :]
                    dve.tensor_copy(dst, tb[q % 4][:, 0:n * P]).then_inc(taken_d, 1)
                ns = ny = 0
                for t, d, g in steps:
                    c = SCAN[d][t]
                    r0 = d * SSD_H + g * HG
                    if c < LCH:
                        dve.wait_ge(yoff_done, ny + 1)
                        if ny >= 2:
                            dve.wait_ge(y_added, ny - 1)
                        dve.tensor_tensor(tmp[:, ny % 2, :].rearrange("p (h e) -> p h e", e=SSD_P),
                                          tb[ny % 2][:].rearrange("p (h e) -> p h e", e=SSD_P),
                                          heads(tq[:, Q_EA, c, r0:r0 + HG]), ALU.mult).then_inc(tmp_ready, 1)
                        ny += 1
                    if t < NCH - 1:
                        hs = h[:, d, g, :]
                        dve.wait_ge(st_done, ns + 1)
                        if t == 0:
                            dve.tensor_copy(hs, tb[2 + ns % 2][:]).then_inc(h_ready, 1)
                        else:
                            dve.tensor_tensor(hs.rearrange("p (h e) -> p h e", e=SSD_P), hs.rearrange("p (h e) -> p h e", e=SSD_P),
                                              heads(tq[:, Q_ETOT, c, r0:r0 + HG]), ALU.mult)
                            dve.drain()
                            dve.tensor_tensor(hs, hs, tb[2 + ns % 2][:], ALU.add).then_inc(h_ready, 1)
                        ns += 1
                dve.sem_inc(m_ready, 2)
                dve.sem_inc(y_ready, 2)
                dve.wait_ge(cb_taken, 2)
                dve.wait_ge(y_added, len(lat_steps))

                def add_head(i, j, g, n):
                    dve.wait_ge(diag_done, n + 1)
                    at = y[:, :, bass.ds(i * 2 * SSD_P + (g * HG + j) * SSD_P, SSD_P)]
                    dve.tensor_tensor(at, at, pb[2 + j][:, 0:LCH * SSD_P].rearrange("p (c e) -> p c e", c=LCH), ALU.add)\
                        .then_inc(y_ready, 1)

                for g in range(SSD_G):
                    with dve.Fori(0, HG // 2) as i:
                        for j in range(2):
                            n = i * 2 + (g * HG + j)
                            dve.wait_ge(e_ready, n + 1)
                            dve.wait_ge(y_ready, n + 1)
                            for d in range(2):
                                for c in range(LCH):
                                    op = dve.scalar_tensor_tensor(out=M[:, j, d, c, :], in0=E[:, j, d, c, :],
                                                                  scalar=tq[:, Q_DT, c, bass.ds(n + d * SSD_H, 1)],
                                                                  in1=cb[:, g, c, :], op0=ALU.mult, op1=ALU.mult)
                            op.then_inc(m_ready, 1)
                        for j in range(2):
                            add_head(i, j, g, i * 2 + (g * HG + j))
                dve.wait_ge(z_loaded, 16)
                for k in range(XT):
                    dve.wait_ge(out_turned, k + 1)
                    dve.tensor_tensor(zT[:, k, :], tb[k % 4][:], zT[:, k, :], ALU.mult).then_inc(gated, 1)
                dve.wait_ge(summed, XT)
                for g in range(SSD_G):
                    dve.tensor_scalar(rs[:, g, :], pb[g][:], 1.0 / GW, EPS, ALU.mult, ALU.add)
                dve.drain().then_inc(var_ready, 1)
                dve.wait_ge(root_ready, 1)
                dve.reciprocal(rs[:], rs[:])
                dve.drain()
                for k in range(XT):
                    dve.scalar_tensor_tensor(out=zT[:, k, :], in0=zT[:, k, :], scalar=cols[:, COL["ssd_norm_w"] + k:COL["ssd_norm_w"] + k + 1],
                                             in1=rs[:, k // 4, :], op0=ALU.mult, op1=ALU.mult).then_inc(out_ready, 1)


def gdn(nc, dr, cols, tq, ident):
    HG = 4
    GW = HG * P
    LV = NLEVEL - 1
    ZT = SSD_W // P
    with Phase(nc, "gdn") as ph:
        qT, kT, vT = ph.sb("qT", [P, HG, LAT]), ph.sb("kT", [P, HG, TOK]), ph.sb("vT", [P, HG, TOK])
        zT = ph.sb("zT", [P, HG, LAT])
        sq = ph.sb("sq", [P, 2, TOK])
        k_tok, v_tok = ph.sb("k_tok", [P, NCH, GW]), ph.sb("v_tok", [P, NCH, GW])
        kk, kq = ph.sb("kk", [P, NCH, GW]), ph.sb("kq", [P, LCH, GW])
        E = ph.sb("E", [P, 2, HG, NCH, P])
        neg, strict = ph.sb("neg", [P, 2, P]), ph.sb("strict", [P, 2, P])
        level = ph.sb("level", [P, 2, NLEVEL, P])
        ones = ph.sb("ones", [P, P])
        idb = ph.sb("idb", [P, HG, P], BF16)
        AT, T, TT, Q = (ph.sb(n, [P, 2, GW]) for n in ("AT", "T", "TT", "Q"))
        attn, r, vn, vp, S = (ph.sb(n, [P, 2, GW]) for n in ("attn", "r", "vn", "vp", "S"))
        o = ph.sb("o", [P, LCH, GW])
        var = ph.sb("var", [P, LCH * HG])
        eps = ph.sb("eps", [P, 2])
        Pm, Tp, TTp, X = ([ph.pb(f"{n}{d}") for d in range(2)] for n in ("Pm", "Tp", "TTp", "X"))

        def two(name):
            return [ph.sem(f"{name}{d}") for d in range(2)]

        q_loaded, k_loaded, v_loaded, z_loaded = (ph.sem(n) for n in ("q_loaded", "k_loaded", "v_loaded", "z_loaded"))
        e_loaded, e_masked, e_ready = two("e_loaded"), ph.sem("e_masked"), ph.sem("e_ready")
        c_loaded, idb_ready, eps_ready = ph.sem("c_loaded"), ph.sem("idb_ready"), ph.sem("eps_ready")
        squared, summed, logged, inverted, unit = (ph.sem(n) for n in ("squared", "summed", "logged", "inverted", "unit"))
        group_done, taken_d, taken_a = (ph.sem(n) for n in ("group_done", "taken_d", "taken_a"))
        es_ready, at_ready, tt0_ready, attn_ready = (two(n) for n in ("es_ready", "at_ready", "tt0_ready", "attn_ready"))
        pm_done, q_ready, t_ready, tp_done, ttp_done, tt_ready = (
            two(n) for n in ("pm_done", "q_ready", "t_ready", "tp_done", "ttp_done", "tt_ready"))
        ks_done, qs_done, r_ready, y_done, vp_ready, vn_ready = (
            two(n) for n in ("ks_done", "qs_done", "r_ready", "y_done", "vp_ready", "vn_ready"))
        ds_done, av_done, s_ready, o_done = (two(n) for n in ("ds_done", "av_done", "s_ready", "o_done"))
        osq_ready, var_ready, std_ready, inv_ready, o_normed = (
            ph.sem(n) for n in ("osq_ready", "var_ready", "std_ready", "inv_ready", "o_normed"))
        o_turned, out_ready, stored, turn_over = ph.sem("o_turned"), ph.sem("out_ready"), ph.sem("stored"), ph.sem("turn_over")

        NT = 2 * HG
        banks4 = [X[0], X[1], TTp[0], TTp[1]]
        groups = [("v", c) for c in range(NCH)] + [("k", c) for c in range(NCH)] \
            + [("kk", c) for c in range(NCH)] + [("kq", c) for c in range(LCH)]
        NG = len(groups)
        lat_before = [max(0, t - CCH) for t in range(NCH)]

        def per_head(ap):
            return ap.rearrange("p (h e) -> p h e", h=HG)

        def tile_of(n):
            return (qT, n, LAT) if n < HG else (kT, n - HG, TOK)

        def norm_of(n):
            return kq[:, n, 0:LAT] if n < HG else kk[:].rearrange("p c e -> p (c e)")[:, (n - HG) * TOK:(n - HG + 1) * TOK]

        def group_dst(q):
            kind, c = groups[q]
            return {"v": v_tok, "k": k_tok, "kk": kk, "kq": kq}[kind][:, c, :]

        with nc.Block() as block:
            @block.sync
            def _(sp):
                def const(t, at, n):
                    sp.dma_start(t, dr.consts[:, at:at + n * P].rearrange("p (n q) -> p n q", n=n)).then_inc(c_loaded, 16)

                const(neg[:], C_NEG, 2)
                const(strict[:], C_STRICT, 2)
                const(level[:].rearrange("p d v q -> p (d v) q"), C_LEVEL, 2 * NLEVEL)
                const(ones[:].unsqueeze(1), C_ONES, 1)
                with sp.Fori(0, GDN_H // HG) as i:
                    rows = bass.ds(i * GW, GW)
                    for dst, src, sem in ((qT, dr.qT, q_loaded), (kT, dr.kvT, k_loaded)):
                        sp.dma_start(dst[:], src[rows, :].rearrange("(k p) t -> p k t", p=P)).then_inc(sem, 16)
                    sp.dma_start(vT[:], dr.kvT[bass.ds(i * GW + GDN_W, GW), :].rearrange("(k p) t -> p k t", p=P)).then_inc(v_loaded, 16)
                    for d in range(2):
                        sp.dma_start(E[:, d].rearrange("p h c q -> p (h c q)"),
                                     dr.arow[bass.ds(i * HG + (ALPHA0 + d * GDN_H), HG), :].rearrange("a t -> (a t)").partition_broadcast(P))\
                            .then_inc(e_loaded[d], 16)
                    sp.dma_start(zT[:], dr.zT[bass.ds(i * GW + SSD_W, GW), :].rearrange("(k p) t -> p k t", p=P)).then_inc(z_loaded, 16)
                    for h in range(HG):
                        sp.wait_ge(out_ready, i * HG + (h + 1))
                        sp.dma_start(dr.yT[bass.ds(i * GW + (SSD_W + h * P), P), :], zT[:, h, :]).then_inc(stored, 16)
                    sp.wait_ge(stored, i * (16 * HG) + 16 * HG)
                    sp.sem_inc(turn_over, 1)

            @block.gpsimd
            def _(pool):
                pool.wait_ge(c_loaded, 64)
                pool.tensor_copy(idb[:], bc(ident[:], HG, 1)).then_inc(idb_ready, 1)
                with pool.Fori(0, GDN_H // HG) as i:
                    for d in range(2):
                        pool.wait_ge(e_loaded[d], i * 16 + 16)
                        flat = E[:, d].rearrange("p h c q -> p (h c) q")
                        pool.tensor_tensor(flat, flat, bc(neg[:, d, :], HG * NCH, 1), ALU.add).then_inc(e_masked, 1)
                    pool.memset(o[:], 0.0)
                    for n in range(NT):
                        pool.wait_ge(inverted, i * NT + (n + 1))
                        x, h, _ = tile_of(n)
                        pool.tensor_tensor(x[:, h, :], x[:, h, :], norm_of(n), ALU.mult).then_inc(unit, 1)
                    pool.wait_ge(taken_d, i * (NG // 2) + NG // 2)
                    pool.wait_ge(taken_a, i * (NG // 2) + NG // 2)
                    for t in range(NCH):
                        for d in range(2):
                            c = SCAN[d][t]
                            pool.wait_ge(e_ready, i * 2 + (d + 1))
                            if t:
                                pool.wait_ge(pm_done[d], i * (NCH * NLEVEL) + t * NLEVEL)
                            pool.tensor_tensor(per_head(AT[:, d, :]), E[:, d, :, c, :], bc(strict[:, d, :], HG, 1), ALU.mult)\
                                .then_inc(es_ready[d], 1)
                        for d in range(2):
                            c = SCAN[d][t]
                            pool.wait_ge(at_ready[d], i * NCH + (t + 1))
                            if t:
                                pool.wait_ge(y_done[d], i * NCH + t)
                            pool.tensor_tensor(per_head(TT[:, d, :]), per_head(AT[:, d, :]), bc(level[:, 1 - d, 0, :], HG, 1), ALU.mult)
                            pool.drain()
                            pool.tensor_tensor(per_head(TT[:, d, :]), per_head(TT[:, d, :]), bc(ident[:], HG, 1), ALU.add)\
                                .then_inc(tt0_ready[d], 1)
                        for d in range(2):
                            c = SCAN[d][t]
                            if c < LCH:
                                if lat_before[t]:
                                    pool.wait_ge(av_done[d], i * LCH + lat_before[t])
                                pool.tensor_tensor(per_head(attn[:, d, :]), E[:, d, :, c, :], per_head(kq[:, c, :]), ALU.mult)\
                                    .then_inc(attn_ready[d], 1)
                    for d in range(2):
                        pool.wait_ge(o_done[d], i * LCH + LCH)
                    for c in range(LCH):
                        op = pool.tensor_tensor(kq[:, c, :], o[:, c, :], o[:, c, :], ALU.mult)
                    op.then_inc(osq_ready, 1)
                    pool.wait_ge(inv_ready, i + 1)
                    for c in range(LCH):
                        pool.tensor_tensor(per_head(o[:, c, :]), per_head(o[:, c, :]),
                                           bc(var[:, c * HG:(c + 1) * HG], P, 2), ALU.mult).then_inc(o_normed, 1)

            @block.tensor
            def _(pe):
                pe.wait_ge(c_loaded, 64)
                pe.wait_ge(idb_ready, 1)
                with pe.Fori(0, GDN_H // HG) as i:
                    def w(sem, per, n):
                        pe.wait_ge(sem, i * per + n)

                    for n in range(NT):
                        w(squared, NT, n + 1)
                        if n >= 2:
                            w(logged, NT, n - 1)
                        _, _, wd = tile_of(n)
                        mm = pe.matmul(Pm[n % 2][:], ones[:], sq[:, n % 2, 0:LAT], start=True, stop=True)
                        if wd > LAT:
                            mm = pe.matmul(Tp[n % 2][:, 0:CTX], ones[:], sq[:, n % 2, LAT:TOK], start=True, stop=True)
                        mm.then_inc(summed, 1)
                    w(v_loaded, 16, 16)
                    for q, (kind, c) in enumerate(groups):
                        if kind == "k" and c == 0:
                            w(unit, NT, NT)
                        if q >= 4:
                            w(taken_a if q % 2 else taken_d, NG // 2, (q - 4) // 2 + 1)
                        for h in range(HG):
                            out, at = banks4[q % 4][:, h * P:(h + 1) * P], slice(c * P, (c + 1) * P)
                            if kind in "vk" and kind != "kk":
                                mm = pe.transpose(out, (vT if kind == "v" else kT)[:, h, at], ident[:])
                            else:
                                mm = pe.matmul(out, kT[:, h, at], (kT if kind == "kk" else qT)[:, h, at], start=True, stop=True)
                        mm.then_inc(group_done, 1)
                    w(taken_a, NG // 2, NG // 2)
                    w(taken_d, NG // 2, NG // 2)

                    def grow(t, d, v):
                        if v == 0:
                            w(at_ready[d], NCH, t + 1)
                            if t:
                                w(s_ready[d], NCH - 1, t)
                        else:
                            w(t_ready[d], NCH * LV, t * LV + v)
                        pe.matmul(Pm[d][:], idb[:, 0, :], idb[:].rearrange("p h e -> p (h e)"), start=True, stop=False, skip_group_check=True)
                        for h in range(HG):
                            at = slice(h * P, (h + 1) * P)
                            mm = pe.matmul(Pm[d][:, at], AT[:, d, at], ident[:] if v == 0 else T[:, d, at], start=False,
                                           stop=(h == HG - 1), skip_group_check=True)
                        mm.then_inc(pm_done[d], 1)

                    def update(t, d, v):
                        w(q_ready[d], NCH * LV, t * LV + v)
                        if v == 1:
                            w(tt0_ready[d], NCH, t + 1)
                            if lat_before[t] > 0:
                                w(o_done[d], LCH, lat_before[t])
                        else:
                            w(tt_ready[d], NCH * LV, t * LV + v - 1)
                        if v < LV:
                            for h in range(HG):
                                at = slice(h * P, (h + 1) * P)
                                mm = pe.matmul(Tp[d][:, at], TT[:, d, at], Q[:, d, at], start=True, stop=True)
                            mm.then_inc(tp_done[d], 1)
                        for h in range(HG):
                            at = slice(h * P, (h + 1) * P)
                            mm = pe.matmul(TTp[d][:, at], Q[:, d, at], TT[:, d, at], start=True, stop=True)
                        mm.then_inc(ttp_done[d], 1)

                    def heads_product(bank, lhs, rhs, sem):
                        for h in range(HG):
                            mm = pe.matmul(bank[:, h * P:(h + 1) * P], lhs(h), rhs[:, h * P:(h + 1) * P], start=True, stop=True)
                        mm.then_inc(sem, 1)

                    for t in range(NCH):
                        for v in range(NLEVEL):
                            for d in range(2):
                                grow(t, d, v)
                            if v:
                                for d in range(2):
                                    update(t, d, v)
                        for d in range(2):
                            c = SCAN[d][t]
                            at = slice(c * P, (c + 1) * P)
                            w(q_ready[d], NCH * LV, (t + 1) * LV)
                            w(tt_ready[d], NCH * LV, (t + 1) * LV)
                            if t:
                                heads_product(Pm[d], lambda h: kT[:, h, at], S[:, d, :], ks_done[d])
                            if c < LCH:
                                heads_product(TTp[d], lambda h: qT[:, h, at], S[:, d, :], qs_done[d])
                        for d in range(2):
                            w(r_ready[d], NCH, t + 1)
                            heads_product(Tp[d], lambda h: TT[:, d, h * P:(h + 1) * P], r[:, d, :], y_done[d])
                        for d in range(2):
                            c = SCAN[d][t]
                            if t < NCH - 1:
                                w(vp_ready[d], NCH - 1, t + 1)
                                heads_product(Pm[d], lambda h: k_tok[:, c, h * P:(h + 1) * P], vp[:, d, :], ds_done[d])
                            if c < LCH:
                                w(vn_ready[d], LCH, lat_before[t] + 1)
                                w(attn_ready[d], LCH, lat_before[t] + 1)
                                heads_product(X[d], lambda h: attn[:, d, h * P:(h + 1) * P], vn[:, d, :], av_done[d])
                    w(o_done[0], LCH, LCH)
                    w(o_done[1], LCH, LCH)
                    w(o_normed, LCH, LCH)
                    for h in range(HG):
                        for c in range(LCH):
                            mm = pe.transpose(banks4[h][:, c * P:(c + 1) * P], o[:, c, h * P:(h + 1) * P], ident[:])
                        mm.then_inc(o_turned, 1)

            @block.scalar
            def _(act):
                act.wait_ge(eps_ready, 1)
                with act.Fori(0, GDN_H // HG) as i:
                    act.wait_ge(q_loaded, i * 16 + 16)

                    def log_of(n):
                        act.wait_ge(summed, i * NT + (n + 1))
                        for bank, at, nt in ((Pm, 0, LAT), (Tp, LAT, CTX)):
                            if at < tile_of(n)[2]:
                                op = act.activation(norm_of(n)[:, at:at + nt], bank[n % 2][:, 0:nt], ACT.Ln,
                                                    bias=eps[:, 0:1] if n < HG else eps[:, 1:2], scale=float(P) if n < HG else 1.0)
                        op.then_inc(logged, 1)

                    for n in range(NT):
                        if n == HG:
                            act.wait_ge(k_loaded, i * 16 + 16)
                        x, h, wd = tile_of(n)
                        if n >= 2:
                            act.wait_ge(summed, i * NT + (n - 1))
                        act.activation(sq[:, n % 2, 0:wd], x[:, h, :], ACT.Square).then_inc(squared, 1)
                        if n:
                            log_of(n - 1)
                    log_of(NT - 1)
                    act.drain()
                    for n in range(NT):
                        act.activation(norm_of(n), norm_of(n), ACT.Exp, scale=-0.5).then_inc(inverted, 1)
                    for d in range(2):
                        act.wait_ge(e_masked, i * 2 + (d + 1))
                        for h in range(HG):
                            for c in range(NCH):
                                op = act.activation(E[:, d, h, c, :], E[:, d, h, c, :], ACT.Exp,
                                                    bias=tq[:, Q_NA, c, bass.ds(i * HG + (ALPHA0 + d * GDN_H + h), 1)])
                        op.then_inc(e_ready, 1)
                    for q in range(1, NG, 2):
                        act.wait_ge(group_done, i * NG + (q + 1))
                        act.activation(group_dst(q), banks4[q % 4][:], ACT.Copy).then_inc(taken_a, 1)
                    for t in range(NCH):
                        for v in range(1, NLEVEL):
                            for d in range(2):
                                act.wait_ge(ttp_done[d], i * (NCH * LV) + (t * LV + v))
                                act.activation(TT[:, d, :], TTp[d][:], ACT.Copy).then_inc(tt_ready[d], 1)
                    act.wait_ge(var_ready, i + 1)
                    act.activation(var[:], var[:], ACT.Sqrt).then_inc(std_ready, 1)

            @block.vector
            def _(dve):
                dve.memset(eps[:, 0:1], EPS * P)
                dve.memset(eps[:, 1:2], EPS)
                dve.drain().then_inc(eps_ready, 1)
                dve.wait_ge(c_loaded, 64)
                with dve.Fori(0, GDN_H // HG) as i:
                    def w(sem, per, n):
                        dve.wait_ge(sem, i * per + n)

                    def col(q, c, d, h, first, n=1):
                        return tq[:, q, c, bass.ds(i * HG + (first + d * GDN_H + h), n)]

                    for q in range(0, NG, 2):
                        w(group_done, NG, q + 1)
                        dve.tensor_copy(group_dst(q), banks4[q % 4][:]).then_inc(taken_d, 1)
                    w(taken_a, NG // 2, NG // 2)
                    for t in range(NCH):
                        for d in range(2):
                            c = SCAN[d][t]
                            w(es_ready[d], NCH, t + 1)
                            for h in range(HG):
                                at = slice(h * P, (h + 1) * P)
                                op = dve.scalar_tensor_tensor(out=AT[:, d, at], in0=AT[:, d, at], scalar=col(Q_NBETA, c, d, h, BETA0),
                                                              in1=kk[:, c, at], op0=ALU.mult, op1=ALU.mult)
                            op.then_inc(at_ready[d], 1)
                        for d in range(2):
                            w(pm_done[d], NCH * NLEVEL, t * NLEVEL + 1)
                            dve.tensor_tensor(per_head(T[:, d, :]), per_head(Pm[d][:]), bc(level[:, d, 0, :], HG, 1), ALU.mult)\
                                .then_inc(t_ready[d], 1)
                        for v in range(1, NLEVEL):
                            for d in range(2):
                                w(pm_done[d], NCH * NLEVEL, t * NLEVEL + v + 1)
                                if t * LV + v > 1:
                                    w(ttp_done[d], NCH * LV, t * LV + v - 1)
                                dve.tensor_tensor(per_head(Q[:, d, :]), per_head(Pm[d][:]), bc(level[:, d, v, :], HG, 1), ALU.mult)\
                                    .then_inc(q_ready[d], 1)
                            if v < LV:
                                for d in range(2):
                                    w(tp_done[d], NCH * (LV - 1), t * (LV - 1) + v)
                                    dve.tensor_copy(T[:, d, :], Tp[d][:]).then_inc(t_ready[d], 1)
                        for d in range(2):
                            c = SCAN[d][t]
                            if t:
                                w(ks_done[d], NCH - 1, t)
                                for h in range(HG):
                                    at = slice(h * P, (h + 1) * P)
                                    op = dve.scalar_tensor_tensor(out=r[:, d, at], in0=Pm[d][:, at], scalar=col(Q_NEA, c, d, h, ALPHA0),
                                                                  in1=v_tok[:, c, at], op0=ALU.mult, op1=ALU.add)
                            else:
                                op = dve.tensor_copy(r[:, d, :], v_tok[:, c, :])
                            op.then_inc(r_ready[d], 1)
                        for d in range(2):
                            c = SCAN[d][t]
                            w(y_done[d], NCH, t + 1)
                            if t < NCH - 1:
                                dve.tensor_tensor(per_head(vp[:, d, :]), per_head(Tp[d][:]),
                                                  bc(col(Q_BEND, c, d, 0, BETA0, HG), P, 2), ALU.mult).then_inc(vp_ready[d], 1)
                            if c < LCH:
                                dve.tensor_tensor(per_head(vn[:, d, :]), per_head(Tp[d][:]),
                                                  bc(col(Q_BETA, c, d, 0, BETA0, HG), P, 2), ALU.mult).then_inc(vn_ready[d], 1)
                        for d in range(2):
                            c = SCAN[d][t]
                            if c < LCH:
                                w(qs_done[d], LCH, lat_before[t] + 1)
                            if t < NCH - 1:
                                w(ds_done[d], NCH - 1, t + 1)
                                if t == 0:
                                    op = dve.tensor_copy(S[:, d, :], Pm[d][:])
                                else:
                                    for h in range(HG):
                                        at = slice(h * P, (h + 1) * P)
                                        op = dve.scalar_tensor_tensor(out=S[:, d, at], in0=S[:, d, at], scalar=col(Q_ETOT, c, d, h, ALPHA0),
                                                                      in1=Pm[d][:, at], op0=ALU.mult, op1=ALU.add)
                                op.then_inc(s_ready[d], 1)
                        for d in range(2):
                            c = SCAN[d][t]
                            if c < LCH:
                                for h in range(HG):
                                    at = slice(h * P, (h + 1) * P)
                                    dve.scalar_tensor_tensor(out=o[:, c, at], in0=TTp[d][:, at], scalar=col(Q_EA, c, d, h, ALPHA0),
                                                             in1=o[:, c, at], op0=ALU.mult, op1=ALU.add)
                                dve.drain()
                                w(av_done[d], LCH, lat_before[t] + 1)
                                dve.tensor_tensor(o[:, c, :], o[:, c, :], X[d][:], ALU.add).then_inc(o_done[d], 1)
                                dve.drain()
                    w(osq_ready, 1, 1)
                    dve.tensor_reduce(var[:], kq[:].rearrange("p c (h e) -> p (c h) e", h=HG), AX.X, ALU.add)
                    dve.drain()
                    dve.tensor_scalar(var[:], var[:], 1.0 / P, EPS, ALU.mult, ALU.add).then_inc(var_ready, 1)
                    w(std_ready, 1, 1)
                    dve.reciprocal(var[:], var[:]).then_inc(inv_ready, 1)
                    w(z_loaded, 16, 16)
                    for h in range(HG):
                        w(o_turned, HG, h + 1)
                        dve.scalar_tensor_tensor(out=zT[:, h, :], in0=banks4[h][:], scalar=cols[:, COL["gdn_norm_w"]:COL["gdn_norm_w"] + 1],
                                                 in1=zT[:, h, :], op0=ALU.mult, op1=ALU.mult).then_inc(out_ready, 1)


def t_lat(step):
    return step[0] >= CCH


def project_plain(nc, dr, name, w_v, T, u_hi, u_lo, pairs, out):
    with Phase(nc, name) as ph:
        st = Stream(ph, ctx=T < LAT)
        obuf = ph.sb("obuf", [P, 2, 2, T])
        out_ready, stored = ph.sem("out_ready"), [ph.sem(f"stored{c}") for c in range(2)]
        BASE = [0]
        for pair in pairs:
            BASE.append(BASE[-1] + 2 * pair[0])

        def bank(s, m):
            return st.lat[s][m][:] if T == LAT else st.ctx[s][:, m * CTX:(m + 1) * CTX]

        with nc.Block() as block:
            @block.sync
            def _(sp):
                for n, (turns, ca, cb, _, _) in enumerate(pairs):
                    if n == 0:
                        st.load(sp, 0, [(0, w_v[:, :, ca:ca + 256])], first=True)
                        st.load(sp, 1, [(0, w_v[:, :, cb:cb + 256])])
                    with sp.Fori(1 if n == 0 else 0, turns) as i:
                        for c, col in enumerate((ca, cb)):
                            st.load(sp, i * 2 + (BASE[n] + c), [(0, w_v[:, :, bass.ds(i * 256 + col, 256)])])

            @block.gpsimd
            def _(pool):
                for n, (turns, ca, cb, _, _) in enumerate(pairs):
                    with pool.Fori(0, turns) as i:
                        for c, col in enumerate((ca, cb)):
                            pool.wait_ge(out_ready, i * 4 + (2 * BASE[n] + 2 * c + 2))
                            pool.dma_start(out[bass.ds(i * 256 + col, 256), :].rearrange("(m p) t -> p m t", p=P),
                                           obuf[:, c, :, :]).then_inc(stored[c], 16)
                for c in range(2):
                    pool.wait_ge(stored[c], 8 * BASE[-1])

            @block.tensor
            def _(pe):
                for n, (turns, *_) in enumerate(pairs):
                    with pe.Fori(0, turns) as i:
                        for c in range(2):
                            st.products(pe, i * 2 + (BASE[n] + c), c, u_hi, u_lo, lat=T == LAT, ctx=T < LAT)

            @block.scalar
            def _(act):
                def epilogue(n, i, c):
                    func = pairs[n][3 + c]
                    act.wait_ge(st.unit_done, i * 4 + (2 * BASE[n] + 2 * c + 2))
                    for m in range(2):
                        act.activation(obuf[:, c, m, :], bank(c, m), func).then_inc(out_ready, 1)
                    act.wait_ge(stored[c], i * 16 + 8 * BASE[n] + 16)

                st.split_hi(act, 0, 16, first=True)
                for n in range(len(pairs)):
                    last = n == len(pairs) - 1
                    with act.Fori(0, pairs[n][0] - last) as i:
                        for c in range(2):
                            st.split_hi(act, i * 2 + (BASE[n] + c + 1), i * 32 + 16 * (BASE[n] + c + 2))
                            epilogue(n, i, c)
                    if last:
                        i = pairs[n][0] - 1
                        st.split_hi(act, i * 2 + BASE[n] + 1, i * 32 + 16 * (BASE[n] + 2))
                        epilogue(n, i, 0)
                        epilogue(n, i, 1)

            @block.vector
            def _(dve):
                def free(n, i, c):
                    dve.wait_ge(out_ready, i * 4 + (2 * BASE[n] + 2 * c + 2))
                    dve.sem_inc(st.bank_free, 1)

                dve.sem_inc(st.bank_free, 2)
                st.split_lo(dve, 0)
                for n in range(len(pairs)):
                    last = n == len(pairs) - 1
                    with dve.Fori(0, pairs[n][0] - last) as i:
                        for c in range(2):
                            st.split_lo(dve, i * 2 + (BASE[n] + c + 1))
                            free(n, i, c)
                    if last:
                        i = pairs[n][0] - 1
                        st.split_lo(dve, i * 2 + BASE[n] + 1)
                        free(n, i, 0)


def project_out(nc, dr, name, w_v, src_x, dst_x, cols, post):
    NB = D // 256
    with Phase(nc, name) as ph:
        st = Stream(ph, ctx=False)
        y_hi, y_lo = ph.sb("y_hi", [P, KT, LAT], F32R), ph.sb("y_lo", [P, KT, LAT], F32R)
        x = ph.sb("x", [P, KT, LAT])
        res = ph.sb("res", [P, KT, LAT])
        sq = ph.sb("sq", [P, 2, LAT])
        rs, ones, gate = ph.sb("rs", [P, LAT]), ph.sb("ones", [P, P]), ph.sb("gate", [P, KT])
        pss = ph.pb("pss")
        y_loaded, x_loaded, c_loaded = [ph.sem(f"y_loaded{g}") for g in range(4)], ph.sem("x_loaded"), ph.sem("c_loaded")
        y_hi_ready, y_ready, zero_ready = ph.sem("y_hi_ready"), ph.sem("y_ready"), ph.sem("zero_ready")
        moved, squared, summed = ph.sem("moved"), ph.sem("squared"), ph.sem("summed")
        var_ready, std_ready, rs_ready, scaled = ph.sem("var_ready"), ph.sem("std_ready"), ph.sem("rs_ready"), ph.sem("scaled")
        added, stored = ph.sem("added"), ph.sem("stored")
        y_v, x_v, o_v = (a.rearrange("(k p) t -> p k t", p=P) for a in (dr.yT, src_x, dst_x))

        with nc.Block() as block:
            @block.sync
            def _(sp):
                st.load(sp, 0, [(0, w_v[:, :, 0:256])], first=True)
                sp.dma_start(ones[:], dr.consts[:, C_ONES:C_ONES + P]).then_inc(c_loaded, 16)
                for g in range(4):
                    sp.dma_start(x[:, 4 * g:4 * g + 4, :], y_v[:, 4 * g:4 * g + 4, :]).then_inc(y_loaded[g], 16)
                with sp.Fori(1, NB) as i:
                    st.load(sp, i, [(0, w_v[:, :, bass.ds(i * 256, 256)])])
                sp.wait_ge(y_ready, KT)
                sp.dma_start(x[:], x_v[:, :, 0:LAT]).then_inc(x_loaded, 16)
                for g in range(4):
                    sp.wait_ge(added, 4 * g + 4)
                    sp.dma_start(o_v[:, 4 * g:4 * g + 4, :], x[:, 4 * g:4 * g + 4, :]).then_inc(stored, 16)
                sp.wait_ge(stored, 64)

            @block.gpsimd
            def _(pool):
                if post:
                    pool.wait_ge(rs_ready, 1)
                    for k in range(KT):
                        pool.tensor_tensor(res[:, k, :], res[:, k, :], rs[:], ALU.mult).then_inc(scaled, 1)

            @block.tensor
            def _(pe):
                pe.wait_ge(y_ready, KT)
                pe.wait_ge(c_loaded, 16)
                if post:
                    pe.sem_inc(summed, 2)
                    pe.wait_ge(zero_ready, 1)
                    pe.matmul(pss[:], ones[:], rs[:], start=True, stop=False, skip_group_check=True)
                with pe.Fori(0, NB // 2) as i:
                    for c in range(2):
                        st.products(pe, i * 2 + c, c, y_hi, y_lo, ctx=False)
                    if post:
                        for n in range(4):
                            pe.wait_ge(squared, i * 4 + (n + 1))
                            pe.matmul(pss[:], ones[:], sq[:, n % 2, :], start=False, stop=False, skip_group_check=True).then_inc(summed, 1)

            @block.scalar
            def _(act):
                def epilogue(i, c):
                    act.wait_ge(st.unit_done, i * 4 + (2 * c + 2))
                    for m in range(2):
                        at = res[:, bass.ds(i * 4 + (2 * c + m), 1), :].rearrange("p a t -> p (a t)")
                        act.activation(at, st.lat[c][m][:], ACT.Copy).then_inc(moved, 1)
                    if post:
                        for m in range(2):
                            act.wait_ge(summed, i * 4 + (2 * c + m + 1))
                            act.activation(sq[:, m, :], st.lat[c][m][:], ACT.Square).then_inc(squared, 1)

                st.split_hi(act, 0, 16, first=True)
                for k in range(KT):
                    if k % 4 == 0:
                        act.wait_ge(y_loaded[k // 4], 16)
                    act.activation(y_hi[:, k, :], x[:, k, :], ACT.Copy).then_inc(y_hi_ready, 1)
                with act.Fori(0, NB // 2 - 1) as i:
                    for c in range(2):
                        st.split_hi(act, i * 2 + (c + 1), i * 32 + 16 * (c + 2))
                        epilogue(i, c)
                i = NB // 2 - 1
                st.split_hi(act, i * 2 + 1, i * 32 + 32)
                epilogue(i, 0)
                epilogue(i, 1)
                if post:
                    act.wait_ge(var_ready, 1)
                    act.activation(rs[:], rs[:], ACT.Sqrt).then_inc(std_ready, 1)

            @block.vector
            def _(dve):
                def free(i, c):
                    dve.wait_ge(squared if post else moved, i * 4 + (2 * c + 2))
                    dve.sem_inc(st.bank_free, 1)

                dve.sem_inc(st.bank_free, 2)
                if post:
                    dve.memset(rs[:], 0.0).then_inc(zero_ready, 1)
                st.split_lo(dve, 0)
                for k in range(KT):
                    dve.wait_ge(y_hi_ready, k + 1)
                    dve.tensor_tensor(y_lo[:, k, :], x[:, k, :], y_hi[:, k, :].bitcast(F32), ALU.subtract).then_inc(y_ready, 1)
                with dve.Fori(0, NB // 2 - 1) as i:
                    for c in range(2):
                        st.split_lo(dve, i * 2 + (c + 1))
                        free(i, c)
                i = NB // 2 - 1
                st.split_lo(dve, i * 2 + 1)
                free(i, 0)
                dve.wait_ge(x_loaded, 16)
                if post:
                    g0 = COL["mod"] + 2 * KT
                    dve.tensor_tensor(gate[:], cols[:, g0:g0 + KT], cols[:, COL["post_norm_w"]:COL["post_norm_w"] + KT], ALU.mult)
                    dve.wait_ge(moved, KT)
                    dve.wait_ge(summed, KT + 2)
                    dve.tensor_scalar(rs[:], pss[:], 1.0 / D, EPS, ALU.mult, ALU.add).then_inc(var_ready, 1)
                    dve.wait_ge(std_ready, 1)
                    dve.reciprocal(rs[:], rs[:]).then_inc(rs_ready, 1)
                    for k in range(KT):
                        dve.wait_ge(scaled, k + 1)
                        dve.scalar_tensor_tensor(out=x[:, k, :], in0=res[:, k, :], scalar=gate[:, k:k + 1], in1=x[:, k, :],
                                                 op0=ALU.mult, op1=ALU.add).then_inc(added, 1)
                else:
                    dve.wait_ge(moved, KT)
                    for k in range(KT):
                        dve.tensor_tensor(x[:, k, :], x[:, k, :], res[:, k, :], ALU.add).then_inc(added, 1)


def finish(nc, dr, src, ident):
    with Phase(nc, "fin") as ph:
        x, o = ph.sb("x", [P, KT, LAT]), ph.sb("o", [P, LCH, D])
        bank = [ph.pb(f"bank{i}") for i in range(4)]
        loaded, turned, taken_d, taken_a, stored = ([ph.sem(f"loaded{g}") for g in range(4)], ph.sem("turned"),
                                                    ph.sem("taken_d"), ph.sem("taken_a"), ph.sem("stored"))
        order = [(g, t) for g in range(4) for t in range(LCH)]

        with nc.Block() as block:
            @block.sync
            def _(sp):
                for g in range(4):
                    sp.dma_start(x[:, 4 * g:4 * g + 4, :], src.rearrange("(k p) t -> p k t", p=P)[:, 4 * g:4 * g + 4, :]).then_inc(loaded[g], 16)
                for g in range(4):
                    sp.wait_ge(taken_d, 2 * g + 2)
                    sp.wait_ge(taken_a, 2 * g + 2)
                    sp.dma_start(dr.out[0].rearrange("(t p) n -> p t n", p=P)[:, :, g * 512:(g + 1) * 512],
                                 o[:, :, g * 512:(g + 1) * 512]).then_inc(stored, 16)
                sp.wait_ge(stored, 64)

            @block.tensor
            def _(pe):
                for q, (g, t) in enumerate(order):
                    pe.wait_ge(loaded[g], 16)
                    if q >= 4:
                        pe.wait_ge(taken_a if q % 2 else taken_d, (q - 4) // 2 + 1)
                    for k in range(4):
                        mm = pe.transpose(bank[q % 4][:, k * P:(k + 1) * P], x[:, 4 * g + k, t * P:(t + 1) * P], ident[:])
                    mm.then_inc(turned, 1)

            @block.vector
            def _(dve):
                for q, (g, t) in enumerate(order):
                    if q % 2 == 0:
                        dve.wait_ge(turned, q + 1)
                        dve.tensor_copy(o[:, t, g * 512:(g + 1) * 512], bank[q % 4][:]).then_inc(taken_d, 1)

            @block.scalar
            def _(act):
                for q, (g, t) in enumerate(order):
                    if q % 2 == 1:
                        act.wait_ge(turned, q + 1)
                        act.activation(o[:, t, g * 512:(g + 1) * 512], bank[q % 4][:], ACT.Copy).then_inc(taken_a, 1)


def mix(nc, dr, l, cols, ident):
    lam_init = 0.8 - 0.6 * float(np.exp(-0.3 * l))
    NQK = 2 * DH
    NN = NQK + 2 * MH
    R_DQ, R_DV, R_DG = 4 * W_CONV, 4 * W_CONV + 2 * W_DIFF, 4 * W_CONV + 3 * W_DIFF
    R_MQ = 4 * W_CONV + 4 * W_DIFF
    R_MG = R_MQ + W_MEM
    CT = W_CONV // P
    MT = MEMTOK // P
    with Phase(nc, f"mix{l}") as ph:
        qk = ph.sb("qk", [P, NQK, LAT])
        mq, mk = ph.sb("mq", [P, MH, LAT]), ph.sb("mk", [P, MH, MEMTOK])
        inv = ph.sb("inv", [P, NQK + 2 * MH, LAT])
        sq = ph.sb("sq", [P, 2, LAT])
        half, ones = ph.sb("half", [P, P]), ph.sb("ones", [P, P])
        alibi = ph.sb("alibi", [P, 2, ABIAS])
        v_tok, mv_tok = ph.sb("v_tok", [P, LCH, W_DIFF]), ph.sb("mv_tok", [P, MT, W_MEM])
        sc = ph.sb("sc", [P, 8, LAT])
        mvT = ph.sb("mvT", [P, MH, MEMTOK])
        qs, ks = ph.sb("qs", [P, 2, LAT]), ph.sb("ks", [P, 2, LAT])
        PT = ph.sb("PT", [P, 2, LCH, P])
        mx, nmx = ph.sb("mx", [P, 8]), ph.sb("nmx", [P, 8])
        sums, rc = ph.sb("sums", [P, 8 * (DH + MH)]), ph.sb("rc", [P, 8])
        lamv, lamp, lam = ph.sb("lamv", [P, 4, DIFF_HALF]), ph.sb("lamp", [P, 2, DIFF_HALF]), ph.sb("lam", [P, 4])
        o, otmp = ph.sb("o", [P, DH + MH, LAT]), ph.sb("otmp", [P, LAT])
        osq, var, gain = ph.sb("osq", [P, 2, LAT]), ph.sb("var", [P, DH * LCH]), ph.sb("gain", [P, 1])
        eps = ph.sb("eps", [P, 4])
        cv = ph.sb("cv", [P, 2, 4, LAT])
        cz = ph.sb("cz", [P, 2, LAT])
        sb, tb, ob, nb = ([ph.pb(f"{n}{j}") for j in range(2)] for n in ("sb", "tb", "ob", "nb"))
        c_loaded, qk_loaded, m_loaded, v_loaded = (ph.sem(n) for n in ("c_loaded", "qk_loaded", "m_loaded", "v_loaded"))
        alibi_loaded = [ph.sem(f"alibi_loaded{j}") for j in range(2)]
        cv_loaded = [ph.sem(f"cv_loaded{j}") for j in range(2)]
        cu_ready, cm_ready, cz_ready, cy_ready = (ph.sem(n) for n in ("cu_ready", "cm_ready", "cz_ready", "cy_ready"))
        cv_stored = [ph.sem(f"cv_stored{j}") for j in range(2)]
        eps_ready, squared, summed, logged, inverted = (ph.sem(n) for n in ("eps_ready", "squared", "summed", "logged", "inverted"))
        turned, taken_d, taken_a = (ph.sem(n) for n in ("turned", "taken_d", "taken_a"))
        lam_sum, lam_exp, passed = ph.sem("lam_sum"), ph.sem("lam_exp"), ph.sem("passed")
        qk_ready, score_done, read_done, max_ready, exp_done = (ph.sem(n) for n in ("qk_ready", "score_done", "read_done", "max_ready", "exp_done"))
        tr_done, pt_ready, pv_done, comb_done = ph.sem("tr_done"), [ph.sem(f"pt_ready{j}") for j in range(2)], ph.sem("pv_done"), ph.sem("comb_done")
        ms_done, mmax, mexp, mtr, mpt, mpv, mcomb = (ph.sem(n) for n in ("ms_done", "mmax", "mexp", "mtr", "mpt", "mpv", "mcomb"))
        osq_ready, osq_summed, var_ready, std_ready, inv_ready, o_ready = (
            ph.sem(n) for n in ("osq_ready", "osq_summed", "var_ready", "std_ready", "inv_ready", "o_ready"))
        gate_loaded, o_turned, out_ready, stored = (ph.sem(n) for n in ("gate_loaded", "o_turned", "out_ready", "stored"))

        def norm_tile(n):
            if n < NQK:
                return qk[:, n, :], LAT, half, (1.0, 0) if n < DH else (1.0 / DIFF_HALF, 1)
            if n < NQK + MH:
                return mq[:, n - NQK, :], LAT, ones, (1.0, 2)
            return mk[:, n - NQK - MH, :], MEMTOK, ones, (1.0 / P, 1)

        groups = [(0, t) for t in range(LCH)] + [(1, t) for t in range(LCH)] + [(2, t) for t in range(MT)]
        NG = len(groups)
        banks4 = [sb[0], sb[1], tb[0], tb[1]]

        def group_dst(q):
            kind, t = groups[q]
            return v_tok[:, t, 0:512] if kind == 0 else v_tok[:, t, 512:768] if kind == 1 else mv_tok[:, t, :]

        def group_width(q):
            return 256 if groups[q][0] == 1 else 512

        def rows(first, n):
            return dr.pT[first:first + n * P, :].rearrange("(k p) t -> p k t", p=P)

        kv_v = dr.mkvT[l].rearrange("(k p) t -> p k t", p=P)

        with nc.Block() as block:
            @block.sync
            def _(sp):
                for t, at in ((half, C_HALF), (ones, C_ONES)):
                    sp.dma_start(t[:], dr.consts[:, at:at + P]).then_inc(c_loaded, 16)
                sp.dma_start(qk[:], rows(R_DQ, NQK)).then_inc(qk_loaded, 16)
                sp.dma_start(mq[:], rows(R_MQ, MH)).then_inc(m_loaded, 16)
                sp.dma_start(mk[:], kv_v[:, 0:MH, :]).then_inc(m_loaded, 16)
                sp.dma_start(sc[:, 0:DH, :], rows(R_DV, DH)).then_inc(v_loaded, 16)
                sp.dma_start(mvT[:], kv_v[:, MH:2 * MH, :]).then_inc(v_loaded, 16)
                for j in range(2):
                    sp.dma_start(alibi[:, j, :], dr.alibi[:, j * ABIAS:(j + 1) * ABIAS]).then_inc(alibi_loaded[j], 16)
                for n, v in enumerate((dr.lambda_q1_2, dr.lambda_k1_2, dr.lambda_q2_2, dr.lambda_k2_2)):
                    sp.dma_start(lamv[:, n, :], v[l].partition_broadcast(P)).then_inc(c_loaded, 16)
                conv_rows = dr.pT[0:4 * W_CONV, :].rearrange("(v k p) t -> p k v t", p=P, v=4)
                for k in range(CT):
                    if k >= 2:
                        sp.wait_ge(cv_stored[k % 2], 16 * (k // 2))
                    sp.dma_start(cv[:, k % 2, :, :], conv_rows[:, k, :, :]).then_inc(cv_loaded[k % 2], 16)
                with sp.Fori(1, DH // 2) as i:
                    for j in range(2):
                        sp.wait_ge(qk_ready, i * 2 + j)
                        sp.dma_start(alibi[:, j, :], dr.alibi[:, bass.ds(i * (2 * ABIAS) + j * ABIAS, ABIAS)]).then_inc(alibi_loaded[j], 16)
                sp.wait_ge(comb_done, DH + 1)
                sp.wait_ge(mcomb, MH + 1)
                sp.dma_start(inv[:, 0:DH, :], rows(R_DG, DH)).then_inc(gate_loaded, 16)
                sp.dma_start(inv[:, DH:DH + MH, :], rows(R_MG, MH)).then_inc(gate_loaded, 16)
                for n in range(DH + MH):
                    sp.wait_ge(out_ready, n + 1)
                    sp.dma_start(dr.yT[W_CONV + n * P:W_CONV + (n + 1) * P, :], inv[:, n, :]).then_inc(stored, 16)
                sp.wait_ge(stored, 16 * (DH + MH))

            @block.gpsimd
            def _(pool):
                def conv_out(k):
                    j = k % 2
                    pool.wait_ge(cz_ready, k + 1)
                    pool.tensor_tensor(cv[:, j, 1, :], cv[:, j, 1, :], cv[:, j, 3, :], ALU.mult)
                    pool.drain()
                    pool.tensor_tensor(cz[:, j, :], cz[:, j, :], cv[:, j, 1, :], ALU.mult).then_inc(cy_ready, 1)
                    pool.wait_ge(cy_ready, k + 1)
                    pool.dma_start(dr.yT[k * P:(k + 1) * P, :], cz[:, j, :]).then_inc(cv_stored[j], 16)

                for k in range(CT):
                    j = k % 2
                    pool.wait_ge(cv_loaded[j], 16 * (k // 2 + 1))
                    pool.tensor_tensor(cv[:, j, 0, :], cv[:, j, 0, :], cv[:, j, 2, :], ALU.mult).then_inc(cu_ready, 1)
                    if k:
                        conv_out(k - 1)
                conv_out(CT - 1)
                for j in range(2):
                    pool.wait_ge(cv_stored[j], 16 * CT // 2)
                for n in range(DH):
                    pool.wait_ge(comb_done, n + 2)
                    if n >= 2:
                        pool.wait_ge(osq_summed, n - 1)
                    pool.tensor_tensor(osq[:, n % 2, :], o[:, n, :], o[:, n, :], ALU.mult).then_inc(osq_ready, 1)
                pool.wait_ge(inv_ready, 1)
                for n in range(DH):
                    pool.tensor_tensor(o[:, n, :].rearrange("p (b e) -> p b e", b=LCH), o[:, n, :].rearrange("p (b e) -> p b e", b=LCH),
                                       bc(var[:, n * LCH:(n + 1) * LCH], P, 2), ALU.mult).then_inc(o_ready, 1)

            @block.tensor
            def _(pe):
                pe.sem_inc(pv_done, 2)
                pe.wait_ge(c_loaded, 16 * 6)
                for n in range(NN):
                    _, wd, mat, _ = norm_tile(n)
                    pe.wait_ge(squared, n + 1)
                    if n >= 2:
                        pe.wait_ge(logged, n - 1)
                    pe.matmul(nb[n % 2][:, 0:wd], mat[:], sq[:, n % 2, 0:wd], start=True, stop=True).then_inc(summed, 1)
                pe.wait_ge(v_loaded, 32)
                for q, (kind, t) in enumerate(groups):
                    if q >= 4:
                        pe.wait_ge(taken_a if q % 2 else taken_d, (q - 4) // 2 + 1)
                    tiles = range(4) if kind != 1 else range(4, 6)
                    for m, k in enumerate(tiles):
                        src = mvT[:, k, t * P:(t + 1) * P] if kind == 2 else sc[:, k, t * P:(t + 1) * P]
                        mm = pe.transpose(banks4[q % 4][:, m * P:(m + 1) * P], src, ident[:])
                    mm.then_inc(turned, 1)
                pe.wait_ge(taken_a, NG // 2)
                pe.wait_ge(taken_d, NG // 2)

                def scores(i, s):
                    j, c = s // 2, s % 2
                    r = slice(64 * c, 64 * c + 64)
                    pe.wait_ge(qk_ready, i * 2 + (j + 1))
                    for b in range(LCH):
                        pe.wait_ge(read_done, i * 16 + (4 * s + b))
                        pe.matmul(sb[b % 2][:], qs[r, j, b * P:(b + 1) * P], ks[r, j, :], start=True, stop=True).then_inc(score_done, 1)

                def weigh(i, s):
                    j, c = s // 2, s % 2
                    pe.wait_ge(comb_done, i * 2 + (j + 1))

                    def turn(b):
                        u = 4 * s + b
                        pe.wait_ge(exp_done, i * 16 + (u + 1))
                        pe.wait_ge(pt_ready[b % 2], i * 8 + (u // 2 + 1))
                        for k in range(LCH):
                            mm = pe.transpose(tb[b % 2][:, k * P:(k + 1) * P], sc[:, 4 * c + b, k * P:(k + 1) * P], ident[:])
                        mm.then_inc(tr_done, 1)

                    def times_v(b):
                        u = 4 * s + b
                        pe.wait_ge(pt_ready[b % 2], i * 8 + (u // 2 + 2))
                        for k in range(LCH):
                            mm = pe.matmul(ob[c][:, b * P:(b + 1) * P], PT[:, b % 2, k, :],
                                           v_tok[:, k, bass.ds(i * 2 * P + j * P, P)], start=(k == 0), stop=(k == LCH - 1))
                        mm.then_inc(pv_done, 1)

                    turn(0)
                    for b in range(1, LCH):
                        turn(b)
                        times_v(b - 1)
                    times_v(LCH - 1)

                scores(0, 0)
                with pe.Fori(0, DH // 2 - 1) as i:
                    for s in range(4):
                        if s < 3:
                            scores(i, s + 1)
                        else:
                            scores(i + 1, 0)
                        weigh(i, s)
                i = DH // 2 - 1
                for s in range(4):
                    if s < 3:
                        scores(i, s + 1)
                    weigh(i, s)

                pe.wait_ge(comb_done, DH + 1)
                with pe.Fori(0, MH // 2) as i:
                    for j in range(2):
                        pe.wait_ge(qk_ready, i * 2 + (DH + j + 1))
                        for g in range(2):
                            pe.wait_ge(mexp, i * 4 + (2 * j + g + 1))
                            for b in range(2):
                                at = (2 * g + b) * P
                                mm = pe.matmul(sb[g][:, b * MEMTOK:(b + 1) * MEMTOK], qs[:, j, at:at + P], ks[:, j, 0:MEMTOK],
                                               start=True, stop=True)
                            mm.then_inc(ms_done, 1)
                        pe.wait_ge(mcomb, i * 2 + (j + 1))
                        for g in range(2):
                            pe.wait_ge(mexp, i * 4 + (2 * j + g + 3))
                            for b in range(2):
                                for k in range(MT):
                                    mm = pe.transpose(tb[g][:, (b * MT + k) * P:(b * MT + k + 1) * P],
                                                      sc[:, 2 * g + b, k * P:(k + 1) * P], ident[:])
                            mm.then_inc(mtr, 1)
                        for g in range(2):
                            pe.wait_ge(mpt, i * 4 + (2 * j + g + 1))
                            for b in range(2):
                                for k in range(MT):
                                    mm = pe.matmul(ob[0][:, (2 * g + b) * P:(2 * g + b + 1) * P], PT[:, g, b * MT + k, :],
                                                   mv_tok[:, k, bass.ds(i * 2 * P + j * P, P)], start=(k == 0), stop=(k == MT - 1))
                            mm.then_inc(mpv, 1)
                pe.wait_ge(mcomb, MH + 1)
                for n in range(DH + MH):
                    if n < DH:
                        pe.wait_ge(o_ready, n + 1)
                    if n >= 2:
                        pe.wait_ge(out_ready, n - 1)
                    for b in range(LCH):
                        mm = pe.transpose(nb[n % 2][:, b * P:(b + 1) * P], o[:, n, b * P:(b + 1) * P], ident[:])
                    mm.then_inc(o_turned, 1)

            @block.scalar
            def _(act):
                act.wait_ge(eps_ready, 1)
                act.wait_ge(qk_loaded, 16)

                def log_of(n):
                    _, wd, _, (scale, e) = norm_tile(n)
                    act.wait_ge(summed, n + 1)
                    act.activation(inv[:, n, 0:wd], nb[n % 2][:, 0:wd], ACT.Ln, bias=eps[:, e:e + 1], scale=scale).then_inc(logged, 1)

                for n in range(NN):
                    if n == NQK:
                        act.wait_ge(m_loaded, 32)
                    x, wd, _, _ = norm_tile(n)
                    if n >= 2:
                        act.wait_ge(summed, n - 1)
                    act.activation(sq[:, n % 2, 0:wd], x, ACT.Square).then_inc(squared, 1)
                    if n:
                        log_of(n - 1)
                log_of(NN - 1)
                act.drain()
                for n in range(NN):
                    wd = norm_tile(n)[1]
                    op = act.activation(inv[:, n, 0:wd], inv[:, n, 0:wd], ACT.Exp, scale=-0.5)
                op.then_inc(inverted, 1)
                act.wait_ge(lam_sum, 1)
                act.activation(lam[:, 0:2], lam[:, 0:2], ACT.Exp).then_inc(lam_exp, 1)
                for q in range(1, NG, 2):
                    act.wait_ge(turned, q + 1)
                    act.activation(group_dst(q), banks4[q % 4][:, 0:group_width(q)], ACT.Copy).then_inc(taken_a, 1)
                for k in range(CT):
                    act.wait_ge(cu_ready, k + 1)
                    if k >= 2:
                        act.wait_ge(cv_stored[k % 2], 16 * (k // 2))
                    w1 = COL["conv_w_2"] + (3 * l + 1) * CT + k
                    b0 = COL["conv_b_2"] + l * CT + k
                    act.activation(cz[:, k % 2, :], cv[:, k % 2, 0, :], ACT.Identity, bias=cols[:, b0:b0 + 1],
                                   scale=cols[:, w1:w1 + 1]).then_inc(cm_ready, 1)

                def exps(i, s):
                    c = s % 2
                    act.wait_ge(max_ready, i * 4 + (s + 1))
                    for b in range(LCH):
                        act.activation(sc[:, 4 * c + b, :], sc[:, 4 * c + b, :], ACT.Exp, bias=nmx[:, 4 * c + b:4 * c + b + 1],
                                       accum_out=sums[:, bass.ds(i * 16 + (4 * s + b), 1)]).then_inc(exp_done, 1)

                def copies(i, s):
                    for b in (1, 3):
                        u = 4 * s + b
                        act.wait_ge(tr_done, i * 16 + (u + 1))
                        act.wait_ge(pv_done, i * 16 + (u + 1))
                        act.activation(PT[:, 1].rearrange("p k q -> p (k q)"), tb[1][:], ACT.Copy).then_inc(pt_ready[1], 1)

                act.sem_inc(pt_ready[1], 1)
                exps(0, 0)
                with act.Fori(0, DH // 2 - 1) as i:
                    for s in range(4):
                        if s < 3:
                            exps(i, s + 1)
                        else:
                            exps(i + 1, 0)
                        copies(i, s)
                i = DH // 2 - 1
                for s in range(4):
                    if s < 3:
                        exps(i, s + 1)
                    copies(i, s)

                act.sem_inc(mexp, 2)
                with act.Fori(0, MH // 2) as i:
                    for j in range(2):
                        for g in range(2):
                            act.wait_ge(mmax, i * 4 + (2 * j + g + 1))
                            for b in range(2):
                                op = act.activation(sc[:, 2 * g + b, 0:MEMTOK], sb[g][:, b * MEMTOK:(b + 1) * MEMTOK], ACT.Exp,
                                                    bias=nmx[:, 2 * g + b:2 * g + b + 1],
                                                    accum_out=sums[:, bass.ds(i * 8 + (8 * DH + 4 * j + 2 * g + b), 1)])
                            op.then_inc(mexp, 1)
                act.wait_ge(var_ready, 1)
                act.activation(var[:], var[:], ACT.Sqrt).then_inc(std_ready, 1)

            @block.vector
            def _(dve):
                for e, v in enumerate((DIFF_HALF * EPS, EPS, P * EPS)):
                    dve.memset(eps[:, e:e + 1], v)
                dve.drain().then_inc(eps_ready, 1)
                dve.wait_ge(c_loaded, 16 * 6)
                for n in range(2):
                    dve.tensor_tensor(lamp[:, n, :], lamv[:, 2 * n, :], lamv[:, 2 * n + 1, :], ALU.mult)
                dve.drain()
                dve.tensor_reduce(lam[:, 0:2], lamp[:], AX.X, ALU.add).then_inc(lam_sum, 1)
                h0 = COL["diff_head_norm_g_2"] + l
                dve.tensor_scalar(gain[:], cols[:, h0:h0 + 1], 1.0 - lam_init, None, ALU.mult)
                for q in range(0, NG, 2):
                    dve.wait_ge(turned, q + 1)
                    dve.tensor_copy(group_dst(q), banks4[q % 4][:, 0:group_width(q)]).then_inc(taken_d, 1)
                dve.wait_ge(turned, NG)
                dve.wait_ge(lam_exp, 1)
                dve.tensor_tensor(lam[:, 2:3], lam[:, 1:2], lam[:, 0:1], ALU.subtract)
                dve.drain()
                dve.tensor_scalar(lam[:, 2:3], lam[:, 2:3], -lam_init, None, ALU.add)
                for k in range(CT):
                    dve.wait_ge(cm_ready, k + 1)
                    for tap, (a, z, off) in ((0, (1, LAT, -1)), (2, (0, LAT - 1, 1))):
                        wc = COL["conv_w_2"] + (3 * l + tap) * CT + k
                        if tap:
                            dve.drain()
                        op = dve.scalar_tensor_tensor(out=cz[:, k % 2, a:z], in0=cv[:, k % 2, 0, a + off:z + off], scalar=cols[:, wc:wc + 1],
                                                      in1=cz[:, k % 2, a:z], op0=ALU.mult, op1=ALU.add)
                    op.then_inc(cz_ready, 1)
                dve.wait_ge(inverted, 1)

                def unit(x, out, gcol, iv, wd=LAT):
                    return dve.scalar_tensor_tensor(out=out[:, 0:wd], in0=x, scalar=cols[:, gcol:gcol + 1], in1=iv,
                                                    op0=ALU.mult, op1=ALU.mult)

                def dyn(t, first, n=LAT):
                    return t[:, first, 0:n].rearrange("p a t -> p (a t)")

                def head(i, j):
                    unit(dyn(qk, bass.ds(i * 2 + j, 1)), qs[:, j, :], COL["diff_q_norm_g_2"] + l, dyn(inv, bass.ds(i * 2 + j, 1)))
                    unit(dyn(qk, bass.ds(i * 2 + (DH + j), 1)), ks[:, j, :], COL["diff_k_norm_g_2"] + l,
                         dyn(inv, bass.ds(i * 2 + (DH + j), 1)))

                def maxima(i, s, first=False):
                    j, c = s // 2, s % 2
                    if c == 0:
                        head(i, j)
                        dve.drain().then_inc(qk_ready, 1)
                    if not first and s != 1:
                        dve.wait_ge(tr_done, i * 16 + 4 * (s - 1))
                    if c == 0:
                        dve.wait_ge(alibi_loaded[j], i * 16 + 16)
                    for b in range(LCH):
                        dve.wait_ge(score_done, i * 16 + (4 * s + b + 1))
                        dve.sem_inc(passed, 1)
                        dve.tensor_tensor_reduce(out=sc[:, 4 * c + b, :], in0=sb[b % 2][:],
                                                 in1=alibi[:, j, (LCH - 1 - b) * P:(LCH - 1 - b) * P + LAT],
                                                 scale=1.0, scalar=-3.0e38, op0=ALU.add, op1=ALU.max,
                                                 accum_out=mx[:, 4 * c + b:4 * c + b + 1]).then_inc(read_done, 1)
                    dve.drain()
                    dve.tensor_scalar(nmx[:, 4 * c:4 * c + 4], mx[:, 4 * c:4 * c + 4], -1.0, None, ALU.mult).then_inc(max_ready, 1)

                def copies(i, s):
                    for b in (0, 2):
                        u = 4 * s + b
                        dve.wait_ge(tr_done, i * 16 + (u + 1))
                        dve.wait_ge(pv_done, i * 16 + (u + 1))
                        dve.tensor_copy(PT[:, 0].rearrange("p k q -> p (k q)"), tb[0][:]).then_inc(pt_ready[0], 1)

                def blocks(ap):
                    return ap.rearrange("p (b e) -> p b e", b=LCH)

                def combine(i, j):
                    dve.wait_ge(exp_done, i * 16 + (8 * j + 8))
                    dve.reciprocal(rc[:], sums[:, bass.ds(i * 16 + 8 * j, 8)])
                    dve.drain()
                    dve.tensor_scalar(rc[:, 4:8], rc[:, 4:8], lam[:, 2:3], None, ALU.mult)
                    dve.drain()
                    dve.wait_ge(pv_done, i * 16 + (8 * j + 10))
                    at = dyn(o, bass.ds(i * 2 + j, 1))
                    dve.tensor_tensor(blocks(at), blocks(ob[0][:]), bc(rc[:, 0:4], P, 2), ALU.mult)
                    dve.tensor_tensor(blocks(otmp[:]), blocks(ob[1][:]), bc(rc[:, 4:8], P, 2), ALU.mult)
                    dve.drain()
                    dve.tensor_tensor(at, at, otmp[:], ALU.add).then_inc(comb_done, 1)

                for sem in (read_done, pt_ready[0], comb_done, mcomb):
                    dve.sem_inc(sem, 1)
                maxima(0, 0, first=True)
                with dve.Fori(0, DH // 2 - 1) as i:
                    for s in range(4):
                        if s < 3:
                            maxima(i, s + 1)
                        else:
                            maxima(i + 1, 0)
                        copies(i, s)
                        if s % 2:
                            combine(i, s // 2)
                i = DH // 2 - 1
                for s in range(4):
                    if s < 3:
                        maxima(i, s + 1)
                    copies(i, s)
                    if s % 2:
                        combine(i, s // 2)

                with dve.Fori(0, MH // 2) as i:
                    for j in range(2):
                        unit(dyn(mq, bass.ds(i * 2 + j, 1)), qs[:, j, :], COL["mem_q_norm_g_2"] + l, dyn(inv, bass.ds(i * 2 + (NQK + j), 1)))
                        unit(dyn(mk, bass.ds(i * 2 + j, 1), MEMTOK), ks[:, j, :], COL["mem_k_norm_g_2"] + l,
                             dyn(inv, bass.ds(i * 2 + (NQK + MH + j), 1), MEMTOK), MEMTOK)
                        dve.drain().then_inc(qk_ready, 1)
                        for g in range(2):
                            dve.wait_ge(ms_done, i * 4 + (2 * j + g + 1))
                            dve.tensor_reduce(mx[:, 2 * g:2 * g + 2], sb[g][:].rearrange("p (b m) -> p b m", b=2), AX.X, ALU.max)
                            dve.drain()
                            dve.tensor_scalar(nmx[:, 2 * g:2 * g + 2], mx[:, 2 * g:2 * g + 2], -1.0, None, ALU.mult).then_inc(mmax, 1)
                        for g in range(2):
                            dve.wait_ge(mtr, i * 4 + (2 * j + g + 1))
                            dve.tensor_copy(PT[:, g].rearrange("p k q -> p (k q)"), tb[g][:]).then_inc(mpt, 1)
                        dve.reciprocal(rc[:, 0:4], sums[:, bass.ds(i * 8 + (8 * DH + 4 * j), 4)])
                        dve.drain()
                        dve.wait_ge(mpv, i * 4 + (2 * j + 2))
                        at = dyn(o, bass.ds(i * 2 + (DH + j), 1))
                        dve.tensor_tensor(blocks(at), blocks(ob[0][:]), bc(rc[:, 0:4], P, 2), ALU.mult).then_inc(mcomb, 1)
                for n in range(DH):
                    dve.wait_ge(osq_ready, n + 1)
                    dve.tensor_reduce(var[:, n * LCH:(n + 1) * LCH], blocks(osq[:, n % 2, :]), AX.X, ALU.add).then_inc(osq_summed, 1)
                dve.drain()
                dve.tensor_scalar(var[:], var[:], 1.0 / P, EPS, ALU.mult, ALU.add).then_inc(var_ready, 1)
                dve.wait_ge(std_ready, 1)
                dve.reciprocal(var[:], var[:]).then_inc(inv_ready, 1)
                dve.wait_ge(gate_loaded, 32)
                for n in range(DH + MH):
                    dve.wait_ge(o_turned, n + 1)
                    if n < DH:
                        op = dve.scalar_tensor_tensor(out=inv[:, n, :], in0=nb[n % 2][:], scalar=gain[:], in1=inv[:, n, :],
                                                      op0=ALU.mult, op1=ALU.mult)
                    else:
                        op = dve.tensor_tensor(inv[:, n, :], nb[n % 2][:], inv[:, n, :], ALU.mult)
                    op.then_inc(out_ready, 1)


INPUTS = ["x", "c", "ctx", "c_ctx", "w_ada", "b_ada", "pre_norm_w", "post_norm_w", "w_in", "conv_ssd_w", "conv_ssd_b",
          "conv_gdn_w", "ssd_a_log", "ssd_dt_bias", "ssd_d", "ssd_norm_w", "gdn_a_log", "gdn_dt_bias", "gdn_norm_w",
          "w_out", "mem_2", "norm_g_2", "w_in_2", "conv_w_2", "conv_b_2", "diff_q_norm_g_2", "diff_k_norm_g_2",
          "lambda_q1_2", "lambda_k1_2", "lambda_q2_2", "lambda_k2_2", "diff_head_norm_g_2", "mem_norm_g_2",
          "w_mem_kv_2", "mem_q_norm_g_2", "mem_k_norm_g_2", "w_out_2"]
SCRATCH = {"mod": (2, 3 * D), "xT": (D, TOK), "memT": (D, MEMTOK), "zT": (D, LAT), "xbcT": (XBC, TOK),
           "qT": (GDN_W, LAT), "kvT": (2 * GDN_W, TOK), "smallT": (NSMALL, TOK), "arow": (NSMALL, TOK), "yT": (D, LAT), "x1T": (D, LAT), "x2T": (D, LAT), "x3T": (D, LAT), "pT": (IN2, LAT),
           "mkvT": (LAYERS, 2 * W_MEM, MEMTOK)}


def program(nc, dr):
    mod = COL["mod"]
    with Phase(nc, "all") as whole:
        cols = whole.sb("cols", [P, NCOL])
        ident = whole.sb("ident", [P, P])
        modulate(nc, dr)
        columns(nc, dr, cols, ident)
        with Phase(nc, "b1") as first:
            u_hi = first.sb("u_hi", [P, KT, TOK], F32R)
            u_lo = first.sb("u_lo", [P, KT, TOK], F32R)
            norm_split(nc, dr, "nrm", dr.xT, TOK, u_hi, u_lo, cols,
                       [(0, LAT, cols[:, mod + KT:mod + 2 * KT], cols[:, mod:mod + KT]),
                        (LAT, CTX, cols[:, mod + 4 * KT:mod + 5 * KT], cols[:, mod + 3 * KT:mod + 4 * KT])],
                       modulated=True)
            project(nc, dr, cols, u_hi, u_lo)
        with Phase(nc, "mixers") as ph:
            tq = ph.sb("tq", [P, NQ, NCH, NSMALL])
            decays(nc, dr, tq, ident)
            ssd(nc, dr, cols, tq, ident)
            gdn(nc, dr, cols, tq, ident)
        project_out(nc, dr, "out0", dr.w_out.rearrange("a (k p) n -> p (a k) n", p=P), dr.xT, dr.x1T, cols, True)
        xs = [dr.x1T, dr.x2T, dr.x3T]
        for l in range(LAYERS):
            with Phase(nc, f"mem{l}") as ph:
                u_hi, u_lo = ph.sb("u_hi", [P, KT, MEMTOK], F32R), ph.sb("u_lo", [P, KT, MEMTOK], F32R)
                g0 = COL["mem_norm_g_2"] + l * KT
                norm_split(nc, dr, f"nm{l}", dr.memT, MEMTOK, u_hi, u_lo, cols, [(0, MEMTOK, cols[:, g0:g0 + KT], None)])
                project_plain(nc, dr, f"kv{l}", dr.w_mem_kv_2[l].rearrange("(k p) n -> p k n", p=P), MEMTOK, u_hi, u_lo,
                              [(2, 0, W_MEM, ACT.Copy, ACT.Copy)], dr.mkvT[l])
            with Phase(nc, f"lay{l}") as ph:
                u_hi, u_lo = ph.sb("u_hi", [P, KT, LAT], F32R), ph.sb("u_lo", [P, KT, LAT], F32R)
                g0 = COL["norm_g_2"] + l * KT
                norm_split(nc, dr, f"nl{l}", xs[l], LAT, u_hi, u_lo, cols, [(0, LAT, cols[:, g0:g0 + KT], None)])
                C = W_CONV
                project_plain(nc, dr, f"pl{l}", dr.w_in_2[l].rearrange("(k p) n -> p k n", p=P), LAT, u_hi, u_lo,
                              [(C // 256, 0, C, ACT.Copy, ACT.Copy), (C // 256, 2 * C, 4 * C, ACT.Copy, ACT.Copy),
                               (C // 256, 5 * C, 6 * C, ACT.Copy, ACT.Copy), (C // 256, 3 * C, 7 * C, ACT.Silu, ACT.Silu),
                               (W_MEM // 256, 8 * C, 8 * C + W_MEM, ACT.Copy, ACT.Silu)], dr.pT)
            mix(nc, dr, l, cols, ident)
            project_out(nc, dr, f"outl{l}", dr.w_out_2[l].rearrange("(k p) n -> p k n", p=P), xs[l], xs[l + 1], cols, False)
        finish(nc, dr, xs[LAYERS], ident)


def kernel(**inputs):
    import types as _types
    import concourse.bacc as _bacc
    from concourse.bass_utils import run_bass_kernel_spmd as _run

    nc = _bacc.Bacc("TRN2", target_bir_lowering=False, num_devices=1)
    arrays, dr = {}, {}
    for name in INPUTS:
        a = np.ascontiguousarray(inputs[name])
        arrays[f"in_{name}_dram"] = a
        dr[name] = nc.dram_tensor(f"in_{name}_dram", a.shape, mybir.dt.from_np(a.dtype), kind="ExternalInput").ap()
    dr["mem"] = dr["mem_2"]
    for name, a in zip(("consts", "alibi"), constants()):
        arrays[f"{name}_dram"] = a
        dr[name] = nc.dram_tensor(f"{name}_dram", a.shape, F32, kind="ExternalInput").ap()
    for name, shape in SCRATCH.items():
        dr[name] = nc.dram_tensor(f"scr_{name}", shape, F32, kind="Internal").ap()
    dr["out"] = nc.dram_tensor("out_0_dram", (1, LAT, D), F32, kind="ExternalOutput").ap()
    program(nc, _types.SimpleNamespace(**dr))
    return _run(nc, [arrays], core_ids=[0]).results[0]["out_0_dram"]
```

```python
import numpy as np
import concourse.bass as bass
from concourse import mybir
from contextlib import ExitStack

F32 = mybir.dt.float32
F32R = mybir.dt.float32r
BF16 = mybir.dt.bfloat16
ACT = mybir.ActivationFunctionType
ALU = mybir.AluOpType
AX = mybir.AxisListType

P = 128
D = 2048
KT = D // P
LAT, CTX = 512, 256
TOK = LAT + CTX
EPS = 1e-6
GRID = 64
TAPS = 5
SSD_W, SSD_H, SSD_P, SSD_N, SSD_G = 1024, 16, 64, 128, 2
GDN_W, GDN_H = 1024, 8
XBC = SSD_W + 2 * SSD_G * SSD_N
OFF_XBC = D
OFF_DT = OFF_XBC + XBC
OFF_QKV = OFF_DT + 2 * SSD_H
OFF_BETA = OFF_QKV + 3 * GDN_W
NSMALL = 2 * SSD_H + 4 * GDN_H
LCH, CCH = LAT // P, CTX // P
NCH = LCH + CCH
SCAN = ([LCH + c for c in range(CCH)] + list(range(LCH)),
        [LCH + c for c in range(CCH)][::-1] + list(range(LCH))[::-1])
BETA0, ALPHA0 = 2 * SSD_H, 2 * SSD_H + 2 * GDN_H

LAYERS = 2
W_CONV, W_DIFF, W_MEM = 768, 768, 512
IN2 = 4 * W_CONV + 4 * W_DIFF + 2 * W_MEM
MEMTOK = 256
DH, MH = W_DIFF // P, W_MEM // P
DIFF_HALF = 64
ABIAS = LAT + LAT - P
NEG = -1e30

C_ID, C_ONES, C_HALF, C_CUM, C_NEG, C_STRICT, C_LEVEL = 0, 128, 256, 384, 640, 896, 1152
NLEVEL = 7
C_END = C_LEVEL + 2 * NLEVEL * P


def constants():
    i = np.arange(P)[:, None]
    j = np.arange(P)[None, :]
    c = np.zeros((P, C_END), np.float32)
    c[:, C_ID:C_ID + P] = i == j
    c[:, C_ONES:C_ONES + P] = 1.0
    c[:, C_HALF:C_HALF + P] = (i // 64) == (j // 64)
    c[:, C_CUM:C_CUM + P] = i <= j
    c[:, C_CUM + P:C_CUM + 2 * P] = i >= j
    c[:, C_NEG:C_NEG + P] = np.where(i <= j, 0.0, NEG)
    c[:, C_NEG + P:C_NEG + 2 * P] = np.where(i >= j, 0.0, NEG)
    c[:, C_STRICT:C_STRICT + P] = i < j
    c[:, C_STRICT + P:C_STRICT + 2 * P] = i > j
    for d in range(2):
        for v in range(NLEVEL):
            s = 1 << v
            a, b = (i, j) if d == 0 else (j, i)
            pair = (a // (2 * s) == b // (2 * s)) & ((a // s) % 2 == 1) & ((b // s) % 2 == 0)
            at = C_LEVEL + (d * NLEVEL + v) * P
            c[:, at:at + P] = pair | (i == j)
    m = np.arange(ABIAS)[None, :] - (LAT - P)
    dist = np.abs(m - i).astype(np.float32)
    slopes = np.array([2.0 ** (-8.0 * (h + 1) / DH) for h in range(DH)], np.float32)
    bias = (-slopes[None, :, None] * dist[:, None, :]).astype(np.float32)
    return c, np.ascontiguousarray(bias.reshape(P, DH * ABIAS))


ROWS = [
    [("b_ada", 48), ("pre_norm_w", 16), ("post_norm_w", 16)],
    [("norm_g_2", 32), ("mem_norm_g_2", 32), ("conv_ssd_w", 60), ("gdn_norm_w", 1), ("diff_head_norm_g_2", 2)],
    [("conv_gdn_w", 120), ("ssd_norm_w", 8)],
    [("conv_ssd_b", 12), ("conv_w_2", 36), ("conv_b_2", 12), ("diff_q_norm_g_2", 2),
     ("diff_k_norm_g_2", 2), ("mem_q_norm_g_2", 2), ("mem_k_norm_g_2", 2)],
]
COL = {}
for _t, _rows in enumerate(ROWS):
    _at = 0
    for _name, _n in _rows:
        COL[_name] = _t * P + _at
        _at += _n
NMOD = 3 * KT
COL["mod"] = len(ROWS) * P
NCOL = COL["mod"] + 2 * NMOD


class Phase:

    def __init__(self, nc, name):
        self.nc, self.name, self.ctx, self.sems = nc, name, ExitStack(), []

    def __enter__(self):
        self.ctx.__enter__()
        return self

    def __exit__(self, *a):
        if self.sems:
            self.nc.clear_and_free_semaphores(self.sems)
            self.nc.all_engine_barrier()
        return self.ctx.__exit__(*a)

    def sb(self, name, shape, dt=F32):
        return self.ctx.enter_context(self.nc.sbuf_tensor(f"{self.name}_{name}", shape, dt))

    def pb(self, name, n=512):
        return self.ctx.enter_context(self.nc.psum_tensor(f"{self.name}_{name}", [P, n], F32))

    def sem(self, name):
        self.sems.append(self.nc.alloc_semaphore(f"{self.name}_{name}"))
        return self.sems[-1]


def bc(ap, n, at):
    v = ap.unsqueeze(at)
    shape = list(v.shape)
    shape[at] = n
    return v.to_broadcast(shape)


def modulate(nc, dr, cols, ident, x_sb, rs):
    BT = 3
    NB = 3 * D // 256
    tiles = [(dr.mem, t) for t in range(MEMTOK // P)] + [(dr.x, t) for t in range(LCH)] + [(dr.ctx, t) for t in range(CCH)]
    assert BT * len(tiles) == NB
    MTL = MEMTOK // P
    with Phase(nc, "ada") as ph:
        st = Stream(ph, banks=False, uk=KT // 4, deep=4, slots=4)
        crow = ph.sb("crow", [2 * KT, P])
        cact = ph.sb("cact", [2 * KT, P])
        c_hi, c_lo, zero = ph.sb("c_hi", [P, KT, P], F32R), ph.sb("c_lo", [P, KT, P], F32R), ph.sb("zero", [P, P])
        rows = ph.sb("rows", [2, 2, 256])
        rowt = ph.sb("rowt", [P, len(ROWS), P])
        xin = ph.sb("xin", [P, 2, D])
        mem = ph.sb("mem", [P, KT, MEMTOK])
        acc, pst, turned = [ph.pb(f"acc{j}") for j in range(2)], [ph.pb(f"pst{g}") for g in range(4)], [ph.pb(f"turned{j}") for j in range(2)]
        modc = ph.sb("modc", [P, 2 * NMOD])
        NTL = len(tiles)
        square, root = ph.sb("square", [P, D]), ph.sb("root", [P, NTL])
        diag, ones = ph.sb("diag", [P, NTL, P]), ph.sb("ones", [P, P])
        squared, var_ready, root_ready, diag_ready, rs_done = (ph.sem(n) for n in ("squared", "var_ready", "root_ready", "diag_ready", "rs_done"))
        c_loaded, rows_loaded, x_loaded = ph.sem("c_loaded"), ph.sem("rows_loaded"), [ph.sem(f"x_loaded{j}") for j in range(2)]
        act_done, c_turned, c_rounded, c_ready = ph.sem("act_done"), ph.sem("c_turned"), ph.sem("c_rounded"), ph.sem("c_ready")
        rows_turned, c_zeroed = ph.sem("rows_turned"), ph.sem("c_zeroed")
        row_ready, mod_turned, passed = ph.sem("row_ready"), ph.sem("mod_turned"), ph.sem("passed")
        x_turned, taken, stored = ph.sem("x_turned"), ph.sem("taken"), ph.sem("stored")
        w_v = dr.w_ada.rearrange("a (k p) n -> p (a k) n", p=P)
        NR = len(ROWS)
        height = [sum(n for _, n in rows) for rows in ROWS]
        views = {
            "gdn_norm_w": dr.gdn_norm_w, "diff_head_norm_g_2": dr.diff_head_norm_g_2,
            "mem_q_norm_g_2": dr.mem_q_norm_g_2, "mem_k_norm_g_2": dr.mem_k_norm_g_2,
            "conv_ssd_w": dr.conv_ssd_w.rearrange("a t (k p) -> (a t k) p", p=P),
            "conv_gdn_w": dr.conv_gdn_w.rearrange("a t (k p) -> (a t k) p", p=P),
            "conv_w_2": dr.conv_w_2.rearrange("a t (k p) -> (a t k) p", p=P),
        }
        for n, v in (("b_ada", dr.b_ada), ("pre_norm_w", dr.pre_norm_w), ("post_norm_w", dr.post_norm_w), ("norm_g_2", dr.norm_g_2),
                     ("mem_norm_g_2", dr.mem_norm_g_2), ("ssd_norm_w", dr.ssd_norm_w),
                     ("conv_ssd_b", dr.conv_ssd_b), ("conv_b_2", dr.conv_b_2)):
            views[n] = v.rearrange("a (k p) -> (a k) p", p=P)
        ndma = sum(len(r) for r in ROWS) + 2

        def in_turns(eng, body):
            for n in range(MTL):
                body(BT * n, n % 2, n, mem[:, :, n * P:(n + 1) * P])
            with eng.Fori(0, (len(tiles) - MTL) // 2) as i:
                for j in range(2):
                    body(i * (2 * BT) + BT * (MTL + j), j, i * 2 + (MTL + j), x_sb[:, :, bass.ds(i * (2 * P) + j * P, P)])

        with nc.Block() as block:
            @block.sync
            def _(sp):
                sp.dma_start(ident[:], dr.consts[:, C_ID:C_ID + P]).then_inc(c_loaded, 16)
                sp.dma_start(ones[:], dr.consts[:, C_ONES:C_ONES + P]).then_inc(c_loaded, 16)
                sp.dma_start(crow[0:KT, :], dr.c.rearrange("a (k p) -> (a k) p", p=P)).then_inc(c_loaded, 16)
                sp.dma_start(crow[KT:2 * KT, :], dr.c_ctx.rearrange("(k p) -> k p", p=P)).then_inc(c_loaded, 16)
                st.load(sp, 0, [(0, w_v[:, :, 0:256])], first=True)
                with sp.Fori(1, NB) as b:
                    st.load(sp, b, [(0, w_v[:, :, bass.ds(b * 256, 256)])])

            @block.gpsimd
            def _(pool):
                def load(n):
                    src, t = tiles[n]
                    pool.dma_start(xin[:, n % 2, :], src[0, t * P:(t + 1) * P, :]).then_inc(x_loaded[n % 2], 16)

                load(0)
                load(1)
                for t, rows in enumerate(ROWS):
                    at = 0
                    for name, n in rows:
                        if name in ("diff_q_norm_g_2", "diff_k_norm_g_2"):
                            src = dr.diff_q_norm_g_2 if name == "diff_q_norm_g_2" else dr.diff_k_norm_g_2
                            for half in range(2):
                                pool.dma_start(rowt[at:at + n, t, half * 64:half * 64 + 64], src).then_inc(rows_loaded, 16)
                        else:
                            pool.dma_start(rowt[at:at + n, t, :], views[name]).then_inc(rows_loaded, 16)
                        at += n
                for n in range(2, len(tiles)):
                    pool.wait_ge(x_turned, 4 * (n - 1))
                    pool.wait_ge(squared, n - 1)
                    load(n)
                    if n == MTL + 1:
                        pool.wait_ge(taken, 4 * MTL)
                        pool.dma_start(dr.memT.rearrange("(k p) t -> p k t", p=P), mem[:]).then_inc(stored, 16)
                pool.wait_ge(taken, 4 * (MTL + LCH))
                pool.dma_start(dr.xT.rearrange("(k p) t -> p k t", p=P), x_sb[:, :, 0:LAT]).then_inc(stored, 16)
                pool.wait_ge(stored, 32)

            @block.tensor
            def _(pe):
                pe.wait_ge(act_done, 1)
                pe.transpose(pst[0][:, 0:2 * KT], cact[:], ident[0:2 * KT, 0:2 * KT]).then_inc(c_turned, 1)
                pe.wait_ge(c_ready, 1)

                def turn_rows(b, s):
                    pe.wait_ge(row_ready, b + 1)
                    pe.sem_inc(passed, 1)
                    for m in range(2):
                        mm = pe.transpose(turned[s][:, 2 * m:2 * m + 2], rows[:, s, m * P:(m + 1) * P], ident[0:2, 0:2])
                    mm.then_inc(mod_turned, 1)

                def body(b0, j, n, dst):
                    pe.wait_ge(x_loaded[j], (n - j) * 8 + 16)
                    for g in range(4):
                        if type(n) is not int or n:
                            pe.wait_ge(taken, n * 4 + g - 3)
                        for k in range(4):
                            mm = pe.transpose(pst[g][:, k * P:(k + 1) * P], xin[:, j, (4 * g + k) * P:(4 * g + k + 1) * P], ident[:])
                        mm.then_inc(x_turned, 1)
                    for q in range(BT):
                        b, s = b0 + q, (j + q) % 2
                        if type(b) is not int or b >= 2:
                            pe.wait_ge(row_ready, b - 1)
                        for u in range(st.U):
                            pe.wait_ge(st.lo_ready, b * st.U + (u + 1))
                            for k in range(st.UK):
                                kt = u * st.UK + k
                                for p, (wt, ct) in enumerate(((st.whi, c_hi), (st.whi, c_lo), (st.wlo, c_hi))):
                                    mm = pe.matmul(acc[s][:, 0:256], ct[:, kt, :], wt[:, u, k, :], start=(kt == p == 0),
                                                   stop=(kt == KT - 1 and p == 2))
                            mm.then_inc(st.unit_done, 1)
                        if type(b) is not int or b >= 1:
                            turn_rows(b - 1, 1 - s)

                in_turns(pe, body)
                pe.wait_ge(rows_loaded, 16 * ndma)
                pe.wait_ge(taken, 4 * NTL)
                for t in range(NR):
                    mm = pe.transpose(pst[1][:, t * P:t * P + height[t]], rowt[0:height[t], t, :],
                                      ident[0:height[t], 0:height[t]])
                mm.then_inc(rows_turned, 1)
                turn_rows(NB - 1, 1)
                pe.wait_ge(diag_ready, 1)
                for n in range(2):
                    mm = pe.matmul(pst[2 + n][:], ones[:], diag[:, 4 * n:4 * n + 4, :].rearrange("p n t -> p (n t)"), start=True, stop=True)
                mm.then_inc(rs_done, 1)

            @block.scalar
            def _(act):
                act.wait_ge(c_loaded, 64)
                act.activation(cact[:], crow[:], ACT.Silu).then_inc(act_done, 1)
                act.wait_ge(c_turned, 1)
                act.wait_ge(c_zeroed, 1)
                act.activation(c_hi[:, :, 0:2].rearrange("p k v -> p v k"), pst[0][:, 0:2 * KT].rearrange("p (v k) -> p v k", v=2), ACT.Copy)\
                    .then_inc(c_rounded, 1)

                def body(b0, j, n, dst):
                    for q in range(BT):
                        first = q == 0 and type(b0) is int and b0 == 0
                        st.split_hi(act, b0 + q, (b0 + (q + 1)) * 16, first=first)
                        if q == 0:
                            for g in range(4):
                                act.wait_ge(x_turned, n * 4 + (g + 1))
                                act.activation(dst[:, 4 * g:4 * g + 4, :], pst[g][:].rearrange("p (k t) -> p k t", k=4), ACT.Copy)\
                                    .then_inc(taken, 1)
                            act.activation(square[:], xin[:, j, :], ACT.Square, accum_out=root[:, bass.ds(n, 1)]).then_inc(squared, 1)

                in_turns(act, body)
                act.wait_ge(var_ready, 1)
                act.activation(root[:], root[:], ACT.Sqrt).then_inc(root_ready, 1)

            @block.vector
            def _(dve):
                dve.memset(zero[:], 0.0)
                dve.memset(cols[:], 0.0)
                dve.drain()
                dve.tensor_copy(c_hi[:], bc(zero[:], KT, 1))
                dve.tensor_copy(c_lo[:], bc(zero[:], KT, 1))
                dve.drain().then_inc(c_zeroed, 1)
                dve.wait_ge(c_rounded, 1)
                dve.tensor_tensor(c_lo[:, :, 0:2].rearrange("p k v -> p v k"), pst[0][:, 0:2 * KT].rearrange("p (v k) -> p v k", v=2),
                                  c_hi[:, :, 0:2].rearrange("p k v -> p v k").bitcast(F32), ALU.subtract).then_inc(c_ready, 1)

                def collect(b, s):
                    dve.wait_ge(mod_turned, b + 1)
                    dve.tensor_copy(modc[:, bass.ds(b * 4, 4)], turned[s][:, 0:4])

                def take(b, s):
                    dve.wait_ge(st.unit_done, b * st.U + st.U)
                    if type(b) is not int or b >= 2:
                        collect(b - 2, s)
                    dve.tensor_copy(rows[:, s, :], acc[s][0:2, 0:256]).then_inc(row_ready, 1)

                st.split_lo(dve, 0)
                st.split_lo(dve, 1)
                take(0, 0)
                st.split_lo(dve, 2)
                take(1, 1)
                st.split_lo(dve, 3)
                take(2, 0)
                with dve.Fori(2, NB // 2) as i:
                    for s in range(2):
                        st.split_lo(dve, i * 2 + s)
                        take(i * 2 + (s - 1), 1 - s)
                take(NB - 1, 1)
                dve.wait_ge(squared, NTL)
                dve.tensor_scalar(root[:], root[:], 1.0 / D, EPS, ALU.mult, ALU.add).then_inc(var_ready, 1)
                dve.wait_ge(rows_turned, 1)
                for t in range(NR):
                    dve.tensor_copy(cols[:, t * P:t * P + height[t]], pst[1][:, t * P:t * P + height[t]])
                for s in range(2):
                    collect(NB - 2 + s, s)
                dve.wait_ge(root_ready, 1)
                dve.reciprocal(root[:], root[:])
                dve.drain()
                for n in range(NTL):
                    dve.tensor_scalar(diag[:, n, :], ident[:], root[:, n:n + 1], None, ALU.mult)
                dve.drain().then_inc(diag_ready, 1)
                b0, m0 = COL["b_ada"], COL["mod"]
                dve.tensor_tensor(cols[:, m0:m0 + 2 * NMOD].rearrange("p (v n) -> p v n", v=2),
                                  modc[:].rearrange("p (n v) -> p v n", v=2), bc(cols[:, b0:b0 + NMOD], 2, 1), ALU.add)
                dve.wait_ge(rs_done, 1)
                for n in range(2):
                    dve.tensor_copy(rs[:, 512 * n:512 * n + 512], pst[2 + n][:])


class Stream:

    def __init__(self, ph, ctx=True, banks=True, uk=KT // 2, deep=2, slots=2):
        self.UK, self.U, self.deep, self.slots = uk, KT // uk, deep, slots
        self.stage = ph.sb("stage", [P, deep, uk, 256])
        self.whi = ph.sb("whi", [P, slots, uk, 256], F32R)
        self.wlo = ph.sb("wlo", [P, slots, uk, 256], F32R)
        self.w_loaded = [ph.sem(f"w_loaded{j}") for j in range(deep)]
        self.hi_ready, self.lo_ready = ph.sem("hi_ready"), ph.sem("lo_ready")
        self.unit_done, self.bank_free = ph.sem("unit_done"), ph.sem("bank_free")
        self.lat = [[ph.pb(f"lat{s}{m}") for m in range(2)] for s in range(2)] if banks else None
        self.ctx = [ph.pb(f"ctx{s}") for s in range(2)] if banks and ctx else None

    def load(self, sp, b, pieces, first=False):
        for j in range(self.U):
            if not first or j >= self.deep:
                sp.wait_ge(self.lo_ready, b * self.U + (j - self.deep + 1))
            for at, src in pieces:
                n = src.shape[2]
                sp.dma_start(self.stage[:, j % self.deep, :, at:at + n], src[:, j * self.UK:(j + 1) * self.UK, :])\
                    .then_inc(self.w_loaded[j % self.deep], 16)

    def split_hi(self, act, b, loaded, n=256, first=False, pieces=1, units=None):
        for j in units or range(self.U):
            act.wait_ge(self.w_loaded[j % self.deep], loaded + j // self.deep * (16 * pieces))
            if not first or j >= self.slots:
                act.wait_ge(self.unit_done, b * self.U + (j - self.slots + 1))
            act.activation(self.whi[:, j % self.slots, :, 0:n], self.stage[:, j % self.deep, :, 0:n], ACT.Copy).then_inc(self.hi_ready, 1)

    def split_lo(self, dve, b, n=256, units=None):
        for j in units or range(self.U):
            dve.wait_ge(self.hi_ready, b * self.U + (j + 1))
            dve.tensor_tensor(self.wlo[:, j % self.slots, :, 0:n], self.stage[:, j % self.deep, :, 0:n],
                              self.whi[:, j % self.slots, :, 0:n].bitcast(F32), ALU.subtract).then_inc(self.lo_ready, 1)

    def products(self, pe, b, s, u_hi, u_lo, tiles=2, lat=True, ctx=True, u_ready=None):
        pe.wait_ge(self.bank_free, b + 1)
        for j in range(self.U):
            pe.wait_ge(self.lo_ready, b * self.U + (j + 1))
            for k in range(self.UK):
                kt = j * self.UK + k
                if u_ready is not None:
                    pe.wait_ge(u_ready, kt + 1)
                for m in range(tiles):
                    for wt, ut, p in ((self.whi, u_hi, 0), (self.whi, u_lo, 1), (self.wlo, u_hi, 2)):
                        w = wt[:, j % self.slots, k, m * P:(m + 1) * P]
                        head, last = kt == 0 and p == 0, kt == KT - 1 and p == 2
                        if lat:
                            mm = pe.matmul(self.lat[s][m][:], w, ut[:, kt, 0:LAT], start=head, stop=last)
                        if ctx:
                            mm = pe.matmul(self.ctx[s][:, m * CTX:(m + 1) * CTX], w, ut[:, kt, LAT if lat else 0:][:, 0:CTX],
                                           start=head and m == 0, stop=last, skip_group_check=True)
            mm.then_inc(self.unit_done, 1)


class Norm:

    def __init__(self, ph, src, T, outs, x, cols, modulated=False, rs=None):
        self.src, self.T, self.outs, self.x, self.cols, self.modulated, self.given = src, T, outs, x, cols, modulated, rs is not None
        if self.given:
            self.rs = rs
        else:
            self.sq, self.ones, self.rs = ph.sb("sq", [P, 2, T]), ph.sb("ones", [P, P]), ph.sb("rs", [P, T])
        self.sc = ph.sb("sc", [P, sum(len(segs) for _, _, segs in outs), KT])
        self.banks = [(0, LAT if T > LAT else T)] + ([(LAT, CTX)] if T > LAT else [])
        self.pss = None if self.given else [ph.pb(f"pss{i}") for i in range(len(self.banks))]
        self.ones_loaded, self.x_loaded = ph.sem("ones_loaded"), [ph.sem(f"x_loaded{g}") for g in range(4)]
        self.sq_ready, self.sq_used, self.var_ready = ph.sem("sq_ready"), ph.sem("sq_used"), ph.sem("var_ready")
        self.root_ready, self.scaled, self.moved = ph.sem("root_ready"), ph.sem("scaled"), ph.sem("moved")
        self.round_ready, self.scale_ready, self.u_ready = ph.sem("round_ready"), ph.sem("scale_ready"), ph.sem("u_ready")

    def load(self, sp, dr):
        if not self.given:
            sp.dma_start(self.ones[:], dr.consts[:, C_ONES:C_ONES + P]).then_inc(self.ones_loaded, 16)
        for g in range(4 if self.src is not None else 0):
            x_v = self.src.rearrange("(k p) t -> p k t", p=P)
            sp.dma_start(self.x[:, 4 * g:4 * g + 4, :], x_v[:, 4 * g:4 * g + 4, 0:self.T]).then_inc(self.x_loaded[g], 16)

    def on_act(self, act):
        for k in range(0 if self.given else KT):
            if self.src is not None and k % 4 == 0:
                act.wait_ge(self.x_loaded[k // 4], 16)
            if k >= 2:
                act.wait_ge(self.sq_used, k - 1)
            act.activation(self.sq[:, k % 2, :], self.x[:, k, :], ACT.Square).then_inc(self.sq_ready, 1)
        if not self.given:
            act.wait_ge(self.var_ready, 1)
            act.activation(self.rs[:], self.rs[:], ACT.Sqrt).then_inc(self.root_ready, 1)
        act.wait_ge(self.scale_ready, 1)
        for k in range(KT):
            act.wait_ge(self.scaled, k + 1)
            n = 0
            for i, (u_hi, _, segs) in enumerate(self.outs):
                for t0, nt, _, shift in segs:
                    if shift is None:
                        op = act.activation(u_hi[:, k, t0:t0 + nt], self.x[:, k, t0:t0 + nt], ACT.Copy, scale=self.sc[:, n, k:k + 1])
                    else:
                        op = act.activation(self.x[:, k, t0:t0 + nt], self.x[:, k, t0:t0 + nt], ACT.Identity,
                                            bias=shift[:, k:k + 1], scale=self.sc[:, n, k:k + 1])
                    n += 1
                if segs[0][3] is not None:
                    op.then_inc(self.moved, 1)
                    act.wait_ge(self.moved, k + 1)
                    op = act.activation(u_hi[:, k, :], self.x[:, k, :], ACT.Copy)
                op.then_inc(self.round_ready, 1)

    def on_pe(self, pe):
        if self.given:
            return
        pe.wait_ge(self.ones_loaded, 16)
        for k in range(KT):
            pe.wait_ge(self.sq_ready, k + 1)
            for i, (t0, nt) in enumerate(self.banks):
                mm = pe.matmul(self.pss[i][:, 0:nt], self.ones[:], self.sq[:, k % 2, t0:t0 + nt], start=(k == 0), stop=(k == KT - 1))
            mm.then_inc(self.sq_used, 1)

    def on_dve(self, dve):
        n = 0
        for _, _, segs in self.outs:
            for _, _, scale, _ in segs:
                if self.modulated:
                    w0 = COL["pre_norm_w"]
                    dve.scalar_tensor_tensor(out=self.sc[:, n, :], in0=scale, scalar=1.0, in1=self.cols[:, w0:w0 + KT],
                                             op0=ALU.add, op1=ALU.mult)
                else:
                    dve.tensor_copy(self.sc[:, n, :], scale)
                n += 1
        dve.drain().then_inc(self.scale_ready, 1)
        if not self.given:
            dve.wait_ge(self.sq_used, KT)
            for i, (t0, nt) in enumerate(self.banks):
                dve.tensor_scalar(self.rs[:, t0:t0 + nt], self.pss[i][:, 0:nt], 1.0 / D, EPS, ALU.mult, ALU.add)
            dve.drain().then_inc(self.var_ready, 1)
            dve.wait_ge(self.root_ready, 1)
            dve.reciprocal(self.rs[:], self.rs[:])
            dve.drain()

        def left(k):
            n = 0
            for i, (u_hi, u_lo, segs) in enumerate(self.outs):
                dve.wait_ge(self.round_ready, k * len(self.outs) + i + 1)
                if segs[0][3] is None:
                    for t0, nt, _, _ in segs:
                        op = dve.scalar_tensor_tensor(out=u_lo[:, k, t0:t0 + nt], in0=self.x[:, k, t0:t0 + nt],
                                                      scalar=self.sc[:, n, k:k + 1], in1=u_hi[:, k, t0:t0 + nt].bitcast(F32),
                                                      op0=ALU.mult, op1=ALU.subtract)
                        n += 1
                else:
                    op = dve.tensor_tensor(u_lo[:, k, :], self.x[:, k, :], u_hi[:, k, :].bitcast(F32), ALU.subtract)
            op.then_inc(self.u_ready, 1)

        for k in range(KT):
            if self.given and self.src is not None and k % 4 == 0:
                dve.wait_ge(self.x_loaded[k // 4], 16)
            dve.tensor_tensor(self.x[:, k, :], self.x[:, k, :], self.rs[:], ALU.mult).then_inc(self.scaled, 1)
            if k >= 1:
                left(k - 1)
        left(KT - 1)


def project(nc, dr, cols, x_sb, rs):
    w_v = dr.w_in.rearrange("a (k p) n -> p (a k) n", p=P)
    GT = 3 * GDN_W // P
    SEGS = [
        (XBC // 256, OFF_XBC, True, COL["conv_ssd_w"], XBC // P, COL["conv_ssd_b"], dr.xbcT),
        (GDN_W // 256, OFF_QKV, False, COL["conv_gdn_w"], GT, None, dr.qT),
        (2 * GDN_W // 256, OFF_QKV + GDN_W, True, COL["conv_gdn_w"] + GDN_W // P, GT, None, dr.kvT),
        (D // 256, 0, False, None, None, None, dr.zT),
    ]
    with Phase(nc, "proj") as ph:
        u_hi, u_lo = ph.sb("u_hi", [P, KT, TOK], F32R), ph.sb("u_lo", [P, KT, TOK], F32R)
        st = Stream(ph, uk=KT // 4)
        mod = COL["mod"]
        norm = Norm(ph, None, TOK, [(u_hi, u_lo, [(0, LAT, cols[:, mod + KT:mod + 2 * KT], cols[:, mod:mod + KT]),
                                                   (LAT, CTX, cols[:, mod + 4 * KT:mod + 5 * KT], cols[:, mod + 3 * KT:mod + 4 * KT])])],
                    x_sb, cols, modulated=True, rs=rs)
        obuf = ph.sb("obuf", [P, 2, TOK])
        zeroed, center, taps_done = ph.sem("zeroed"), ph.sem("center"), ph.sem("taps_done")
        out_ready, stored = [ph.sem(f"out_ready{m}") for m in range(2)], [ph.sem(f"stored{m}") for m in range(2)]
        BASE = [1]
        for seg in SEGS:
            BASE.append(BASE[-1] + seg[0])
        CONVS = [0, SEGS[0][0], SEGS[0][0] + SEGS[1][0], SEGS[0][0] + SEGS[1][0] + SEGS[2][0]]

        with nc.Block() as block:
            @block.sync
            def _(sp):
                norm.load(sp, dr)
                sp.wait_ge(zeroed, 1)
                st.load(sp, 0, [(0, w_v[:, :, OFF_DT:OFF_DT + BETA0]), (BETA0, w_v[:, :, OFF_BETA:OFF_BETA + NSMALL - BETA0])], first=True)
                for n, (nb, c0, *_) in enumerate(SEGS):
                    with sp.Fori(0, nb) as i:
                        st.load(sp, i + BASE[n], [(0, w_v[:, :, bass.ds(i * 256 + c0, 256)])])

            @block.gpsimd
            def _(pool):
                pool.memset(st.stage[:, :, :, NSMALL:P], 0.0).then_inc(zeroed, 1)
                pool.wait_ge(out_ready[0], 1)
                pool.dma_start(dr.smallT, obuf[0:NSMALL, 0, :]).then_inc(stored[0], 16)
                for n, (nb, _, ctx, _, _, _, out) in enumerate(SEGS):
                    T = TOK if ctx else LAT
                    with pool.Fori(0, nb) as i:
                        for m in range(2):
                            pool.wait_ge(out_ready[m], i + (BASE[n] + 1 - m))
                            pool.dma_start(out[bass.ds(i * 256 + m * P, P), :], obuf[:, m, 0:T]).then_inc(stored[m], 16)
                for m in range(2):
                    pool.wait_ge(stored[m], 16 * (BASE[-1] - m))

            @block.tensor
            def _(pe):
                norm.on_pe(pe)
                st.products(pe, 0, 0, u_hi, u_lo, tiles=1, u_ready=norm.u_ready)
                for n, (nb, _, ctx, *_) in enumerate(SEGS):
                    with pe.Fori(0, nb // 2) as i:
                        for c in range(2):
                            st.products(pe, i * 2 + (BASE[n] + c), (BASE[n] + c) % 2, u_hi, u_lo, ctx=ctx)

            @block.scalar
            def _(act):
                def written_out(b):
                    for m in range(2):
                        act.wait_ge(stored[m], (b - m + 1) * 16)

                def epilogue(n, i, c, following=True):
                    nb, _, ctx, wcol, step, bcol, _ = SEGS[n]
                    b, s = i * 2 + (BASE[n] + c), (BASE[n] + c) % 2
                    T = TOK if ctx else LAT
                    if following:
                        st.split_hi(act, b + 1, b * 32 + 80, units=(0, 1))
                    act.wait_ge(st.unit_done, b * st.U + st.U)
                    for m in range(2):
                        if wcol is None:
                            act.activation(obuf[:, m, 0:LAT], st.lat[s][m][:], ACT.Silu).then_inc(out_ready[m], 1)
                            continue
                        mid = cols[:, bass.ds(i * 4 + (wcol + 2 * step + 2 * c + m), 1)]
                        for src, at, nt in ([(st.lat[s][m][:], 0, LAT)] + ([(st.ctx[s][:, m * CTX:(m + 1) * CTX], LAT, CTX)] if ctx else [])):
                            if bcol is None:
                                op = act.activation(obuf[:, m, at:at + nt], src, ACT.Copy, scale=mid)
                            else:
                                op = act.activation(obuf[:, m, at:at + nt], src, ACT.Identity, scale=mid,
                                                    bias=cols[:, bass.ds(i * 4 + (bcol + 2 * c + m), 1)])
                        op.then_inc(center, 1)
                    if following:
                        st.split_hi(act, b + 1, b * 32 + 80, units=(2, 3))
                    if wcol is not None:
                        for m in range(2):
                            act.wait_ge(taps_done, i * 4 + (2 * CONVS[n] + 2 * c + m + 1))
                            act.activation(obuf[:, m, 0:T], obuf[:, m, 0:T], ACT.Silu).then_inc(out_ready[m], 1)
                    written_out(b)

                act.wait_ge(zeroed, 1)
                st.split_hi(act, 0, 32, n=P, first=True, pieces=2, units=(0, 1))
                norm.on_act(act)
                st.split_hi(act, 0, 32, n=P, first=True, pieces=2, units=(2, 3))
                st.split_hi(act, 1, 32 + 48)
                act.wait_ge(st.unit_done, st.U)
                act.activation(obuf[:, 0, 0:LAT], st.lat[0][0][:], ACT.Copy)
                act.activation(obuf[:, 0, LAT:TOK], st.ctx[0][:, 0:CTX], ACT.Copy)
                act.drain().then_inc(out_ready[0], 1)
                act.wait_ge(stored[0], 16)
                for n in range(len(SEGS)):
                    last = n == len(SEGS) - 1
                    with act.Fori(0, SEGS[n][0] // 2 - last) as i:
                        for c in range(2):
                            epilogue(n, i, c)
                    if last:
                        i = SEGS[n][0] // 2 - 1
                        epilogue(n, i, 0)
                        epilogue(n, i, 1, following=False)

            @block.vector
            def _(dve):
                def taps(n, i, c):
                    nb, _, ctx, wcol, step, bcol, _ = SEGS[n]
                    if wcol is None:
                        dve.wait_ge(out_ready[1], i * 2 + (BASE[n] + c))
                        dve.sem_inc(st.bank_free, 1)
                        return
                    s = (BASE[n] + c) % 2
                    dve.wait_ge(center, i * 4 + (2 * CONVS[n] + 2 * c + 2))
                    for m in range(2):
                        views = [(st.lat[s][m][:].rearrange("p (r w) -> p r w", w=GRID),
                                  obuf[:, m, 0:LAT].rearrange("p (r w) -> p r w", w=GRID), GRID)]
                        if ctx:
                            views.append((st.ctx[s][:, m * CTX:(m + 1) * CTX].unsqueeze(1), obuf[:, m, LAT:TOK].unsqueeze(1), CTX))
                        for tap in (0, 1, 3, 4):
                            off = tap - TAPS // 2
                            a, z = max(0, -off), max(0, off)
                            if tap:
                                dve.drain()
                            for x, o, w in views:
                                op = dve.scalar_tensor_tensor(
                                    out=o[:, :, a:w - z], in0=x[:, :, a + off:w - z + off],
                                    scalar=cols[:, bass.ds(i * 4 + (wcol + tap * step + 2 * c + m), 1)],
                                    in1=o[:, :, a:w - z], op0=ALU.mult, op1=ALU.add)
                        op.then_inc(taps_done, 1)
                    dve.drain().then_inc(st.bank_free, 1)

                dve.sem_inc(st.bank_free, 2)
                st.split_lo(dve, 0, n=P, units=(0, 1))
                norm.on_dve(dve)
                st.split_lo(dve, 0, n=P, units=(2, 3))
                st.split_lo(dve, 1)
                dve.wait_ge(out_ready[0], 1)
                dve.sem_inc(st.bank_free, 1)
                for n in range(len(SEGS)):
                    last = n == len(SEGS) - 1
                    with dve.Fori(0, SEGS[n][0] // 2 - last) as i:
                        for c in range(2):
                            st.split_lo(dve, i * 2 + (BASE[n] + c + 1), units=(0, 1))
                            taps(n, i, c)
                            st.split_lo(dve, i * 2 + (BASE[n] + c + 1), units=(2, 3))
                    if last:
                        i = SEGS[n][0] // 2 - 1
                        st.split_lo(dve, i * 2 + BASE[n] + 1, units=(0, 1))
                        taps(n, i, 0)
                        st.split_lo(dve, i * 2 + BASE[n] + 1, units=(2, 3))
                        taps(n, i, 1)



Q_NA, Q_EA, Q_NEA, Q_ETOT, Q_DT, Q_DTEND, Q_BETA, Q_NBETA, Q_BEND = range(9)
NQ = 9


def decays(nc, dr, tq, ident):
    with Phase(nc, "dec") as ph:
        raw = ph.sb("raw", [NSMALL, TOK])
        bias = ph.sb("bias", [NSMALL, 2])
        xs, ab, ex = ph.sb("xs", [NSMALL, TOK]), ph.sb("ab", [NSMALL, TOK]), ph.sb("ex", [NSMALL, TOK])
        u, ln, sg = ph.sb("u", [NSMALL, TOK]), ph.sb("ln", [NSMALL, TOK]), ph.sb("sg", [NSMALL, TOK])
        lnu = ph.sb("lnu", [NSMALL, TOK])
        rate = ph.sb("rate", [NSMALL, 1])
        cum = ph.sb("cum", [P, 3, P])
        lg, a, tot = ph.sb("lg", [P, NCH, NSMALL]), ph.sb("a", [P, NCH, NSMALL]), ph.sb("tot", [P, NCH, NSMALL])
        arow = ph.sb("arow", [NSMALL, TOK])
        bank = [ph.pb(f"bank{i}") for i in range(8)]
        zeroed, c_loaded, raw_loaded = ph.sem("zeroed"), ph.sem("c_loaded"), ph.sem("raw_loaded")
        d_done, a_done, p_done, stored = ph.sem("d_done"), ph.sem("a_done"), ph.sem("p_done"), ph.sem("stored")
        W = NCH * NSMALL

        def flat(t):
            return t.rearrange("p c r -> p (c r)")

        with nc.Block() as block:
            @block.sync
            def _(sp):
                sp.dma_start(raw[:], dr.smallT).then_inc(raw_loaded, 16)
                sp.dma_start(cum[:, 0:2, :], dr.consts[:, C_CUM:C_CUM + 2 * P].rearrange("p (n q) -> p n q", n=2)).then_inc(c_loaded, 16)
                sp.dma_start(cum[:, 2, :], dr.consts[:, C_ONES:C_ONES + P]).then_inc(c_loaded, 16)
                sp.wait_ge(zeroed, 1)
                for n, (s, g) in enumerate(((dr.ssd_dt_bias, dr.gdn_dt_bias), (dr.ssd_a_log, dr.gdn_a_log))):
                    sp.dma_start(bias[0:BETA0, n:n + 1], s.rearrange("a d h -> (d h) a")).then_inc(c_loaded, 16)
                    sp.dma_start(bias[ALPHA0:NSMALL, n:n + 1], g.rearrange("a d h -> (d h) a")).then_inc(c_loaded, 16)
                sp.wait_ge(d_done, 6)
                sp.dma_start(dr.arow, arow[:]).then_inc(stored, 16)
                sp.wait_ge(stored, 16)

            @block.vector
            def _(dve):
                dve.memset(bias[:], 0.0).then_inc(zeroed, 1)
                dve.wait_ge(c_loaded, 96)
                dve.wait_ge(raw_loaded, 16)
                dve.tensor_scalar(xs[:], raw[:], bias[:, 0:1], None, ALU.add).then_inc(d_done, 1)
                dve.wait_ge(a_done, 2)
                dve.tensor_scalar(u[:], ab[:], 1.0, None, ALU.add)
                dve.tensor_scalar(ex[:], ex[:], 1.0, None, ALU.add)
                dve.drain().then_inc(d_done, 1)
                dve.reciprocal(sg[:], ex[:])
                dve.tensor_scalar(ln[:], u[:], -1.0, None, ALU.add)
                dve.drain()
                dve.tensor_tensor(ln[:], ab[:], ln[:], ALU.subtract)
                dve.reciprocal(ex[:], u[:])
                dve.drain()
                dve.tensor_tensor(ln[:], ln[:], ex[:], ALU.mult)
                dve.tensor_scalar(xs[:], xs[:], 0.0, None, ALU.max)
                dve.drain()
                dve.tensor_tensor(xs[:], xs[:], ln[:], ALU.add)
                dve.wait_ge(a_done, 3)
                dve.drain()
                dve.tensor_tensor(xs[:], xs[:], lnu[:], ALU.add)
                dve.tensor_scalar(rate[:], rate[:], -1.0, None, ALU.mult)
                dve.drain()
                dve.tensor_scalar(ab[:], xs[:], rate[:], None, ALU.mult)
                dve.drain().then_inc(d_done, 1)
                dve.wait_ge(p_done, 1)
                dve.tensor_copy(flat(lg[:]), bank[0][:, 0:W])
                dve.tensor_copy(flat(tq[:, Q_DT]), bank[1][:, 0:W])
                dve.tensor_copy(flat(tq[:, Q_BETA]), bank[2][:, 0:W])
                dve.drain().then_inc(d_done, 1)
                dve.wait_ge(p_done, 2)
                dve.tensor_copy(flat(a[:]), bank[3][:, 0:W])
                dve.tensor_copy(flat(tot[:]), bank[5][:, 0:W])
                dve.drain()
                back = bank[4][:, 0:W].rearrange("p (c r) -> p c r", c=NCH)
                for r0, n in ((SSD_H, SSD_H), (ALPHA0 + GDN_H, GDN_H)):
                    dve.tensor_copy(a[:, :, r0:r0 + n], back[:, :, r0:r0 + n])
                dve.drain()
                dve.tensor_scalar(flat(tq[:, Q_NA]), flat(a[:]), -1.0, None, ALU.mult)
                dve.tensor_tensor(flat(lg[:]), flat(tot[:]), flat(a[:]), ALU.subtract)
                dve.tensor_scalar(flat(tq[:, Q_NBETA]), flat(tq[:, Q_BETA]), -1.0, None, ALU.mult)
                dve.drain().then_inc(d_done, 1)
                dve.wait_ge(p_done, 3)
                for n in range(2):
                    w = LAT if n == 0 else CTX
                    dve.tensor_copy(arow[:, n * LAT:n * LAT + w], bank[6 + n][0:NSMALL, 0:w])
                dve.drain().then_inc(d_done, 1)
                dve.wait_ge(a_done, 4)
                dve.tensor_scalar(flat(tq[:, Q_NEA]), flat(tq[:, Q_EA]), -1.0, None, ALU.mult)
                dve.tensor_tensor(flat(tq[:, Q_DTEND]), flat(tq[:, Q_DT]), flat(lg[:]), ALU.mult)
                dve.memset(tq[:, Q_BEND], 0.0)
                dve.drain()
                dve.tensor_tensor(tq[:, Q_BEND, :, BETA0:ALPHA0], tq[:, Q_BETA, :, BETA0:ALPHA0],
                                  lg[:, :, ALPHA0:NSMALL], ALU.mult)
                dve.drain()

            @block.scalar
            def _(act):
                act.wait_ge(d_done, 1)
                act.activation(ab[:], xs[:], ACT.Abs)
                act.activation(rate[:], bias[:, 1:2], ACT.Exp)
                act.activation(ex[:], raw[:], ACT.Exp, scale=-1.0).then_inc(a_done, 1)
                act.drain()
                act.activation(ab[:], ab[:], ACT.Exp, scale=-1.0).then_inc(a_done, 1)
                act.wait_ge(d_done, 2)
                act.activation(lnu[:], u[:], ACT.Ln).then_inc(a_done, 1)
                act.wait_ge(d_done, 5)
                act.activation(flat(tq[:, Q_EA]), flat(a[:]), ACT.Exp)
                act.activation(flat(tq[:, Q_ETOT]), flat(tot[:]), ACT.Exp)
                act.activation(flat(lg[:]), flat(lg[:]), ACT.Exp)
                act.drain().then_inc(a_done, 1)

            @block.tensor
            def _(pe):
                pe.wait_ge(d_done, 3)
                for n, src in enumerate((ab, xs, sg)):
                    for c in range(NCH):
                        mm = pe.transpose(bank[n][:, c * NSMALL:(c + 1) * NSMALL], src[:, c * P:(c + 1) * P],
                                          ident[0:NSMALL, 0:NSMALL])
                mm.then_inc(p_done, 1)
                pe.wait_ge(d_done, 4)
                for n in range(3):
                    mm = pe.matmul(bank[3 + n][:, 0:W], cum[:, n, :], flat(lg[:]), start=True, stop=True)
                mm.then_inc(p_done, 1)
                pe.wait_ge(d_done, 5)
                for c in range(NCH):
                    mm = pe.transpose(bank[6 + c // LCH][0:NSMALL, (c % LCH) * P:(c % LCH + 1) * P], a[:, c, :], ident[:])
                mm.then_inc(p_done, 1)


def ssd(nc, dr, cols, tq, ident):
    XT, NT = SSD_W // P, XBC // P
    GW = SSD_W // SSD_G
    HG = SSD_H // SSD_G
    with Phase(nc, "ssd") as ph:
        xT = ph.sb("xT", [P, NT, TOK])
        x_tok, b_tok = ph.sb("x_tok", [P, NCH, SSD_W]), ph.sb("b_tok", [P, NCH, SSD_G * SSD_N])
        cb = ph.sb("cb", [P, SSD_G, LCH, P])
        h = ph.sb("h", [P, 2, SSD_G, GW])
        y = ph.sb("y", [P, LCH, SSD_W])
        dsk = ph.sb("dsk", [P, SSD_H])
        neg = ph.sb("neg", [P, 2, P])
        ones = ph.sb("ones", [P, P])
        EB = 4
        E = ph.sb("E", [P, EB, 2, LCH, P])
        M = ph.sb("M", [P, 2, 2, LCH, P])
        tmp, xw = ph.sb("tmp", [P, 2, GW]), ph.sb("xw", [P, 2, GW])
        zT, sq = ph.sb("zT", [P, XT, LAT]), ph.sb("sq", [P, 2, LAT])
        rs = ph.sb("rs", [P, SSD_G, LAT])
        tb = [ph.pb(f"tb{i}") for i in range(4)]
        pb = [ph.pb(f"pb{i}") for i in range(4)]
        loaded, c_loaded, z_loaded = ph.sem("loaded"), ph.sem("c_loaded"), ph.sem("z_loaded")
        turned, taken_d, taken_a = ph.sem("turned"), ph.sem("taken_d"), ph.sem("taken_a")
        cb_done, cb_taken, y_init = ph.sem("cb_done"), ph.sem("cb_taken"), ph.sem("y_init")
        yoff_done, tmp_ready, y_added = ph.sem("yoff_done"), ph.sem("tmp_ready"), ph.sem("y_added")
        xw_ready, st_done, h_ready = ph.sem("xw_ready"), ph.sem("st_done"), ph.sem("h_ready")
        e_loaded, e_masked = [ph.sem(f"e_loaded{j}") for j in range(EB)], ph.sem("e_masked")
        e_ready, m_ready, diag_done, y_ready = ph.sem("e_ready"), ph.sem("m_ready"), ph.sem("diag_done"), ph.sem("y_ready")
        out_turned, gated, squared, summed = ph.sem("out_turned"), ph.sem("gated"), ph.sem("squared"), ph.sem("summed")
        var_ready, root_ready, out_ready, stored = ph.sem("var_ready"), ph.sem("root_ready"), ph.sem("out_ready"), ph.sem("stored")

        steps = [(t, d, g) for t in range(NCH) for d in range(2) for g in range(SSD_G)]
        lat_steps = [s for s in steps if t_lat(s)]
        st_steps = [s for s in steps if s[0] < NCH - 1]
        groups = []
        for c in range(NCH):
            groups += [(c, 0, 4), (c, 4, 4), (c, XT, SSD_G)]

        def heads(ap, n=SSD_P):
            return bc(ap, n, 2)

        with nc.Block() as block:
            @block.sync
            def _(sp):
                sp.dma_start(xT[:], dr.xbcT.rearrange("(k p) t -> p k t", p=P)).then_inc(loaded, 16)
                sp.dma_start(neg[:], dr.consts[:, C_NEG:C_NEG + 2 * P].rearrange("p (d q) -> p d q", d=2)).then_inc(c_loaded, 16)
                sp.dma_start(ones[:], dr.consts[:, C_ONES:C_ONES + P]).then_inc(c_loaded, 16)
                sp.dma_start(dsk[:], dr.ssd_d[0, :].partition_broadcast(P)).then_inc(c_loaded, 16)
                sp.dma_start(zT[:], dr.zT.rearrange("(k p) t -> p k t", p=P)[:, 0:XT, :]).then_inc(z_loaded, 16)
                for g in range(SSD_G):
                    with sp.Fori(0, HG // EB) as i:
                        for j in range(EB):
                            n = i * EB + (g * HG + j)
                            sp.wait_ge(m_ready, n + 1)
                            for d in range(2):
                                sp.dma_start(E[:, j, d, :, :].rearrange("p c q -> p (c q)"),
                                             dr.arow[bass.ds(n + d * SSD_H, 1), 0:LAT].rearrange("a t -> (a t)").partition_broadcast(P))\
                                    .then_inc(e_loaded[j], 16)
                for k in range(XT):
                    sp.wait_ge(out_ready, k + 1)
                    sp.dma_start(dr.yT[k * P:(k + 1) * P, :], zT[:, k, :]).then_inc(stored, 16)
                sp.wait_ge(stored, 16 * XT)

            @block.gpsimd
            def _(pool):
                pool.wait_ge(c_loaded, 48)
                pool.wait_ge(taken_d, len(groups) // 2)
                pool.wait_ge(taken_a, len(groups) // 2)
                for c in range(LCH):
                    op = pool.tensor_tensor(y[:, c, :].rearrange("p (h e) -> p h e", e=SSD_P),
                                            x_tok[:, c, :].rearrange("p (h e) -> p h e", e=SSD_P), heads(dsk[:]), ALU.mult)
                ns = ny = 0
                for t, d, g in steps:
                    c = SCAN[d][t]
                    if t < NCH - 1:
                        if ns >= 2:
                            pool.wait_ge(st_done, ns - 1)
                        r0 = d * SSD_H + g * HG
                        pool.tensor_tensor(xw[:, ns % 2, :].rearrange("p (h e) -> p h e", e=SSD_P),
                                           x_tok[:, c, g * GW:(g + 1) * GW].rearrange("p (h e) -> p h e", e=SSD_P),
                                           heads(tq[:, Q_DTEND, c, r0:r0 + HG]), ALU.mult).then_inc(xw_ready, 1)
                        ns += 1
                    if c < LCH:
                        pool.wait_ge(tmp_ready, ny + 1)
                        pool.drain()
                        at = y[:, c, g * GW:(g + 1) * GW]
                        pool.tensor_tensor(at, at, tmp[:, ny % 2, :], ALU.add).then_inc(y_added, 1)
                        ny += 1
                for g in range(SSD_G):
                    with pool.Fori(0, HG // EB) as i:
                        for j in range(EB):
                            pool.wait_ge(e_loaded[j], i * 32 + (g * HG // EB * 32 + 32))
                            for d in range(2):
                                op = pool.tensor_tensor(E[:, j, d], E[:, j, d], bc(neg[:, d, :], LCH, 1), ALU.add)
                            op.then_inc(e_masked, 1)

            def sum_squares(pe, k):
                pe.wait_ge(squared, k + 1)
                g, n = k // 4, k % 4
                pe.matmul(pb[g][:], ones[:], sq[:, k % 2, :], start=(n == 0), stop=(n == 3)).then_inc(summed, 1)

            @block.tensor
            def _(pe):
                pe.wait_ge(loaded, 16)
                for q, (c, k0, n) in enumerate(groups):
                    if q >= 4:
                        pe.wait_ge(taken_a if q % 2 else taken_d, (q - 4) // 2 + 1)
                    for k in range(n):
                        mm = pe.transpose(tb[q % 4][:, k * P:(k + 1) * P], xT[:, k0 + k, c * P:(c + 1) * P], ident[:])
                    mm.then_inc(turned, 1)
                for g in range(SSD_G):
                    for c in range(LCH):
                        mm = pe.matmul(pb[g][:, c * P:(c + 1) * P], xT[:, XT + g, c * P:(c + 1) * P],
                                       xT[:, XT + SSD_G + g, c * P:(c + 1) * P], start=True, stop=True)
                    mm.then_inc(cb_done, 1)
                pe.wait_ge(taken_d, len(groups) // 2)
                pe.wait_ge(taken_a, len(groups) // 2)
                ns = ny = 0
                for t, d, g in steps:
                    c = SCAN[d][t]
                    if c < LCH:
                        pe.wait_ge(h_ready, steps.index((t - 1, d, g)) + 1)
                        if ny >= 2:
                            pe.wait_ge(tmp_ready, ny - 1)
                        pe.matmul(tb[ny % 2][:], xT[:, XT + SSD_G + g, c * P:(c + 1) * P], h[:, d, g, :],
                                  start=True, stop=True).then_inc(yoff_done, 1)
                        ny += 1
                    if t < NCH - 1:
                        pe.wait_ge(xw_ready, ns + 1)
                        if ns >= 2:
                            pe.wait_ge(h_ready, ns - 1)
                        pe.matmul(tb[2 + ns % 2][:], b_tok[:, c, g * P:(g + 1) * P], xw[:, ns % 2, :],
                                  start=True, stop=True).then_inc(st_done, 1)
                        ns += 1
                pe.wait_ge(cb_taken, 2)
                for g in range(SSD_G):
                    with pe.Fori(0, HG // 2) as i:
                        for j in range(2):
                            n = i * 2 + (g * HG + j)
                            pe.wait_ge(m_ready, n + (EB + 1))
                            pe.wait_ge(y_ready, n + 1)
                            for c in range(LCH):
                                for d in range(2):
                                    mm = pe.matmul(pb[2 + j][:, c * SSD_P:(c + 1) * SSD_P], M[:, j, d, c, :],
                                                   x_tok[:, c, bass.ds(i * 2 * SSD_P + (g * HG + j) * SSD_P, SSD_P)],
                                                   start=(d == 0), stop=(d == 1))
                            mm.then_inc(diag_done, 1)
                pe.wait_ge(y_ready, SSD_H + 2)
                for k in range(XT):
                    if k >= 4:
                        pe.wait_ge(gated, k - 3)
                    for c in range(LCH):
                        mm = pe.transpose(tb[k % 4][:, c * P:(c + 1) * P], y[:, c, k * P:(k + 1) * P], ident[:])
                    mm.then_inc(out_turned, 1)
                    if k >= 1:
                        sum_squares(pe, k - 1)
                sum_squares(pe, XT - 1)

            @block.scalar
            def _(act):
                for q, (c, k0, n) in enumerate(groups):
                    if q % 2 == 0:
                        continue
                    act.wait_ge(turned, q + 1)
                    dst = x_tok[:, c, k0 * P:(k0 + n) * P] if k0 < XT else b_tok[:, c, :]
                    act.activation(dst, tb[q % 4][:, 0:n * P], ACT.Copy).then_inc(taken_a, 1)
                for g in range(SSD_G):
                    act.wait_ge(cb_done, g + 1)
                    act.activation(cb[:, g].rearrange("p c q -> p (c q)"), pb[g][:], ACT.Copy).then_inc(cb_taken, 1)
                for g in range(SSD_G):
                    with act.Fori(0, HG // EB) as i:
                        for j in range(EB):
                            n = i * EB + (g * HG + j)
                            act.wait_ge(e_masked, n + 1)
                            for d in range(2):
                                for c in range(LCH):
                                    op = act.activation(E[:, j, d, c, :], E[:, j, d, c, :], ACT.Exp,
                                                        bias=tq[:, Q_NA, c, bass.ds(n + d * SSD_H, 1)])
                            op.then_inc(e_ready, 1)
                act.wait_ge(gated, 1)
                for k in range(XT):
                    act.wait_ge(gated, k + 1)
                    if k >= 2:
                        act.wait_ge(summed, k - 1)
                    act.activation(sq[:, k % 2, :], zT[:, k, :], ACT.Square).then_inc(squared, 1)
                act.wait_ge(var_ready, 1)
                act.activation(rs[:], rs[:], ACT.Sqrt).then_inc(root_ready, 1)

            @block.vector
            def _(dve):
                for q, (c, k0, n) in enumerate(groups):
                    if q % 2 == 1:
                        continue
                    dve.wait_ge(turned, q + 1)
                    dst = x_tok[:, c, k0 * P:(k0 + n) * P] if k0 < XT else b_tok[:, c, :]
                    dve.tensor_copy(dst, tb[q % 4][:, 0:n * P]).then_inc(taken_d, 1)
                ns = ny = 0
                for t, d, g in steps:
                    c = SCAN[d][t]
                    r0 = d * SSD_H + g * HG
                    if c < LCH:
                        dve.wait_ge(yoff_done, ny + 1)
                        if ny >= 2:
                            dve.wait_ge(y_added, ny - 1)
                        dve.tensor_tensor(tmp[:, ny % 2, :].rearrange("p (h e) -> p h e", e=SSD_P),
                                          tb[ny % 2][:].rearrange("p (h e) -> p h e", e=SSD_P),
                                          heads(tq[:, Q_EA, c, r0:r0 + HG]), ALU.mult).then_inc(tmp_ready, 1)
                        ny += 1
                    if t < NCH - 1:
                        hs = h[:, d, g, :]
                        dve.wait_ge(st_done, ns + 1)
                        if t == 0:
                            dve.tensor_copy(hs, tb[2 + ns % 2][:]).then_inc(h_ready, 1)
                        else:
                            dve.tensor_tensor(hs.rearrange("p (h e) -> p h e", e=SSD_P), hs.rearrange("p (h e) -> p h e", e=SSD_P),
                                              heads(tq[:, Q_ETOT, c, r0:r0 + HG]), ALU.mult)
                            dve.drain()
                            dve.tensor_tensor(hs, hs, tb[2 + ns % 2][:], ALU.add).then_inc(h_ready, 1)
                        ns += 1
                dve.sem_inc(m_ready, EB)
                dve.sem_inc(y_ready, 2)
                dve.wait_ge(cb_taken, 2)
                dve.wait_ge(y_added, len(lat_steps))

                def add_head(i, j, g, n):
                    dve.wait_ge(diag_done, n + 1)
                    at = y[:, :, bass.ds(i * EB * SSD_P + (g * HG + j) * SSD_P, SSD_P)]
                    dve.tensor_tensor(at, at, pb[2 + j % 2][:, 0:LCH * SSD_P].rearrange("p (c e) -> p c e", c=LCH), ALU.add)\
                        .then_inc(y_ready, 1)

                for g in range(SSD_G):
                    with dve.Fori(0, HG // EB) as i:
                        for j in range(EB):
                            n = i * EB + (g * HG + j)
                            dve.wait_ge(e_ready, n + 1)
                            dve.wait_ge(y_ready, n + 1)
                            for d in range(2):
                                for c in range(LCH):
                                    op = dve.scalar_tensor_tensor(out=M[:, j % 2, d, c, :], in0=E[:, j, d, c, :],
                                                                  scalar=tq[:, Q_DT, c, bass.ds(n + d * SSD_H, 1)],
                                                                  in1=cb[:, g, c, :], op0=ALU.mult, op1=ALU.mult)
                            op.then_inc(m_ready, 1)
                            if j:
                                add_head(i, j - 1, g, n - 1)
                        add_head(i, EB - 1, g, i * EB + (g * HG + EB - 1))
                dve.wait_ge(z_loaded, 16)
                for k in range(XT):
                    dve.wait_ge(out_turned, k + 1)
                    dve.tensor_tensor(zT[:, k, :], tb[k % 4][:], zT[:, k, :], ALU.mult).then_inc(gated, 1)
                dve.wait_ge(summed, XT)
                for g in range(SSD_G):
                    dve.tensor_scalar(rs[:, g, :], pb[g][:], 1.0 / GW, EPS, ALU.mult, ALU.add)
                dve.drain().then_inc(var_ready, 1)
                dve.wait_ge(root_ready, 1)
                dve.reciprocal(rs[:], rs[:])
                dve.drain()
                for k in range(XT):
                    dve.scalar_tensor_tensor(out=zT[:, k, :], in0=zT[:, k, :], scalar=cols[:, COL["ssd_norm_w"] + k:COL["ssd_norm_w"] + k + 1],
                                             in1=rs[:, k // 4, :], op0=ALU.mult, op1=ALU.mult).then_inc(out_ready, 1)


def gdn(nc, dr, cols, tq, ident):
    HG = 4
    GW = HG * P
    LV = NLEVEL - 1
    with Phase(nc, "gdn") as ph:
        qT, kT, vT = ph.sb("qT", [P, HG, LAT]), ph.sb("kT", [P, HG, TOK]), ph.sb("vT", [P, HG, TOK])
        zT = ph.sb("zT", [P, HG, LAT])
        sq = ph.sb("sq", [P, 2, TOK])
        k_tok, v_tok = ph.sb("k_tok", [P, NCH, GW]), ph.sb("v_tok", [P, NCH, GW])
        kk, kq = ph.sb("kk", [P, NCH, GW]), ph.sb("kq", [P, LCH, GW])
        E = ph.sb("E", [P, 2, HG, NCH, P])
        neg, strict = ph.sb("neg", [P, 2, P]), ph.sb("strict", [P, 2, P])
        level = ph.sb("level", [P, 2, NLEVEL, P])
        ones = ph.sb("ones", [P, P])
        idb = ph.sb("idb", [P, HG, P], BF16)
        AT, T, Q = (ph.sb(n, [P, 2, GW]) for n in ("AT", "T", "Q"))
        TT = ph.sb("TT", [P, 2, 2, GW])
        attn, r, vn, vp, S = (ph.sb(n, [P, 2, GW]) for n in ("attn", "r", "vn", "vp", "S"))
        o = ph.sb("o", [P, LCH, GW])
        var = ph.sb("var", [P, LCH * HG])
        eps = ph.sb("eps", [P, 2])
        Pm, Tp, TTp, X = ([ph.pb(f"{n}{d}") for d in range(2)] for n in ("Pm", "Tp", "TTp", "X"))

        def two(name):
            return [ph.sem(f"{name}{d}") for d in range(2)]

        q_loaded, k_loaded, v_loaded, z_loaded = (ph.sem(n) for n in ("q_loaded", "k_loaded", "v_loaded", "z_loaded"))
        e_loaded, e_ready = two("e_loaded"), ph.sem("e_ready")
        e_shifted, o_zeroed = ph.sem("e_shifted"), ph.sem("o_zeroed")
        c_loaded, idb_ready, eps_ready = ph.sem("c_loaded"), ph.sem("idb_ready"), ph.sem("eps_ready")
        squared, summed, logged, inverted, unit = (ph.sem(n) for n in ("squared", "summed", "logged", "inverted", "unit"))
        group_done, taken_d, taken_a = (ph.sem(n) for n in ("group_done", "taken_d", "taken_a"))
        es_ready, at_ready, tt0_ready, attn_ready = (two(n) for n in ("es_ready", "at_ready", "tt0_ready", "attn_ready"))
        pm_done, q_ready, t_ready, tp_done, ttp_done, tt_ready = (
            two(n) for n in ("pm_done", "q_ready", "t_ready", "tp_done", "ttp_done", "tt_ready"))
        ks_done, qs_done, r_ready, y_done, vp_ready, vn_ready = (
            two(n) for n in ("ks_done", "qs_done", "r_ready", "y_done", "vp_ready", "vn_ready"))
        ds_done, av_done, s_ready, oq_done, o_done = (two(n) for n in ("ds_done", "av_done", "s_ready", "oq_done", "o_done"))
        osq_ready, var_ready, std_ready, o_normed = (ph.sem(n) for n in ("osq_ready", "var_ready", "std_ready", "o_normed"))
        o_turned, out_ready, stored = ph.sem("o_turned"), ph.sem("out_ready"), ph.sem("stored")

        NT = 2 * HG
        banks4 = [X[0], X[1], TTp[0], TTp[1]]
        groups = [("v", c) for c in range(NCH)] + [("k", c) for c in range(NCH)] \
            + [("kk", c) for c in range(NCH)] + [("kq", c) for c in range(LCH)]
        NG = len(groups)
        lat_before = [max(0, t - CCH) for t in range(NCH)]

        def per_head(ap):
            return ap.rearrange("p (h e) -> p h e", h=HG)

        def tile_of(n):
            return (qT, n, LAT) if n < HG else (kT, n - HG, TOK)

        def norm_of(n):
            return kq[:, n, 0:LAT] if n < HG else kk[:].rearrange("p c e -> p (c e)")[:, (n - HG) * TOK:(n - HG + 1) * TOK]

        def group_dst(q):
            kind, c = groups[q]
            return {"v": v_tok, "k": k_tok, "kk": kk, "kq": kq}[kind][:, c, :]

        with nc.Block() as block:
            @block.sync
            def _(sp):
                def const(t, at, n):
                    sp.dma_start(t, dr.consts[:, at:at + n * P].rearrange("p (n q) -> p n q", n=n)).then_inc(c_loaded, 16)

                const(neg[:], C_NEG, 2)
                const(strict[:], C_STRICT, 2)
                const(level[:].rearrange("p d v q -> p (d v) q"), C_LEVEL, 2 * NLEVEL)
                const(ones[:].unsqueeze(1), C_ONES, 1)

                def load(i):
                    for dst, src, sem in ((qT, dr.qT, q_loaded), (kT, dr.kvT, k_loaded)):
                        sp.dma_start(dst[:], src[bass.ds(i * GW, GW), :].rearrange("(k p) t -> p k t", p=P)).then_inc(sem, 16)
                    for d in range(2):
                        sp.dma_start(E[:, d].rearrange("p h c q -> p (h c q)"),
                                     dr.arow[bass.ds(i * HG + (ALPHA0 + d * GDN_H), HG), :].rearrange("a t -> (a t)").partition_broadcast(P))\
                            .then_inc(e_loaded[d], 16)
                    sp.dma_start(vT[:], dr.kvT[bass.ds(i * GW + GDN_W, GW), :].rearrange("(k p) t -> p k t", p=P)).then_inc(v_loaded, 16)

                def load_gate(i):
                    sp.dma_start(zT[:], dr.zT[bass.ds(i * GW + SSD_W, GW), :].rearrange("(k p) t -> p k t", p=P)).then_inc(z_loaded, 16)

                def store(i):
                    for h in range(HG):
                        sp.wait_ge(out_ready, i * HG + (h + 1))
                        sp.dma_start(dr.yT[bass.ds(i * GW + (SSD_W + h * P), P), :], zT[:, h, :]).then_inc(stored, 16)
                    sp.wait_ge(stored, i * (16 * HG) + 16 * HG)

                load(0)
                load_gate(0)
                with sp.Fori(0, GDN_H // HG - 1) as i:
                    for d in range(2):
                        sp.wait_ge(o_done[d], i * LCH + LCH)
                    load(i + 1)
                    store(i)
                    load_gate(i + 1)
                store(GDN_H // HG - 1)

            @block.gpsimd
            def _(pool):
                pool.wait_ge(c_loaded, 64)
                pool.tensor_copy(idb[:], bc(ident[:], HG, 1)).then_inc(idb_ready, 1)
                with pool.Fori(0, GDN_H // HG) as i:
                    pool.wait_ge(taken_d, i * (NG // 2) + NG // 2)
                    pool.wait_ge(taken_a, i * (NG // 2) + NG // 2)
                    for t in range(NCH):
                        if t == CCH:
                            pool.memset(o[:], 0.0).then_inc(o_zeroed, 1)
                        for d in range(2):
                            c = SCAN[d][t]
                            pool.wait_ge(e_ready, i * 2 + (d + 1))
                            if t:
                                pool.wait_ge(pm_done[d], i * (NCH * NLEVEL) + t * NLEVEL)
                            pool.tensor_tensor(per_head(AT[:, d, :]), E[:, d, :, c, :], bc(strict[:, d, :], HG, 1), ALU.mult)\
                                .then_inc(es_ready[d], 1)
                        for d in range(2):
                            c = SCAN[d][t]
                            pool.wait_ge(at_ready[d], i * NCH + (t + 1))
                            if t >= 2:
                                pool.wait_ge(y_done[d], i * NCH + t - 1)
                            tt = per_head(TT[:, d, t % 2, :])
                            pool.tensor_tensor(tt, per_head(AT[:, d, :]), bc(level[:, 1 - d, 0, :], HG, 1), ALU.mult)
                            pool.drain()
                            pool.tensor_tensor(tt, tt, bc(ident[:], HG, 1), ALU.add)\
                                .then_inc(tt0_ready[d], 1)
                        for d in range(2):
                            c = SCAN[d][t]
                            if c < LCH:
                                if lat_before[t]:
                                    pool.wait_ge(av_done[d], i * LCH + lat_before[t])
                                pool.tensor_tensor(per_head(attn[:, d, :]), E[:, d, :, c, :], per_head(kq[:, c, :]), ALU.mult)\
                                    .then_inc(attn_ready[d], 1)

            @block.tensor
            def _(pe):
                pe.wait_ge(c_loaded, 64)
                pe.wait_ge(idb_ready, 1)
                with pe.Fori(0, GDN_H // HG) as i:
                    def w(sem, per, n):
                        pe.wait_ge(sem, i * per + n)

                    for n in range(NT):
                        w(squared, NT, n + 1)
                        if n >= 2:
                            w(logged, NT, n - 1)
                        _, _, wd = tile_of(n)
                        mm = pe.matmul(Pm[n % 2][:], ones[:], sq[:, n % 2, 0:LAT], start=True, stop=True)
                        if wd > LAT:
                            mm = pe.matmul(Tp[n % 2][:, 0:CTX], ones[:], sq[:, n % 2, LAT:TOK], start=True, stop=True)
                        mm.then_inc(summed, 1)
                    w(v_loaded, 16, 16)
                    w(unit, NT, 1)
                    for q, (kind, c) in enumerate(groups):
                        if kind == "k" and c == 0:
                            w(unit, NT, NT)
                        if q >= 4:
                            w(taken_a if q % 2 else taken_d, NG // 2, (q - 4) // 2 + 1)
                        for h in range(HG):
                            out, at = banks4[q % 4][:, h * P:(h + 1) * P], slice(c * P, (c + 1) * P)
                            if kind in "vk" and kind != "kk":
                                mm = pe.transpose(out, (vT if kind == "v" else kT)[:, h, at], ident[:])
                            else:
                                mm = pe.matmul(out, kT[:, h, at], (kT if kind == "kk" else qT)[:, h, at], start=True, stop=True)
                        mm.then_inc(group_done, 1)
                    w(taken_a, NG // 2, NG // 2)
                    w(taken_d, NG // 2, NG // 2)

                    def grow(t, d, v):
                        if v == 0:
                            w(at_ready[d], NCH, t + 1)
                            if t:
                                w(q_ready[d], NCH * LV, t * LV)
                        else:
                            w(t_ready[d], NCH * LV, t * LV + v)
                        pe.matmul(Pm[d][:], idb[:, 0, :], idb[:].rearrange("p h e -> p (h e)"), start=True, stop=False, skip_group_check=True)
                        for h in range(HG):
                            at = slice(h * P, (h + 1) * P)
                            mm = pe.matmul(Pm[d][:, at], AT[:, d, at], ident[:] if v == 0 else T[:, d, at], start=False,
                                           stop=(h == HG - 1), skip_group_check=True)
                        mm.then_inc(pm_done[d], 1)

                    def update(t, d, v):
                        w(q_ready[d], NCH * LV, t * LV + v)
                        if v == 1:
                            w(tt0_ready[d], NCH, t + 1)
                            if t:
                                w(tt_ready[d], NCH * LV, t * LV)
                        else:
                            w(tt_ready[d], NCH * LV, t * LV + v - 1)
                        if v < LV:
                            for h in range(HG):
                                at = slice(h * P, (h + 1) * P)
                                mm = pe.matmul(Tp[d][:, at], TT[:, d, t % 2, at], Q[:, d, at], start=True, stop=True)
                            mm.then_inc(tp_done[d], 1)
                        for h in range(HG):
                            at = slice(h * P, (h + 1) * P)
                            mm = pe.matmul(TTp[d][:, at], Q[:, d, at], TT[:, d, t % 2, at], start=True, stop=True)
                        mm.then_inc(ttp_done[d], 1)

                    def heads_product(bank, lhs, rhs, sem):
                        for h in range(HG):
                            mm = pe.matmul(bank[:, h * P:(h + 1) * P], lhs(h), rhs[:, h * P:(h + 1) * P], start=True, stop=True)
                        mm.then_inc(sem, 1)

                    def scan(t, part):
                        for d in range(2):
                            c = SCAN[d][t]
                            at, lat = slice(c * P, (c + 1) * P), c < LCH
                            if part == 1 and t:
                                w(s_ready[d], NCH - 1, t)
                                if lat_before[t]:
                                    w(o_done[d], LCH, lat_before[t])
                                heads_product(X[d], lambda h: kT[:, h, at], S[:, d, :], ks_done[d])
                            if part == 2 and lat:
                                w(r_ready[d], NCH, t + 1)
                                heads_product(X[d], lambda h: qT[:, h, at], S[:, d, :], qs_done[d])
                            if part == 3:
                                w(r_ready[d], NCH, t + 1)
                                w(tt_ready[d], NCH * LV, (t + 1) * LV)
                                if lat:
                                    w(oq_done[d], LCH, lat_before[t] + 1)
                                heads_product(X[d], lambda h: TT[:, d, t % 2, h * P:(h + 1) * P], r[:, d, :], y_done[d])
                            if part == 4 and t < NCH - 1:
                                w(vp_ready[d], NCH - 1, t + 1)
                                if lat:
                                    w(vn_ready[d], LCH, lat_before[t] + 1)
                                heads_product(X[d], lambda h: k_tok[:, c, h * P:(h + 1) * P], vp[:, d, :], ds_done[d])
                            if part == 5 and lat:
                                w(vn_ready[d], LCH, lat_before[t] + 1)
                                w(attn_ready[d], LCH, lat_before[t] + 1)
                                if t < NCH - 1:
                                    w(s_ready[d], NCH - 1, t + 1)
                                heads_product(X[d], lambda h: attn[:, d, h * P:(h + 1) * P], vn[:, d, :], av_done[d])

                    for t in range(NCH):
                        for v in range(NLEVEL):
                            for d in range(2):
                                grow(t, d, v)
                            if v:
                                for d in range(2):
                                    update(t, d, v)
                            if t and 1 <= v <= 5:
                                scan(t - 1, v)
                    for part in range(1, 6):
                        scan(NCH - 1, part)
                    w(o_done[0], LCH, LCH)
                    w(o_done[1], LCH, LCH)
                    w(o_normed, LCH, LCH)
                    for h in range(HG):
                        for c in range(LCH):
                            mm = pe.transpose(banks4[h][:, c * P:(c + 1) * P], o[:, c, h * P:(h + 1) * P], ident[:])
                        mm.then_inc(o_turned, 1)

            @block.scalar
            def _(act):
                act.wait_ge(eps_ready, 1)
                with act.Fori(0, GDN_H // HG) as i:
                    act.wait_ge(q_loaded, i * 16 + 16)

                    def log_of(n):
                        act.wait_ge(summed, i * NT + (n + 1))
                        for bank, at, nt in ((Pm, 0, LAT), (Tp, LAT, CTX)):
                            if at < tile_of(n)[2]:
                                op = act.activation(norm_of(n)[:, at:at + nt], bank[n % 2][:, 0:nt], ACT.Ln,
                                                    bias=eps[:, 0:1] if n < HG else eps[:, 1:2], scale=float(P) if n < HG else 1.0)
                        op.then_inc(logged, 1)

                    for n in range(NT):
                        if n == HG:
                            act.wait_ge(k_loaded, i * 16 + 16)
                        x, h, wd = tile_of(n)
                        if n >= 2:
                            act.wait_ge(summed, i * NT + (n - 1))
                        act.activation(sq[:, n % 2, 0:wd], x[:, h, :], ACT.Square).then_inc(squared, 1)
                        if n:
                            log_of(n - 1)
                    log_of(NT - 1)
                    act.drain()
                    for n in range(NT):
                        act.activation(norm_of(n), norm_of(n), ACT.Exp, scale=-0.5).then_inc(inverted, 1)
                    for d in range(2):
                        act.wait_ge(e_shifted, i * 2 + (d + 1))
                        act.activation(E[:, d], E[:, d], ACT.Exp).then_inc(e_ready, 1)
                    for q in range(1, NG, 2):
                        act.wait_ge(group_done, i * NG + (q + 1))
                        act.activation(group_dst(q), banks4[q % 4][:], ACT.Copy).then_inc(taken_a, 1)
                    for t in range(NCH):
                        for v in range(1, NLEVEL):
                            for d in range(2):
                                act.wait_ge(ttp_done[d], i * (NCH * LV) + (t * LV + v))
                                act.activation(TT[:, d, t % 2, :], TTp[d][:], ACT.Copy).then_inc(tt_ready[d], 1)
                    for d in range(2):
                        act.wait_ge(o_done[d], i * LCH + LCH)
                    act.activation(kq[:], o[:], ACT.Square).then_inc(osq_ready, 1)
                    act.wait_ge(var_ready, i + 1)
                    act.activation(var[:], var[:], ACT.Sqrt).then_inc(std_ready, 1)

            @block.vector
            def _(dve):
                dve.memset(eps[:, 0:1], EPS * P)
                dve.memset(eps[:, 1:2], EPS)
                dve.drain().then_inc(eps_ready, 1)
                dve.wait_ge(c_loaded, 64)
                with dve.Fori(0, GDN_H // HG) as i:
                    def w(sem, per, n):
                        dve.wait_ge(sem, i * per + n)

                    def col(q, c, d, h, first, n=1):
                        return tq[:, q, c, bass.ds(i * HG + (first + d * GDN_H + h), n)]

                    for d in range(2):
                        w(e_loaded[d], 16, 16)
                        for h in range(HG):
                            for c in range(NCH):
                                op = dve.scalar_tensor_tensor(out=E[:, d, h, c, :], in0=E[:, d, h, c, :], scalar=col(Q_NA, c, d, h, ALPHA0),
                                                              in1=neg[:, d, :], op0=ALU.add, op1=ALU.add)
                        op.then_inc(e_shifted, 1)
                    for n in range(NT):
                        w(inverted, NT, n + 1)
                        x, h, _ = tile_of(n)
                        dve.tensor_tensor(x[:, h, :], x[:, h, :], norm_of(n), ALU.mult).then_inc(unit, 1)
                    for q in range(0, NG, 2):
                        w(group_done, NG, q + 1)
                        dve.tensor_copy(group_dst(q), banks4[q % 4][:]).then_inc(taken_d, 1)
                    w(taken_a, NG // 2, NG // 2)
                    def scan(t, part):
                        for d in range(2):
                            c = SCAN[d][t]
                            lat = c < LCH
                            tiles = [(h, slice(h * P, (h + 1) * P)) for h in range(HG)]
                            if part == 1:
                                if t:
                                    w(ks_done[d], NCH - 1, t)
                                    for h, at in tiles:
                                        op = dve.scalar_tensor_tensor(out=r[:, d, at], in0=X[d][:, at], scalar=col(Q_NEA, c, d, h, ALPHA0),
                                                                      in1=v_tok[:, c, at], op0=ALU.mult, op1=ALU.add)
                                else:
                                    op = dve.tensor_copy(r[:, d, :], v_tok[:, c, :])
                                op.then_inc(r_ready[d], 1)
                            if part == 2 and lat:
                                dve.drain()
                                if t == CCH and d == 0:
                                    w(o_zeroed, 1, 1)
                                w(qs_done[d], LCH, lat_before[t] + 1)
                                for h, at in tiles:
                                    op = dve.scalar_tensor_tensor(out=o[:, c, at], in0=X[d][:, at], scalar=col(Q_EA, c, d, h, ALPHA0),
                                                                  in1=o[:, c, at], op0=ALU.mult, op1=ALU.add)
                                op.then_inc(oq_done[d], 1)
                            if part == 3:
                                w(y_done[d], NCH, t + 1)
                                if t < NCH - 1:
                                    dve.tensor_tensor(per_head(vp[:, d, :]), per_head(X[d][:]),
                                                      bc(col(Q_BEND, c, d, 0, BETA0, HG), P, 2), ALU.mult).then_inc(vp_ready[d], 1)
                                if lat:
                                    dve.tensor_tensor(per_head(vn[:, d, :]), per_head(X[d][:]),
                                                      bc(col(Q_BETA, c, d, 0, BETA0, HG), P, 2), ALU.mult).then_inc(vn_ready[d], 1)
                            if part == 4 and t < NCH - 1:
                                w(ds_done[d], NCH - 1, t + 1)
                                if t == 0:
                                    op = dve.tensor_copy(S[:, d, :], X[d][:])
                                else:
                                    for h, at in tiles:
                                        op = dve.scalar_tensor_tensor(out=S[:, d, at], in0=S[:, d, at], scalar=col(Q_ETOT, c, d, h, ALPHA0),
                                                                      in1=X[d][:, at], op0=ALU.mult, op1=ALU.add)
                                op.then_inc(s_ready[d], 1)
                            if part == 5 and lat:
                                dve.drain()
                                w(av_done[d], LCH, lat_before[t] + 1)
                                dve.tensor_tensor(o[:, c, :], o[:, c, :], X[d][:], ALU.add).then_inc(o_done[d], 1)

                    for t in range(NCH):
                        for d in range(2):
                            c = SCAN[d][t]
                            w(es_ready[d], NCH, t + 1)
                            for h in range(HG):
                                at = slice(h * P, (h + 1) * P)
                                op = dve.scalar_tensor_tensor(out=AT[:, d, at], in0=AT[:, d, at], scalar=col(Q_NBETA, c, d, h, BETA0),
                                                              in1=kk[:, c, at], op0=ALU.mult, op1=ALU.mult)
                            op.then_inc(at_ready[d], 1)
                        for d in range(2):
                            w(pm_done[d], NCH * NLEVEL, t * NLEVEL + 1)
                            dve.tensor_tensor(per_head(T[:, d, :]), per_head(Pm[d][:]), bc(level[:, d, 0, :], HG, 1), ALU.mult)\
                                .then_inc(t_ready[d], 1)
                        for v in range(1, NLEVEL):
                            for d in range(2):
                                w(pm_done[d], NCH * NLEVEL, t * NLEVEL + v + 1)
                                if t * LV + v > 1:
                                    w(ttp_done[d], NCH * LV, t * LV + v - 1)
                                dve.tensor_tensor(per_head(Q[:, d, :]), per_head(Pm[d][:]), bc(level[:, d, v, :], HG, 1), ALU.mult)\
                                    .then_inc(q_ready[d], 1)
                            if v < LV:
                                for d in range(2):
                                    w(tp_done[d], NCH * (LV - 1), t * (LV - 1) + v)
                                    dve.tensor_copy(T[:, d, :], Tp[d][:]).then_inc(t_ready[d], 1)
                            if t and v <= 5:
                                scan(t - 1, v)
                    for part in range(1, 6):
                        scan(NCH - 1, part)
                    w(osq_ready, 1, 1)
                    dve.tensor_reduce(var[:], kq[:].rearrange("p c (h e) -> p (c h) e", h=HG), AX.X, ALU.add)
                    dve.drain()
                    dve.tensor_scalar(var[:], var[:], 1.0 / P, EPS, ALU.mult, ALU.add).then_inc(var_ready, 1)
                    w(std_ready, 1, 1)
                    dve.reciprocal(var[:], var[:])
                    dve.drain()
                    for c in range(LCH):
                        dve.tensor_tensor(per_head(o[:, c, :]), per_head(o[:, c, :]),
                                          bc(var[:, c * HG:(c + 1) * HG], P, 2), ALU.mult).then_inc(o_normed, 1)
                    w(z_loaded, 16, 16)
                    for h in range(HG):
                        w(o_turned, HG, h + 1)
                        dve.scalar_tensor_tensor(out=zT[:, h, :], in0=banks4[h][:], scalar=cols[:, COL["gdn_norm_w"]:COL["gdn_norm_w"] + 1],
                                                 in1=zT[:, h, :], op0=ALU.mult, op1=ALU.mult).then_inc(out_ready, 1)


def t_lat(step):
    return step[0] >= CCH


def project_plain(nc, dr, name, src, T, parts, pairs, cols, x=None, rs=None):
    with Phase(nc, name) as ph:
        st = Stream(ph, ctx=T < LAT)
        u = [(ph.sb(f"u_hi{n}", [P, KT, T], F32R), ph.sb(f"u_lo{n}", [P, KT, T], F32R)) for n in range(len(parts))]
        norm = Norm(ph, src, T, [(hi, lo, [(0, T, scale, None)]) for (hi, lo), (_, scale, _) in zip(u, parts)],
                    ph.sb("x", [P, KT, T]) if x is None else x, cols, rs=rs)
        obuf = ph.sb("obuf", [P, 2, 2, T])
        out_ready, stored = ph.sem("out_ready"), [ph.sem(f"stored{c}") for c in range(2)]
        BASE = [0]
        for pair in pairs:
            BASE.append(BASE[-1] + 2 * pair[1])

        def bank(s, m):
            return st.lat[s][m][:] if T == LAT else st.ctx[s][:, m * CTX:(m + 1) * CTX]

        with nc.Block() as block:
            @block.sync
            def _(sp):
                norm.load(sp, dr)
                for n, (part, turns, ca, cb, _, _) in enumerate(pairs):
                    w_v = parts[part][0]
                    if n == 0:
                        st.load(sp, 0, [(0, w_v[:, :, ca:ca + 256])], first=True)
                        st.load(sp, 1, [(0, w_v[:, :, cb:cb + 256])])
                    with sp.Fori(1 if n == 0 else 0, turns) as i:
                        for c, col in enumerate((ca, cb)):
                            st.load(sp, i * 2 + (BASE[n] + c), [(0, w_v[:, :, bass.ds(i * 256 + col, 256)])])

            @block.gpsimd
            def _(pool):
                for n, (part, turns, ca, cb, _, _) in enumerate(pairs):
                    out = parts[part][2]
                    with pool.Fori(0, turns) as i:
                        for c, col in enumerate((ca, cb)):
                            pool.wait_ge(out_ready, i * 4 + (2 * BASE[n] + 2 * c + 2))
                            pool.dma_start(out[bass.ds(i * 256 + col, 256), :].rearrange("(m p) t -> p m t", p=P),
                                           obuf[:, c, :, :]).then_inc(stored[c], 16)
                for c in range(2):
                    pool.wait_ge(stored[c], 8 * BASE[-1])

            @block.tensor
            def _(pe):
                norm.on_pe(pe)
                for c in range(2):
                    st.products(pe, c, c, *u[0], lat=T == LAT, ctx=T < LAT, u_ready=None if c else norm.u_ready)
                for n, (part, turns, *_) in enumerate(pairs):
                    with pe.Fori(0 if n else 1, turns) as i:
                        for c in range(2):
                            st.products(pe, i * 2 + (BASE[n] + c), c, *u[part], lat=T == LAT, ctx=T < LAT)

            @block.scalar
            def _(act):
                def epilogue(n, i, c):
                    func = pairs[n][4 + c]
                    act.wait_ge(st.unit_done, i * 4 + (2 * BASE[n] + 2 * c + 2))
                    for m in range(2):
                        act.activation(obuf[:, c, m, :], bank(c, m), func).then_inc(out_ready, 1)
                    act.wait_ge(stored[c], i * 16 + 8 * BASE[n] + 16)

                st.split_hi(act, 0, 16, first=True)
                norm.on_act(act)
                for n in range(len(pairs)):
                    last = n == len(pairs) - 1
                    with act.Fori(0, pairs[n][1] - last) as i:
                        for c in range(2):
                            st.split_hi(act, i * 2 + (BASE[n] + c + 1), i * 32 + 16 * (BASE[n] + c + 2))
                            epilogue(n, i, c)
                    if last:
                        i = pairs[n][1] - 1
                        st.split_hi(act, i * 2 + BASE[n] + 1, i * 32 + 16 * (BASE[n] + 2))
                        epilogue(n, i, 0)
                        epilogue(n, i, 1)

            @block.vector
            def _(dve):
                def free(n, i, c):
                    dve.wait_ge(out_ready, i * 4 + (2 * BASE[n] + 2 * c + 2))
                    dve.sem_inc(st.bank_free, 1)

                dve.sem_inc(st.bank_free, 2)
                st.split_lo(dve, 0)
                norm.on_dve(dve)
                for n in range(len(pairs)):
                    last = n == len(pairs) - 1
                    with dve.Fori(0, pairs[n][1] - last) as i:
                        for c in range(2):
                            st.split_lo(dve, i * 2 + (BASE[n] + c + 1))
                            free(n, i, c)
                    if last:
                        i = pairs[n][1] - 1
                        st.split_lo(dve, i * 2 + BASE[n] + 1)
                        free(n, i, 0)


def project_out(nc, dr, name, w_v, src_x, dst_x, cols, post, x, x_rs):
    NB = D // 256
    with Phase(nc, name) as ph:
        st = Stream(ph, ctx=False)
        y_hi, y_lo = ph.sb("y_hi", [P, KT, LAT], F32R), ph.sb("y_lo", [P, KT, LAT], F32R)
        res = ph.sb("res", [P, KT, LAT])
        sq = ph.sb("sq", [P, 2, LAT])
        rs, ones, gate = ph.sb("rs", [P, LAT]), ph.sb("ones", [P, P]), ph.sb("gate", [P, KT])
        pss = ph.pb("pss")
        y_loaded, x_loaded, c_loaded = [ph.sem(f"y_loaded{g}") for g in range(4)], ph.sem("x_loaded"), ph.sem("c_loaded")
        y_hi_ready, y_ready, zero_ready = ph.sem("y_hi_ready"), ph.sem("y_ready"), ph.sem("zero_ready")
        moved, squared, summed = ph.sem("moved"), ph.sem("squared"), ph.sem("summed")
        var_ready, std_ready, rs_ready, scaled = ph.sem("var_ready"), ph.sem("std_ready"), ph.sem("rs_ready"), ph.sem("scaled")
        added, stored = ph.sem("added"), ph.sem("stored")
        x_squared, x_summed, x_var_ready, x_root_ready = (ph.sem(n) for n in ("x_squared", "x_summed", "x_var_ready", "x_root_ready"))
        px = ph.pb("px")
        y_v, x_v = (a.rearrange("(k p) t -> p k t", p=P) for a in (dr.yT, src_x))

        with nc.Block() as block:
            @block.sync
            def _(sp):
                st.load(sp, 0, [(0, w_v[:, :, 0:256])], first=True)
                sp.dma_start(ones[:], dr.consts[:, C_ONES:C_ONES + P]).then_inc(c_loaded, 16)
                for g in range(4):
                    sp.dma_start(x[:, 4 * g:4 * g + 4, :], y_v[:, 4 * g:4 * g + 4, :]).then_inc(y_loaded[g], 16)
                with sp.Fori(1, NB) as i:
                    st.load(sp, i, [(0, w_v[:, :, bass.ds(i * 256, 256)])])
                sp.wait_ge(y_ready, KT)
                sp.dma_start(x[:], x_v[:, :, 0:LAT]).then_inc(x_loaded, 16)
                if dst_x is None:
                    return
                o_v = dst_x.rearrange("(k p) t -> p k t", p=P)
                for g in range(4):
                    sp.wait_ge(added, 4 * g + 4)
                    sp.dma_start(o_v[:, 4 * g:4 * g + 4, :], x[:, 4 * g:4 * g + 4, :]).then_inc(stored, 16)
                sp.wait_ge(stored, 64)

            @block.gpsimd
            def _(pool):
                if post:
                    pool.wait_ge(rs_ready, 1)
                    for k in range(KT):
                        pool.tensor_tensor(res[:, k, :], res[:, k, :], rs[:], ALU.mult).then_inc(scaled, 1)

            @block.tensor
            def _(pe):
                pe.wait_ge(c_loaded, 16)
                if post:
                    pe.sem_inc(summed, 2)
                    pe.wait_ge(zero_ready, 1)
                    pe.matmul(pss[:], ones[:], rs[:], start=True, stop=False, skip_group_check=True)

                def add_squares(i):
                    for n in range(4):
                        pe.wait_ge(squared, i * 4 + (n + 1))
                        pe.matmul(pss[:], ones[:], sq[:, n % 2, :], start=False, stop=False, skip_group_check=True).then_inc(summed, 1)

                for c in range(2):
                    st.products(pe, c, c, y_hi, y_lo, ctx=False, u_ready=None if c else y_ready)
                if post:
                    add_squares(0)
                with pe.Fori(1, NB // 2) as i:
                    for c in range(2):
                        st.products(pe, i * 2 + c, c, y_hi, y_lo, ctx=False)
                    if post:
                        add_squares(i)
                if dst_x is not None:
                    for k in range(KT):
                        pe.wait_ge(x_squared, k + 1)
                        pe.matmul(px[:], ones[:], sq[:, k % 2, :], start=(k == 0), stop=(k == KT - 1)).then_inc(x_summed, 1)

            @block.scalar
            def _(act):
                def epilogue(i, c):
                    act.wait_ge(st.unit_done, i * 4 + (2 * c + 2))
                    for m in range(2):
                        at = res[:, bass.ds(i * 4 + (2 * c + m), 1), :].rearrange("p a t -> p (a t)")
                        act.activation(at, st.lat[c][m][:], ACT.Copy).then_inc(moved, 1)
                    if post:
                        for m in range(2):
                            act.wait_ge(summed, i * 4 + (2 * c + m + 1))
                            act.activation(sq[:, m, :], st.lat[c][m][:], ACT.Square).then_inc(squared, 1)

                st.split_hi(act, 0, 16, first=True)
                for k in range(KT):
                    if k % 4 == 0:
                        act.wait_ge(y_loaded[k // 4], 16)
                    act.activation(y_hi[:, k, :], x[:, k, :], ACT.Copy).then_inc(y_hi_ready, 1)
                with act.Fori(0, NB // 2 - 1) as i:
                    for c in range(2):
                        st.split_hi(act, i * 2 + (c + 1), i * 32 + 16 * (c + 2))
                        epilogue(i, c)
                i = NB // 2 - 1
                st.split_hi(act, i * 2 + 1, i * 32 + 32)
                epilogue(i, 0)
                epilogue(i, 1)
                if post:
                    act.wait_ge(var_ready, 1)
                    act.activation(rs[:], rs[:], ACT.Sqrt).then_inc(std_ready, 1)
                if dst_x is not None:
                    for k in range(KT):
                        act.wait_ge(added, k + 1)
                        if k >= 2:
                            act.wait_ge(x_summed, k - 1)
                        act.activation(sq[:, k % 2, :], x[:, k, :], ACT.Square).then_inc(x_squared, 1)
                    act.wait_ge(x_var_ready, 1)
                    act.activation(x_rs[:], x_rs[:], ACT.Sqrt).then_inc(x_root_ready, 1)

            @block.vector
            def _(dve):
                def free(i, c):
                    dve.wait_ge(squared if post else moved, i * 4 + (2 * c + 2))
                    dve.sem_inc(st.bank_free, 1)

                dve.sem_inc(st.bank_free, 2)
                if post:
                    dve.memset(rs[:], 0.0).then_inc(zero_ready, 1)
                st.split_lo(dve, 0)
                for k in range(KT):
                    dve.wait_ge(y_hi_ready, k + 1)
                    dve.tensor_tensor(y_lo[:, k, :], x[:, k, :], y_hi[:, k, :].bitcast(F32), ALU.subtract).then_inc(y_ready, 1)
                with dve.Fori(0, NB // 2 - 1) as i:
                    for c in range(2):
                        st.split_lo(dve, i * 2 + (c + 1))
                        free(i, c)
                i = NB // 2 - 1
                st.split_lo(dve, i * 2 + 1)
                free(i, 0)
                dve.wait_ge(x_loaded, 16)
                if post:
                    g0 = COL["mod"] + 2 * KT
                    dve.tensor_tensor(gate[:], cols[:, g0:g0 + KT], cols[:, COL["post_norm_w"]:COL["post_norm_w"] + KT], ALU.mult)
                    dve.wait_ge(moved, KT)
                    dve.wait_ge(summed, KT + 2)
                    dve.tensor_scalar(rs[:], pss[:], 1.0 / D, EPS, ALU.mult, ALU.add).then_inc(var_ready, 1)
                    dve.wait_ge(std_ready, 1)
                    dve.reciprocal(rs[:], rs[:]).then_inc(rs_ready, 1)
                    for k in range(KT):
                        dve.wait_ge(scaled, k + 1)
                        dve.scalar_tensor_tensor(out=x[:, k, :], in0=res[:, k, :], scalar=gate[:, k:k + 1], in1=x[:, k, :],
                                                 op0=ALU.mult, op1=ALU.add).then_inc(added, 1)
                else:
                    dve.wait_ge(moved, KT)
                    for k in range(KT):
                        dve.tensor_tensor(x[:, k, :], x[:, k, :], res[:, k, :], ALU.add).then_inc(added, 1)
                if dst_x is not None:
                    dve.wait_ge(x_summed, KT)
                    dve.tensor_scalar(x_rs[:], px[:], 1.0 / D, EPS, ALU.mult, ALU.add).then_inc(x_var_ready, 1)
                    dve.wait_ge(x_root_ready, 1)
                    dve.reciprocal(x_rs[:], x_rs[:])


def finish(nc, dr, x, ident):
    with Phase(nc, "fin") as ph:
        o = ph.sb("o", [P, LCH, D])
        bank = [ph.pb(f"bank{i}") for i in range(4)]
        turned, taken_d, taken_a, stored = (ph.sem(n) for n in ("turned", "taken_d", "taken_a", "stored"))
        order = [(g, t) for g in range(4) for t in range(LCH)]

        with nc.Block() as block:
            @block.sync
            def _(sp):
                for g in range(4):
                    sp.wait_ge(taken_d, 2 * g + 2)
                    sp.wait_ge(taken_a, 2 * g + 2)
                    sp.dma_start(dr.out[0].rearrange("(t p) n -> p t n", p=P)[:, :, g * 512:(g + 1) * 512],
                                 o[:, :, g * 512:(g + 1) * 512]).then_inc(stored, 16)
                sp.wait_ge(stored, 64)

            @block.tensor
            def _(pe):
                for q, (g, t) in enumerate(order):
                    if q >= 4:
                        pe.wait_ge(taken_a if q % 2 else taken_d, (q - 4) // 2 + 1)
                    for k in range(4):
                        mm = pe.transpose(bank[q % 4][:, k * P:(k + 1) * P], x[:, 4 * g + k, t * P:(t + 1) * P], ident[:])
                    mm.then_inc(turned, 1)

            @block.vector
            def _(dve):
                for q, (g, t) in enumerate(order):
                    if q % 2 == 0:
                        dve.wait_ge(turned, q + 1)
                        dve.tensor_copy(o[:, t, g * 512:(g + 1) * 512], bank[q % 4][:]).then_inc(taken_d, 1)

            @block.scalar
            def _(act):
                for q, (g, t) in enumerate(order):
                    if q % 2 == 1:
                        act.wait_ge(turned, q + 1)
                        act.activation(o[:, t, g * 512:(g + 1) * 512], bank[q % 4][:], ACT.Copy).then_inc(taken_a, 1)


def mix(nc, dr, l, cols, ident):
    lam_init = 0.8 - 0.6 * float(np.exp(-0.3 * l))
    NQK = 2 * DH
    NN = NQK + 2 * MH
    R_DQ, R_DV, R_DG = 4 * W_CONV, 4 * W_CONV + 2 * W_DIFF, 4 * W_CONV + 3 * W_DIFF
    R_MQ = 4 * W_CONV + 4 * W_DIFF
    R_MG = R_MQ + W_MEM
    CT = W_CONV // P
    MT = MEMTOK // P
    with Phase(nc, f"mix{l}") as ph:
        qk = ph.sb("qk", [P, NQK, LAT])
        mq, mk = ph.sb("mq", [P, MH, LAT]), ph.sb("mk", [P, MH, MEMTOK])
        inv = ph.sb("inv", [P, NQK + 2 * MH, LAT])
        sq = ph.sb("sq", [P, 2, LAT])
        half, ones = ph.sb("half", [P, P]), ph.sb("ones", [P, P])
        alibi = ph.sb("alibi", [P, 2, ABIAS])
        v_tok, mv_tok = ph.sb("v_tok", [P, LCH, W_DIFF]), ph.sb("mv_tok", [P, MT, W_MEM])
        sc = ph.sb("sc", [P, 8, LAT])
        mvT = ph.sb("mvT", [P, MH, MEMTOK])
        qs, ks = ph.sb("qs", [P, 2, LAT]), ph.sb("ks", [P, 2, LAT])
        PT = ph.sb("PT", [P, 2, LCH, P])
        mx, nmx = ph.sb("mx", [P, 8]), ph.sb("nmx", [P, 8])
        sums, rc = ph.sb("sums", [P, 8 * (DH + MH)]), ph.sb("rc", [P, 8])
        lamv, lamp, lam = ph.sb("lamv", [P, 4, DIFF_HALF]), ph.sb("lamp", [P, 2, DIFF_HALF]), ph.sb("lam", [P, 4])
        o, otmp = ph.sb("o", [P, DH + MH, LAT]), ph.sb("otmp", [P, LAT])
        osq, var, gain = ph.sb("osq", [P, 2, LAT]), ph.sb("var", [P, DH * LCH]), ph.sb("gain", [P, 1])
        eps = ph.sb("eps", [P, 4])
        cv = ph.sb("cv", [P, 2, 4, LAT])
        cz = ph.sb("cz", [P, 2, LAT])
        sb, tb, ob, nb = ([ph.pb(f"{n}{j}") for j in range(2)] for n in ("sb", "tb", "ob", "nb"))
        c_loaded, m_loaded, v_loaded = (ph.sem(n) for n in ("c_loaded", "m_loaded", "v_loaded"))
        qk_loaded = [ph.sem(f"qk_loaded{g}") for g in range(3)]
        alibi_loaded = [ph.sem(f"alibi_loaded{j}") for j in range(2)]
        cv_loaded = [ph.sem(f"cv_loaded{j}") for j in range(2)]
        cy_ready = ph.sem("cy_ready")
        cv_stored = [ph.sem(f"cv_stored{j}") for j in range(2)]
        eps_ready, summed, logged, inverted = (ph.sem(n) for n in ("eps_ready", "summed", "logged", "inverted"))
        squared = [ph.sem(f"squared{j}") for j in range(2)]
        turned, taken_d, taken_a = (ph.sem(n) for n in ("turned", "taken_d", "taken_a"))
        lam_sum, lam_exp, passed = ph.sem("lam_sum"), ph.sem("lam_exp"), ph.sem("passed")
        qk_ready, score_done, read_done, max_ready, exp_done = (ph.sem(n) for n in ("qk_ready", "score_done", "read_done", "max_ready", "exp_done"))
        tr_done, pt_ready, pv_done, comb_done = ph.sem("tr_done"), [ph.sem(f"pt_ready{j}") for j in range(2)], ph.sem("pv_done"), ph.sem("comb_done")
        ms_done, mmax, mexp, mtr, mpt, mpv, mcomb = (ph.sem(n) for n in ("ms_done", "mmax", "mexp", "mtr", "mpt", "mpv", "mcomb"))
        osq_ready, osq_summed, var_ready, std_ready, inv_ready, o_ready = (
            ph.sem(n) for n in ("osq_ready", "osq_summed", "var_ready", "std_ready", "inv_ready", "o_ready"))
        gate_loaded, o_turned, out_ready, stored = (ph.sem(n) for n in ("gate_loaded", "o_turned", "out_ready", "stored"))

        def norm_tile(n):
            if n < NQK:
                return qk[:, n, :], LAT, half, (1.0, 0) if n < DH else (1.0 / DIFF_HALF, 1)
            if n < NQK + MH:
                return mq[:, n - NQK, :], LAT, ones, (1.0, 2)
            return mk[:, n - NQK - MH, :], MEMTOK, ones, (1.0 / P, 1)

        groups = [(0, t) for t in range(LCH)] + [(1, t) for t in range(LCH)] + [(2, t) for t in range(MT)]
        NG = len(groups)
        banks4 = [sb[0], sb[1], tb[0], tb[1]]

        def group_dst(q):
            kind, t = groups[q]
            return v_tok[:, t, 0:512] if kind == 0 else v_tok[:, t, 512:768] if kind == 1 else mv_tok[:, t, :]

        def group_width(q):
            return 256 if groups[q][0] == 1 else 512

        def rows(first, n):
            return dr.pT[first:first + n * P, :].rearrange("(k p) t -> p k t", p=P)

        kv_v = dr.mkvT[l].rearrange("(k p) t -> p k t", p=P)

        with nc.Block() as block:
            @block.sync
            def _(sp):
                for t, at in ((half, C_HALF), (ones, C_ONES)):
                    sp.dma_start(t[:], dr.consts[:, at:at + P]).then_inc(c_loaded, 16)
                for n, v in enumerate((dr.lambda_q1_2, dr.lambda_k1_2, dr.lambda_q2_2, dr.lambda_k2_2)):
                    sp.dma_start(lamv[:, n, :], v[l].partition_broadcast(P)).then_inc(c_loaded, 16)
                for g in range(3):
                    sp.dma_start(qk[:, 4 * g:4 * g + 4, :], rows(R_DQ + 4 * g * P, 4)).then_inc(qk_loaded[g], 16)
                conv_rows = dr.pT[0:4 * W_CONV, :].rearrange("(v k p) t -> p k v t", p=P, v=4)
                for k in range(2):
                    sp.dma_start(cv[:, k, :, :], conv_rows[:, k, :, :]).then_inc(cv_loaded[k], 16)
                sp.dma_start(mq[:], rows(R_MQ, MH)).then_inc(m_loaded, 16)
                sp.dma_start(mk[:], kv_v[:, 0:MH, :]).then_inc(m_loaded, 16)
                sp.dma_start(sc[:, 0:DH, :], rows(R_DV, DH)).then_inc(v_loaded, 16)
                sp.dma_start(mvT[:], kv_v[:, MH:2 * MH, :]).then_inc(v_loaded, 16)
                for j in range(2):
                    sp.dma_start(alibi[:, j, :], dr.alibi[:, j * ABIAS:(j + 1) * ABIAS]).then_inc(alibi_loaded[j], 16)
                for k in range(2, CT):
                    sp.wait_ge(cy_ready, k - 1)
                    sp.dma_start(cv[:, k % 2, :, :], conv_rows[:, k, :, :]).then_inc(cv_loaded[k % 2], 16)
                with sp.Fori(1, DH // 2) as i:
                    for j in range(2):
                        sp.wait_ge(qk_ready, i * 2 + j)
                        sp.dma_start(alibi[:, j, :], dr.alibi[:, bass.ds(i * (2 * ABIAS) + j * ABIAS, ABIAS)]).then_inc(alibi_loaded[j], 16)
                sp.wait_ge(comb_done, DH + 1)
                sp.wait_ge(mcomb, MH + 1)
                sp.dma_start(inv[:, 0:DH, :], rows(R_DG, DH)).then_inc(gate_loaded, 16)
                sp.dma_start(inv[:, DH:DH + MH, :], rows(R_MG, MH)).then_inc(gate_loaded, 16)
                for n in range(DH + MH):
                    sp.wait_ge(out_ready, n + 1)
                    sp.dma_start(dr.yT[W_CONV + n * P:W_CONV + (n + 1) * P, :], inv[:, n, :]).then_inc(stored, 16)
                sp.wait_ge(stored, 16 * (DH + MH))

            @block.gpsimd
            def _(pool):
                for n in range(0, NN, 2):
                    x, wd, _, _ = norm_tile(n)
                    if n < NQK:
                        pool.wait_ge(qk_loaded[n // 4], 16)
                    else:
                        pool.wait_ge(m_loaded, 32)
                    if n:
                        pool.wait_ge(summed, n - 1)
                    pool.tensor_tensor(sq[:, 0, 0:wd], x, x, ALU.mult).then_inc(squared[0], 1)
                for k in range(CT):
                    pool.wait_ge(cy_ready, k + 1)
                    pool.dma_start(dr.yT[k * P:(k + 1) * P, :], cz[:, k % 2, :]).then_inc(cv_stored[k % 2], 16)
                for j in range(2):
                    pool.wait_ge(cv_stored[j], 16 * CT // 2)
                for n in range(DH):
                    pool.wait_ge(comb_done, n + 2)
                    if n >= 2:
                        pool.wait_ge(osq_summed, n - 1)
                    pool.tensor_tensor(osq[:, n % 2, :], o[:, n, :], o[:, n, :], ALU.mult).then_inc(osq_ready, 1)
                pool.wait_ge(inv_ready, 1)
                for n in range(DH):
                    pool.tensor_tensor(o[:, n, :].rearrange("p (b e) -> p b e", b=LCH), o[:, n, :].rearrange("p (b e) -> p b e", b=LCH),
                                       bc(var[:, n * LCH:(n + 1) * LCH], P, 2), ALU.mult).then_inc(o_ready, 1)

            @block.tensor
            def _(pe):
                pe.sem_inc(pv_done, 2)
                pe.wait_ge(c_loaded, 16 * 6)
                for n in range(NN):
                    _, wd, mat, _ = norm_tile(n)
                    pe.wait_ge(squared[n % 2], n // 2 + 1)
                    if n >= 2:
                        pe.wait_ge(logged, n - 1)
                    pe.matmul(nb[n % 2][:, 0:wd], mat[:], sq[:, n % 2, 0:wd], start=True, stop=True).then_inc(summed, 1)
                pe.wait_ge(v_loaded, 32)
                for q, (kind, t) in enumerate(groups):
                    if q >= 4:
                        pe.wait_ge(taken_a if q % 2 else taken_d, (q - 4) // 2 + 1)
                    tiles = range(4) if kind != 1 else range(4, 6)
                    for m, k in enumerate(tiles):
                        src = mvT[:, k, t * P:(t + 1) * P] if kind == 2 else sc[:, k, t * P:(t + 1) * P]
                        mm = pe.transpose(banks4[q % 4][:, m * P:(m + 1) * P], src, ident[:])
                    mm.then_inc(turned, 1)
                pe.wait_ge(taken_a, NG // 2)
                pe.wait_ge(taken_d, NG // 2)

                def scores(i, s):
                    j, c = s // 2, s % 2
                    r = slice(64 * c, 64 * c + 64)
                    pe.wait_ge(qk_ready, i * 2 + (j + 1))
                    for b in range(LCH):
                        pe.wait_ge(read_done, i * 16 + (4 * s + b))
                        pe.matmul(sb[b % 2][:], qs[r, j, b * P:(b + 1) * P], ks[r, j, :], start=True, stop=True).then_inc(score_done, 1)

                def weigh(i, s):
                    j, c = s // 2, s % 2
                    pe.wait_ge(comb_done, i * 2 + (j + 1))

                    def turn(b):
                        u = 4 * s + b
                        pe.wait_ge(exp_done, i * 16 + (u + 1))
                        pe.wait_ge(pt_ready[b % 2], i * 8 + (u // 2 + 1))
                        for k in range(LCH):
                            mm = pe.transpose(tb[b % 2][:, k * P:(k + 1) * P], sc[:, 4 * c + b, k * P:(k + 1) * P], ident[:])
                        mm.then_inc(tr_done, 1)

                    def times_v(b):
                        u = 4 * s + b
                        pe.wait_ge(pt_ready[b % 2], i * 8 + (u // 2 + 2))
                        for k in range(LCH):
                            mm = pe.matmul(ob[c][:, b * P:(b + 1) * P], PT[:, b % 2, k, :],
                                           v_tok[:, k, bass.ds(i * 2 * P + j * P, P)], start=(k == 0), stop=(k == LCH - 1))
                        mm.then_inc(pv_done, 1)

                    turn(0)
                    for b in range(1, LCH):
                        turn(b)
                        times_v(b - 1)
                    times_v(LCH - 1)

                scores(0, 0)
                with pe.Fori(0, DH // 2 - 1) as i:
                    for s in range(4):
                        if s < 3:
                            scores(i, s + 1)
                        else:
                            scores(i + 1, 0)
                        weigh(i, s)
                i = DH // 2 - 1
                for s in range(4):
                    if s < 3:
                        scores(i, s + 1)
                    weigh(i, s)

                pe.wait_ge(comb_done, DH + 1)
                with pe.Fori(0, MH // 2) as i:
                    for j in range(2):
                        pe.wait_ge(qk_ready, i * 2 + (DH + j + 1))
                        for g in range(2):
                            pe.wait_ge(mexp, i * 4 + (2 * j + g + 1))
                            for b in range(2):
                                at = (2 * g + b) * P
                                mm = pe.matmul(sb[g][:, b * MEMTOK:(b + 1) * MEMTOK], qs[:, j, at:at + P], ks[:, j, 0:MEMTOK],
                                               start=True, stop=True)
                            mm.then_inc(ms_done, 1)
                        pe.wait_ge(mcomb, i * 2 + (j + 1))
                        for g in range(2):
                            pe.wait_ge(mexp, i * 4 + (2 * j + g + 3))
                            for b in range(2):
                                for k in range(MT):
                                    mm = pe.transpose(tb[g][:, (b * MT + k) * P:(b * MT + k + 1) * P],
                                                      sc[:, 2 * g + b, k * P:(k + 1) * P], ident[:])
                            mm.then_inc(mtr, 1)
                        for g in range(2):
                            pe.wait_ge(mpt, i * 4 + (2 * j + g + 1))
                            for b in range(2):
                                for k in range(MT):
                                    mm = pe.matmul(ob[0][:, (2 * g + b) * P:(2 * g + b + 1) * P], PT[:, g, b * MT + k, :],
                                                   mv_tok[:, k, bass.ds(i * 2 * P + j * P, P)], start=(k == 0), stop=(k == MT - 1))
                            mm.then_inc(mpv, 1)
                pe.wait_ge(mcomb, MH + 1)
                for n in range(DH + MH):
                    if n < DH:
                        pe.wait_ge(o_ready, n + 1)
                    if n >= 2:
                        pe.wait_ge(out_ready, n - 1)
                    for b in range(LCH):
                        mm = pe.transpose(nb[n % 2][:, b * P:(b + 1) * P], o[:, n, b * P:(b + 1) * P], ident[:])
                    mm.then_inc(o_turned, 1)

            @block.scalar
            def _(act):
                act.wait_ge(eps_ready, 1)

                def log_of(n):
                    _, wd, _, (scale, e) = norm_tile(n)
                    act.wait_ge(summed, n + 1)
                    act.activation(inv[:, n, 0:wd], nb[n % 2][:, 0:wd], ACT.Ln, bias=eps[:, e:e + 1], scale=scale).then_inc(logged, 1)

                for n in range(1, NN, 2):
                    x, wd, _, _ = norm_tile(n)
                    if n < NQK:
                        act.wait_ge(qk_loaded[n // 4], 16)
                    else:
                        act.wait_ge(m_loaded, 32)
                    if n >= 2:
                        act.wait_ge(summed, n - 1)
                    act.activation(sq[:, 1, 0:wd], x, ACT.Square).then_inc(squared[1], 1)
                    if n > 1:
                        log_of(n - 2)
                    log_of(n - 1)
                log_of(NN - 1)
                act.drain()
                for n in range(NN):
                    wd = norm_tile(n)[1]
                    op = act.activation(inv[:, n, 0:wd], inv[:, n, 0:wd], ACT.Exp, scale=-0.5)
                op.then_inc(inverted, 1)
                act.wait_ge(lam_sum, 1)
                act.activation(lam[:, 0:2], lam[:, 0:2], ACT.Exp).then_inc(lam_exp, 1)
                for q in range(1, NG, 2):
                    act.wait_ge(turned, q + 1)
                    act.activation(group_dst(q), banks4[q % 4][:, 0:group_width(q)], ACT.Copy).then_inc(taken_a, 1)
                def exps(i, s):
                    c = s % 2
                    act.wait_ge(max_ready, i * 4 + (s + 1))
                    for b in range(LCH):
                        act.activation(sc[:, 4 * c + b, :], sc[:, 4 * c + b, :], ACT.Exp, bias=nmx[:, 4 * c + b:4 * c + b + 1],
                                       accum_out=sums[:, bass.ds(i * 16 + (4 * s + b), 1)]).then_inc(exp_done, 1)

                def copies(i, s):
                    for b in (1, 3):
                        u = 4 * s + b
                        act.wait_ge(tr_done, i * 16 + (u + 1))
                        act.wait_ge(pv_done, i * 16 + (u + 1))
                        act.activation(PT[:, 1].rearrange("p k q -> p (k q)"), tb[1][:], ACT.Copy).then_inc(pt_ready[1], 1)

                act.sem_inc(pt_ready[1], 1)
                exps(0, 0)
                with act.Fori(0, DH // 2 - 1) as i:
                    for s in range(4):
                        if s < 3:
                            exps(i, s + 1)
                        else:
                            exps(i + 1, 0)
                        copies(i, s)
                i = DH // 2 - 1
                for s in range(4):
                    if s < 3:
                        exps(i, s + 1)
                    copies(i, s)

                act.sem_inc(mexp, 2)
                with act.Fori(0, MH // 2) as i:
                    for j in range(2):
                        for g in range(2):
                            act.wait_ge(mmax, i * 4 + (2 * j + g + 1))
                            for b in range(2):
                                op = act.activation(sc[:, 2 * g + b, 0:MEMTOK], sb[g][:, b * MEMTOK:(b + 1) * MEMTOK], ACT.Exp,
                                                    bias=nmx[:, 2 * g + b:2 * g + b + 1],
                                                    accum_out=sums[:, bass.ds(i * 8 + (8 * DH + 4 * j + 2 * g + b), 1)])
                            op.then_inc(mexp, 1)
                act.wait_ge(var_ready, 1)
                act.activation(var[:], var[:], ACT.Sqrt).then_inc(std_ready, 1)

            @block.vector
            def _(dve):
                for e, v in enumerate((DIFF_HALF * EPS, EPS, P * EPS)):
                    dve.memset(eps[:, e:e + 1], v)
                dve.drain().then_inc(eps_ready, 1)
                dve.wait_ge(c_loaded, 16 * 6)
                for n in range(2):
                    dve.tensor_tensor(lamp[:, n, :], lamv[:, 2 * n, :], lamv[:, 2 * n + 1, :], ALU.mult)
                dve.drain()
                dve.tensor_reduce(lam[:, 0:2], lamp[:], AX.X, ALU.add).then_inc(lam_sum, 1)
                h0 = COL["diff_head_norm_g_2"] + l
                dve.tensor_scalar(gain[:], cols[:, h0:h0 + 1], 1.0 - lam_init, None, ALU.mult)
                for k in range(CT):
                    j = k % 2
                    dve.wait_ge(cv_loaded[j], 16 * (k // 2 + 1))
                    dve.tensor_tensor(cv[:, j, 0, :], cv[:, j, 0, :], cv[:, j, 2, :], ALU.mult)
                    dve.tensor_tensor(cv[:, j, 1, :], cv[:, j, 1, :], cv[:, j, 3, :], ALU.mult)
                    if k >= 2:
                        dve.wait_ge(cv_stored[j], 16 * (k // 2))
                    dve.drain()
                    w0 = COL["conv_w_2"] + 3 * l * CT + k
                    b0 = COL["conv_b_2"] + l * CT + k
                    dve.tensor_scalar(cz[:, j, :], cv[:, j, 0, :], cols[:, w0 + CT:w0 + CT + 1], cols[:, b0:b0 + 1], ALU.mult, ALU.add)
                    for wc, (a, z, off) in ((w0, (1, LAT, -1)), (w0 + 2 * CT, (0, LAT - 1, 1))):
                        dve.drain()
                        dve.scalar_tensor_tensor(out=cz[:, j, a:z], in0=cv[:, j, 0, a + off:z + off], scalar=cols[:, wc:wc + 1],
                                                 in1=cz[:, j, a:z], op0=ALU.mult, op1=ALU.add)
                    dve.drain()
                    dve.tensor_tensor(cz[:, j, :], cz[:, j, :], cv[:, j, 1, :], ALU.mult).then_inc(cy_ready, 1)
                for q in range(0, NG, 2):
                    dve.wait_ge(turned, q + 1)
                    dve.tensor_copy(group_dst(q), banks4[q % 4][:, 0:group_width(q)]).then_inc(taken_d, 1)
                dve.wait_ge(turned, NG)
                dve.wait_ge(lam_exp, 1)
                dve.tensor_tensor(lam[:, 2:3], lam[:, 1:2], lam[:, 0:1], ALU.subtract)
                dve.drain()
                dve.tensor_scalar(lam[:, 2:3], lam[:, 2:3], -lam_init, None, ALU.add)
                dve.wait_ge(inverted, 1)

                def unit(x, out, gcol, iv, wd=LAT):
                    return dve.scalar_tensor_tensor(out=out[:, 0:wd], in0=x, scalar=cols[:, gcol:gcol + 1], in1=iv,
                                                    op0=ALU.mult, op1=ALU.mult)

                def dyn(t, first, n=LAT):
                    return t[:, first, 0:n].rearrange("p a t -> p (a t)")

                def head(i, j):
                    unit(dyn(qk, bass.ds(i * 2 + j, 1)), qs[:, j, :], COL["diff_q_norm_g_2"] + l, dyn(inv, bass.ds(i * 2 + j, 1)))
                    unit(dyn(qk, bass.ds(i * 2 + (DH + j), 1)), ks[:, j, :], COL["diff_k_norm_g_2"] + l,
                         dyn(inv, bass.ds(i * 2 + (DH + j), 1)))

                def maxima(i, s, first=False):
                    j, c = s // 2, s % 2
                    if c == 0:
                        head(i, j)
                        dve.drain().then_inc(qk_ready, 1)
                    if not first and s != 1:
                        dve.wait_ge(tr_done, i * 16 + 4 * (s - 1))
                    if c == 0:
                        dve.wait_ge(alibi_loaded[j], i * 16 + 16)
                    for b in range(LCH):
                        dve.wait_ge(score_done, i * 16 + (4 * s + b + 1))
                        dve.sem_inc(passed, 1)
                        dve.tensor_tensor_reduce(out=sc[:, 4 * c + b, :], in0=sb[b % 2][:],
                                                 in1=alibi[:, j, (LCH - 1 - b) * P:(LCH - 1 - b) * P + LAT],
                                                 scale=1.0, scalar=-3.0e38, op0=ALU.add, op1=ALU.max,
                                                 accum_out=mx[:, 4 * c + b:4 * c + b + 1]).then_inc(read_done, 1)
                    dve.drain()
                    dve.tensor_scalar(nmx[:, 4 * c:4 * c + 4], mx[:, 4 * c:4 * c + 4], -1.0, None, ALU.mult).then_inc(max_ready, 1)

                def copies(i, s):
                    for b in (0, 2):
                        u = 4 * s + b
                        dve.wait_ge(tr_done, i * 16 + (u + 1))
                        dve.wait_ge(pv_done, i * 16 + (u + 1))
                        dve.tensor_copy(PT[:, 0].rearrange("p k q -> p (k q)"), tb[0][:]).then_inc(pt_ready[0], 1)

                def blocks(ap):
                    return ap.rearrange("p (b e) -> p b e", b=LCH)

                def combine(i, j):
                    dve.wait_ge(exp_done, i * 16 + (8 * j + 8))
                    dve.reciprocal(rc[:], sums[:, bass.ds(i * 16 + 8 * j, 8)])
                    dve.drain()
                    dve.tensor_scalar(rc[:, 4:8], rc[:, 4:8], lam[:, 2:3], None, ALU.mult)
                    dve.drain()
                    dve.wait_ge(pv_done, i * 16 + (8 * j + 10))
                    at = dyn(o, bass.ds(i * 2 + j, 1))
                    dve.tensor_tensor(blocks(at), blocks(ob[0][:]), bc(rc[:, 0:4], P, 2), ALU.mult)
                    dve.tensor_tensor(blocks(otmp[:]), blocks(ob[1][:]), bc(rc[:, 4:8], P, 2), ALU.mult)
                    dve.drain()
                    dve.tensor_tensor(at, at, otmp[:], ALU.add).then_inc(comb_done, 1)

                for sem in (read_done, pt_ready[0], comb_done, mcomb):
                    dve.sem_inc(sem, 1)
                maxima(0, 0, first=True)
                with dve.Fori(0, DH // 2 - 1) as i:
                    for s in range(4):
                        if s < 3:
                            maxima(i, s + 1)
                        else:
                            maxima(i + 1, 0)
                        copies(i, s)
                        if s % 2:
                            combine(i, s // 2)
                i = DH // 2 - 1
                for s in range(4):
                    if s < 3:
                        maxima(i, s + 1)
                    copies(i, s)
                    if s % 2:
                        combine(i, s // 2)

                with dve.Fori(0, MH // 2) as i:
                    for j in range(2):
                        unit(dyn(mq, bass.ds(i * 2 + j, 1)), qs[:, j, :], COL["mem_q_norm_g_2"] + l, dyn(inv, bass.ds(i * 2 + (NQK + j), 1)))
                        unit(dyn(mk, bass.ds(i * 2 + j, 1), MEMTOK), ks[:, j, :], COL["mem_k_norm_g_2"] + l,
                             dyn(inv, bass.ds(i * 2 + (NQK + MH + j), 1), MEMTOK), MEMTOK)
                        dve.drain().then_inc(qk_ready, 1)
                        for g in range(2):
                            dve.wait_ge(ms_done, i * 4 + (2 * j + g + 1))
                            dve.tensor_reduce(mx[:, 2 * g:2 * g + 2], sb[g][:].rearrange("p (b m) -> p b m", b=2), AX.X, ALU.max)
                            dve.drain()
                            dve.tensor_scalar(nmx[:, 2 * g:2 * g + 2], mx[:, 2 * g:2 * g + 2], -1.0, None, ALU.mult).then_inc(mmax, 1)
                        for g in range(2):
                            dve.wait_ge(mtr, i * 4 + (2 * j + g + 1))
                            dve.tensor_copy(PT[:, g].rearrange("p k q -> p (k q)"), tb[g][:]).then_inc(mpt, 1)
                        dve.reciprocal(rc[:, 0:4], sums[:, bass.ds(i * 8 + (8 * DH + 4 * j), 4)])
                        dve.drain()
                        dve.wait_ge(mpv, i * 4 + (2 * j + 2))
                        at = dyn(o, bass.ds(i * 2 + (DH + j), 1))
                        dve.tensor_tensor(blocks(at), blocks(ob[0][:]), bc(rc[:, 0:4], P, 2), ALU.mult).then_inc(mcomb, 1)
                for n in range(DH):
                    dve.wait_ge(osq_ready, n + 1)
                    dve.tensor_reduce(var[:, n * LCH:(n + 1) * LCH], blocks(osq[:, n % 2, :]), AX.X, ALU.add).then_inc(osq_summed, 1)
                dve.drain()
                dve.tensor_scalar(var[:], var[:], 1.0 / P, EPS, ALU.mult, ALU.add).then_inc(var_ready, 1)
                dve.wait_ge(std_ready, 1)
                dve.reciprocal(var[:], var[:]).then_inc(inv_ready, 1)
                dve.wait_ge(gate_loaded, 32)
                for n in range(DH + MH):
                    dve.wait_ge(o_turned, n + 1)
                    if n < DH:
                        op = dve.scalar_tensor_tensor(out=inv[:, n, :], in0=nb[n % 2][:], scalar=gain[:], in1=inv[:, n, :],
                                                      op0=ALU.mult, op1=ALU.mult)
                    else:
                        op = dve.tensor_tensor(inv[:, n, :], nb[n % 2][:], inv[:, n, :], ALU.mult)
                    op.then_inc(out_ready, 1)


INPUTS = ["x", "c", "ctx", "c_ctx", "w_ada", "b_ada", "pre_norm_w", "post_norm_w", "w_in", "conv_ssd_w", "conv_ssd_b",
          "conv_gdn_w", "ssd_a_log", "ssd_dt_bias", "ssd_d", "ssd_norm_w", "gdn_a_log", "gdn_dt_bias", "gdn_norm_w",
          "w_out", "mem_2", "norm_g_2", "w_in_2", "conv_w_2", "conv_b_2", "diff_q_norm_g_2", "diff_k_norm_g_2",
          "lambda_q1_2", "lambda_k1_2", "lambda_q2_2", "lambda_k2_2", "diff_head_norm_g_2", "mem_norm_g_2",
          "w_mem_kv_2", "mem_q_norm_g_2", "mem_k_norm_g_2", "w_out_2"]
SCRATCH = {"xT": (D, LAT), "memT": (D, MEMTOK), "zT": (D, LAT), "xbcT": (XBC, TOK),
           "qT": (GDN_W, LAT), "kvT": (2 * GDN_W, TOK), "smallT": (NSMALL, TOK), "arow": (NSMALL, TOK), "yT": (D, LAT), "x1T": (D, LAT), "x2T": (D, LAT), "pT": (IN2, LAT),
           "mkvT": (LAYERS, 2 * W_MEM, MEMTOK)}


def program(nc, dr):
    with Phase(nc, "all") as whole:
        cols = whole.sb("cols", [P, NCOL])
        ident = whole.sb("ident", [P, P])
        rs = whole.sb("rs", [P, MEMTOK + TOK])
        with Phase(nc, "tokens") as ph:
            x_sb = ph.sb("x_sb", [P, KT, TOK])
            modulate(nc, dr, cols, ident, x_sb, rs)
            project(nc, dr, cols, x_sb, rs[:, MEMTOK:])
        m0 = COL["mem_norm_g_2"]
        project_plain(nc, dr, "kv", dr.memT, MEMTOK,
                      [(dr.w_mem_kv_2[l].rearrange("(k p) n -> p k n", p=P), cols[:, m0 + l * KT:m0 + (l + 1) * KT], dr.mkvT[l])
                       for l in range(LAYERS)],
                      [(l, 2, 0, W_MEM, ACT.Copy, ACT.Copy) for l in range(LAYERS)], cols, rs=rs[:, 0:MEMTOK])
        with Phase(nc, "mixers") as ph:
            tq = ph.sb("tq", [P, NQ, NCH, NSMALL])
            decays(nc, dr, tq, ident)
            ssd(nc, dr, cols, tq, ident)
            gdn(nc, dr, cols, tq, ident)
        C = W_CONV
        for l in range(LAYERS + 1):
            with Phase(nc, f"x{l}") as ph:
                x, x_rs = ph.sb("x", [P, KT, LAT]), ph.sb("x_rs", [P, LAT])
                if l == 0:
                    project_out(nc, dr, "out0", dr.w_out.rearrange("a (k p) n -> p (a k) n", p=P), dr.xT, dr.x1T, cols, True, x, x_rs)
                else:
                    last = l == LAYERS
                    project_out(nc, dr, f"outl{l}", dr.w_out_2[l - 1].rearrange("(k p) n -> p k n", p=P), dr.x1T if l == 1 else dr.x2T,
                                None if last else dr.x2T, cols, False, x, x_rs)
                    if last:
                        finish(nc, dr, x, ident)
                        break
                g0 = COL["norm_g_2"] + l * KT
                project_plain(nc, dr, f"pl{l}", None, LAT,
                              [(dr.w_in_2[l].rearrange("(k p) n -> p k n", p=P), cols[:, g0:g0 + KT], dr.pT)],
                              [(0, C // 256, 0, C, ACT.Copy, ACT.Copy), (0, C // 256, 2 * C, 4 * C, ACT.Copy, ACT.Copy),
                               (0, C // 256, 5 * C, 6 * C, ACT.Copy, ACT.Copy), (0, C // 256, 3 * C, 7 * C, ACT.Silu, ACT.Silu),
                               (0, W_MEM // 256, 8 * C, 8 * C + W_MEM, ACT.Copy, ACT.Silu)], cols, x, x_rs)
            mix(nc, dr, l, cols, ident)


def kernel(**inputs):
    import types as _types
    import concourse.bacc as _bacc
    from concourse.bass_utils import run_bass_kernel_spmd as _run

    nc = _bacc.Bacc("TRN2", target_bir_lowering=False, num_devices=1)
    arrays, dr = {}, {}
    for name in INPUTS:
        a = np.ascontiguousarray(inputs[name])
        arrays[f"in_{name}_dram"] = a
        dr[name] = nc.dram_tensor(f"in_{name}_dram", a.shape, mybir.dt.from_np(a.dtype), kind="ExternalInput").ap()
    dr["mem"] = dr["mem_2"]
    for name, a in zip(("consts", "alibi"), constants()):
        arrays[f"{name}_dram"] = a
        dr[name] = nc.dram_tensor(f"{name}_dram", a.shape, F32, kind="ExternalInput").ap()
    for name, shape in SCRATCH.items():
        dr[name] = nc.dram_tensor(f"scr_{name}", shape, F32, kind="Internal").ap()
    dr["out"] = nc.dram_tensor("out_0_dram", (1, LAT, D), F32, kind="ExternalOutput").ap()
    program(nc, _types.SimpleNamespace(**dr))
    return _run(nc, [arrays], core_ids=[0]).results[0]["out_0_dram"]
```
